# Optimizing a Trainium2 kernel written in Bass

```python
import jax
import jax.numpy as jnp
from jax import lax
import numpy as np

D_MODEL = 1024
BATCH = 1
SEQ = 2048
DEPTH = 2
DEC_BATCH = 8
DEC_SEQ = 1
PAST_LEN = 2048
PAGE_SIZE = 128

D_MIX = D_MODEL
A_HEADS = 8
A_KV_HEADS = 2
A_HEAD_DIM = 64
A_GROUP = A_HEADS // A_KV_HEADS
A_WIDTH = A_HEADS * A_HEAD_DIM
KV_WIDTH = A_KV_HEADS * A_HEAD_DIM
WINDOW = 128
BLOCK = 128
ROPE_THETA = 10000.0
B_WIDTH = D_MIX // 4
B_HEAD_DIM = 64
B_HEADS = B_WIDTH // B_HEAD_DIM
DECAY_LORA = 32
AAA_LORA = 32
B_SHIFT = 3 * B_WIDTH + DECAY_LORA + AAA_LORA
LNX_EPS = 1e-5 * 8 ** 2
C_WIDTH = D_MIX - A_WIDTH - B_WIDTH
C_BLOCKS = 4
C_BLOCK_DIM = C_WIDTH // C_BLOCKS
CONV_W = 4
LRU_C = 8.0
EPS = 1e-6
IN_SIZES = (A_WIDTH, KV_WIDTH, KV_WIDTH, A_WIDTH, B_SHIFT, B_WIDTH, C_WIDTH, C_WIDTH)
P_IN = sum(IN_SIZES)
IN_OFFSETS = tuple(int(o) for o in np.cumsum(IN_SIZES)[:-1])
B_OFFSETS = (B_WIDTH, 2 * B_WIDTH, 3 * B_WIDTH, 3 * B_WIDTH + DECAY_LORA)

kernel_name = "hymba_swa_rwkv7_rglru_step"

def rmsnorm(x, g):
    xf = x.astype(jnp.float32)
    xf = xf * lax.rsqrt(jnp.mean(xf * xf, axis=-1, keepdims=True) + EPS)
    return (xf * g.astype(jnp.float32)).astype(x.dtype)

def rope(x, pos):
    half = x.shape[-1] // 2
    inv_freq = ROPE_THETA ** (-jnp.arange(half, dtype=jnp.float32) / half)
    ang = pos.astype(jnp.float32)[:, None] * inv_freq[None, :]
    cos = jnp.cos(ang)[:, None, :]
    sin = jnp.sin(ang)[:, None, :]
    xf = x.astype(jnp.float32)
    x1, x2 = xf[..., :half], xf[..., half:]
    return jnp.concatenate([x1 * cos - x2 * sin, x2 * cos + x1 * sin], axis=-1).astype(x.dtype)

def sink_attention(s, mask, sinks, v, eq):
    sink = sinks.astype(jnp.float32).reshape(A_KV_HEADS, A_GROUP)[:, :, None, None]
    s = jnp.where(mask, s, -jnp.inf)
    m = jnp.maximum(jnp.max(s, axis=-1, keepdims=True), sink)
    p = jnp.exp(s - m)
    denom = jnp.sum(p, axis=-1, keepdims=True) + jnp.exp(sink - m)
    return jnp.einsum(eq, (p / denom).astype(v.dtype), v)

def swa_banded(q, k, v, sinks):
    bsz, t = q.shape[:2]
    nb = t // BLOCK
    qb = q.reshape(bsz, nb, BLOCK, A_KV_HEADS, A_GROUP, A_HEAD_DIM)
    kb = k.reshape(bsz, nb, BLOCK, A_KV_HEADS, A_HEAD_DIM)
    vb = v.reshape(bsz, nb, BLOCK, A_KV_HEADS, A_HEAD_DIM)

    def band(xb):
        prev = jnp.concatenate([jnp.zeros_like(xb[:, :1]), xb[:, :-1]], axis=1)
        return jnp.concatenate([prev, xb], axis=2)

    kk, vv = band(kb), band(vb)
    blk = jnp.arange(nb)[:, None] * BLOCK
    qpos = blk + jnp.arange(BLOCK)[None, :]
    kpos = blk - BLOCK + jnp.arange(2 * BLOCK)[None, :]
    diff = qpos[:, :, None] - kpos[:, None, :]
    mask = (diff >= 0) & (diff <= WINDOW) & (kpos[:, None, :] >= 0)
    s = jnp.einsum("bnqkgd,bnskd->bnkgqs", qb, kk, preferred_element_type=jnp.float32) * (A_HEAD_DIM ** -0.5)
    o = sink_attention(s, mask[None, :, None, None], sinks, vv, "bnkgqs,bnskd->bnqkgd")
    return o.reshape(bsz, t, A_WIDTH)

def swa_cached(q, k, v, k_buf, v_buf, sinks, pos0):
    bsz, t = q.shape[:2]
    w_buf = k_buf.shape[1]
    keys = jnp.concatenate([k_buf.astype(k.dtype), k], axis=1)
    vals = jnp.concatenate([v_buf.astype(v.dtype), v], axis=1)
    qpos = pos0 + jnp.arange(t)
    kpos = jnp.concatenate([pos0 - w_buf + jnp.arange(w_buf), qpos])
    diff = qpos[:, None] - kpos[None, :]
    mask = (diff >= 0) & (diff <= WINDOW)
    qg = q.reshape(bsz, t, A_KV_HEADS, A_GROUP, A_HEAD_DIM)
    s = jnp.einsum("bqkgd,bskd->bkgqs", qg, keys, preferred_element_type=jnp.float32) * (A_HEAD_DIM ** -0.5)
    o = sink_attention(s, mask, sinks, vals, "bkgqs,bskd->bqkgd")
    return o.reshape(bsz, t, A_WIDTH)

def wkv_step(s, inp):
    r, w, k, v, kk, a = inp
    sa = jnp.einsum("bhvk,bhk->bhv", s, -kk)
    s = s * w[:, :, None, :] + sa[..., None] * (kk * a)[:, :, None, :] + v[..., None] * k[:, :, None, :]
    return s, jnp.einsum("bhvk,bhk->bhv", s, r)

def rwkv7_time_mix(p, g, shift_prev, wkv0, lp):
    f32 = jnp.float32
    bsz, t, _ = p.shape
    prev = jnp.concatenate([shift_prev[:, None, :].astype(p.dtype), p[:, :-1]], axis=1)
    xs = p + (prev - p) * lp["rwkv_mu"]
    r, k, v, wd, ad = jnp.split(xs, B_OFFSETS, axis=-1)
    w_log = -jax.nn.softplus(-(lp["rwkv_w0"] + jnp.tanh(wd) @ lp["rwkv_w_up"]).astype(f32)) - 0.5
    decay = jnp.exp(-jnp.exp(w_log))
    a = jax.nn.sigmoid((lp["rwkv_a0"] + ad @ lp["rwkv_a_up"]).astype(f32))

    def heads(z):
        return z.astype(f32).reshape(bsz, t, B_HEADS, B_HEAD_DIM)

    kk = heads(k * lp["rwkv_k_k"])
    kk = kk / jnp.maximum(jnp.sqrt(jnp.sum(kk * kk, axis=-1, keepdims=True)), 1e-12)
    k_mod = k.astype(f32) * (1.0 + (a - 1.0) * lp["rwkv_k_a"])
    rh, wh, kh, vh, ah = heads(r), heads(decay), heads(k_mod), heads(v), heads(a)
    seq = tuple(jnp.moveaxis(z, 1, 0) for z in (rh, wh, kh, vh, kk, ah))
    s_last, y = lax.scan(wkv_step, wkv0.astype(f32), seq)
    y = jnp.moveaxis(y, 0, 1)
    mu = jnp.mean(y, axis=-1, keepdims=True)
    var = jnp.mean(jnp.square(y - mu), axis=-1, keepdims=True)
    yn = ((y - mu) * lax.rsqrt(var + LNX_EPS)).reshape(bsz, t, B_WIDTH)
    yn = yn * lp["rwkv_lnx_w"] + lp["rwkv_lnx_b"]
    bonus = jnp.sum(rh * kh * lp["rwkv_r_k"], axis=-1, keepdims=True) * vh
    out = (yn + bonus.reshape(bsz, t, B_WIDTH)) * jax.nn.silu(g.astype(f32))
    return out.astype(p.dtype), p[:, -1], s_last.astype(wkv0.dtype)

def lru_combine(c1, c2):
    a1, b1 = c1
    a2, b2 = c2
    return a1 * a2, a2 * b1 + b2

def rglru_mix(xc, g, conv_buf, h0, pos0, lp):
    f32 = jnp.float32
    bsz, t, _ = xc.shape
    xpad = jnp.concatenate([conv_buf.astype(xc.dtype), xc], axis=1)
    conv_w = lp["lru_conv_w"]
    u = lp["lru_conv_b"] + xpad[:, 0:t] * conv_w[0]
    for i in range(1, CONV_W):
        u = u + xpad[:, i:i + t] * conv_w[i]
    new_buf = xpad[:, -(CONV_W - 1):]
    ub = u.reshape(bsz, t, C_BLOCKS, C_BLOCK_DIM)
    gr = jax.nn.sigmoid((jnp.einsum("btnd,nde->btne", ub, lp["lru_gate_a_w"]).reshape(bsz, t, C_WIDTH)
                         + lp["lru_gate_a_b"]).astype(f32))
    gi = jax.nn.sigmoid((jnp.einsum("btnd,nde->btne", ub, lp["lru_gate_x_w"]).reshape(bsz, t, C_WIDTH)
                         + lp["lru_gate_x_b"]).astype(f32))
    log_a = -LRU_C * gr * jax.nn.softplus(-lp["lru_lambda"].astype(f32))
    reset = ((pos0 + jnp.arange(t)) == 0)[None, :, None]
    a = jnp.where(reset, 0.0, jnp.exp(log_a))
    mult = jnp.where(reset, 1.0, jnp.sqrt(-jnp.expm1(2.0 * log_a)))
    b = mult * gi * u.astype(f32)
    b = b.at[:, 0].add(a[:, 0] * h0.astype(f32))
    _, h = lax.associative_scan(lru_combine, (a, b), axis=1)
    out = h * jax.nn.silu(g.astype(f32))
    return out.astype(xc.dtype), new_buf, h[:, -1].astype(h0.dtype)

def hybrid_layer(x, c, pos0, k_buf, v_buf, shift_prev, wkv0, conv_buf, h0, lp):
    bsz, t, _ = x.shape
    mod = jax.nn.silu(c) @ lp["w_mod"] + lp["b_mod"]
    shift_m, scale_m, gate_m = jnp.split(mod, 3, axis=-1)
    h = rmsnorm(x, lp["norm_pre"]) * (1.0 + scale_m[:, None]) + shift_m[:, None]
    proj = h @ lp["w_in"]
    qa, ka, va, ga, pb, gb, xc, gc = jnp.split(proj, IN_OFFSETS, axis=-1)
    pos = pos0 + jnp.arange(t)
    q = rope(qa.reshape(bsz, t, A_HEADS, A_HEAD_DIM), pos)
    k = rope(ka.reshape(bsz, t, A_KV_HEADS, A_HEAD_DIM), pos)
    v = va.reshape(bsz, t, A_KV_HEADS, A_HEAD_DIM)
    if k_buf is None:
        ya = swa_banded(q, k, v, lp["attn_sinks"])
        k_new, v_new = k[:, -WINDOW:], v[:, -WINDOW:]
    else:
        ya = swa_cached(q, k, v, k_buf, v_buf, lp["attn_sinks"], pos0)
        k_new, v_new = k, v
    ya = ya * jax.nn.silu(ga)
    yb, shift_new, wkv_new = rwkv7_time_mix(pb, gb, shift_prev, wkv0, lp)
    yc, conv_new, h_new = rglru_mix(xc, gc, conv_buf, h0, pos0, lp)
    y = jnp.concatenate([ya, yb, yc], axis=-1) @ lp["w_out"]
    x = x + gate_m[:, None] * rmsnorm(y, lp["norm_post"])
    return x, (k_new, v_new, shift_new, wkv_new, conv_new, h_new)

def setup_inputs(seed: int = 0) -> dict:
    key = jax.random.key(seed)
    ks = iter(jax.random.split(key, 48))

    def nrm(shape, scale=1.0):
        return scale * jax.random.normal(next(ks), shape, jnp.float32)

    def uni(shape, lo, hi):
        return jax.random.uniform(next(ks), shape, jnp.float32, lo, hi)

    w_buf = min(WINDOW, PAST_LEN)
    lru_a = uni((DEPTH, C_WIDTH), 0.9, 0.999) ** (1.0 / LRU_C)
    return {
        "x_prompt": nrm((BATCH, SEQ, D_MODEL)),
        "x_sample": nrm((DEC_BATCH, DEC_SEQ, D_MODEL)),
        "c_prompt": nrm((BATCH, D_MODEL)),
        "c_sample": nrm((DEC_BATCH, D_MODEL)),
        "cache_swa_k": nrm((DEPTH, DEC_BATCH, w_buf, A_KV_HEADS, A_HEAD_DIM)),
        "cache_swa_v": nrm((DEPTH, DEC_BATCH, w_buf, A_KV_HEADS, A_HEAD_DIM)),
        "state_rwkv_shift": nrm((DEPTH, DEC_BATCH, B_SHIFT)),
        "state_rwkv_wkv": nrm((DEPTH, DEC_BATCH, B_HEADS, B_HEAD_DIM, B_HEAD_DIM), 0.3),
        "state_lru_conv": nrm((DEPTH, DEC_BATCH, CONV_W - 1, C_WIDTH)),
        "state_lru_h": nrm((DEPTH, DEC_BATCH, C_WIDTH), 0.5),
        "norm_pre": 1.0 + nrm((DEPTH, D_MODEL), 0.05),
        "norm_post": 1.0 + nrm((DEPTH, D_MODEL), 0.05),
        "w_mod": nrm((DEPTH, D_MODEL, 3 * D_MODEL), 0.5 * D_MODEL ** -0.5),
        "b_mod": nrm((DEPTH, 3 * D_MODEL), 0.02),
        "w_in": nrm((DEPTH, D_MODEL, P_IN), D_MODEL ** -0.5),
        "w_out": nrm((DEPTH, D_MIX, D_MODEL), D_MIX ** -0.5),
        "attn_sinks": nrm((DEPTH, A_HEADS), 0.5),
        "rwkv_mu": uni((DEPTH, B_SHIFT), 0.0, 1.0),
        "rwkv_w0": uni((DEPTH, B_WIDTH), -6.5, -1.5),
        "rwkv_w_up": nrm((DEPTH, DECAY_LORA, B_WIDTH), 0.1),
        "rwkv_a0": nrm((DEPTH, B_WIDTH), 0.1),
        "rwkv_a_up": nrm((DEPTH, AAA_LORA, B_WIDTH), 0.1),
        "rwkv_k_k": 0.85 + nrm((DEPTH, B_WIDTH), 0.05),
        "rwkv_k_a": 1.0 + nrm((DEPTH, B_WIDTH), 0.05),
        "rwkv_r_k": nrm((DEPTH, B_HEADS, B_HEAD_DIM), 0.1),
        "rwkv_lnx_w": 1.0 + nrm((DEPTH, B_WIDTH), 0.05),
        "rwkv_lnx_b": nrm((DEPTH, B_WIDTH), 0.02),
        "lru_conv_w": nrm((DEPTH, CONV_W, C_WIDTH), CONV_W ** -0.5),
        "lru_conv_b": nrm((DEPTH, C_WIDTH), 0.02),
        "lru_gate_a_w": nrm((DEPTH, C_BLOCKS, C_BLOCK_DIM, C_BLOCK_DIM), C_BLOCK_DIM ** -0.5),
        "lru_gate_a_b": nrm((DEPTH, C_WIDTH), 0.02),
        "lru_gate_x_w": nrm((DEPTH, C_BLOCKS, C_BLOCK_DIM, C_BLOCK_DIM), C_BLOCK_DIM ** -0.5),
        "lru_gate_x_b": nrm((DEPTH, C_WIDTH), 0.02),
        "lru_lambda": jnp.log(lru_a) - jnp.log1p(-lru_a),
    }

def reference(x_prompt, x_sample, c_prompt, c_sample,
              cache_swa_k, cache_swa_v, state_rwkv_shift, state_rwkv_wkv, state_lru_conv, state_lru_h,
              norm_pre, norm_post, w_mod, b_mod, w_in, w_out, attn_sinks,
              rwkv_mu, rwkv_w0, rwkv_w_up, rwkv_a0, rwkv_a_up, rwkv_k_k, rwkv_k_a, rwkv_r_k,
              rwkv_lnx_w, rwkv_lnx_b,
              lru_conv_w, lru_conv_b, lru_gate_a_w, lru_gate_a_b, lru_gate_x_w, lru_gate_x_b, lru_lambda):
    yp, ys = x_prompt, x_sample
    bp = x_prompt.shape[0]
    dt = x_prompt.dtype
    outs_p, outs_s = [], []
    for l in range(DEPTH):
        lp = {
            "norm_pre": norm_pre[l], "norm_post": norm_post[l], "w_mod": w_mod[l], "b_mod": b_mod[l],
            "w_in": w_in[l], "w_out": w_out[l], "attn_sinks": attn_sinks[l],
            "rwkv_mu": rwkv_mu[l], "rwkv_w0": rwkv_w0[l], "rwkv_w_up": rwkv_w_up[l],
            "rwkv_a0": rwkv_a0[l], "rwkv_a_up": rwkv_a_up[l], "rwkv_k_k": rwkv_k_k[l],
            "rwkv_k_a": rwkv_k_a[l], "rwkv_r_k": rwkv_r_k[l],
            "rwkv_lnx_w": rwkv_lnx_w[l], "rwkv_lnx_b": rwkv_lnx_b[l],
            "lru_conv_w": lru_conv_w[l], "lru_conv_b": lru_conv_b[l],
            "lru_gate_a_w": lru_gate_a_w[l], "lru_gate_a_b": lru_gate_a_b[l],
            "lru_gate_x_w": lru_gate_x_w[l], "lru_gate_x_b": lru_gate_x_b[l],
            "lru_lambda": lru_lambda[l],
        }
        yp, st_p = hybrid_layer(
            yp, c_prompt, 0, None, None,
            jnp.zeros((bp, B_SHIFT), dt),
            jnp.zeros((bp, B_HEADS, B_HEAD_DIM, B_HEAD_DIM), dt),
            jnp.zeros((bp, CONV_W - 1, C_WIDTH), dt),
            jnp.zeros((bp, C_WIDTH), dt), lp)
        ys, st_s = hybrid_layer(
            ys, c_sample, PAST_LEN, cache_swa_k[l], cache_swa_v[l],
            state_rwkv_shift[l], state_rwkv_wkv[l], state_lru_conv[l], state_lru_h[l], lp)
        outs_p.append(st_p)
        outs_s.append(st_s)
    swa_k_p, swa_v_p, shift_p, wkv_p, conv_p, h_p = [jnp.stack(z) for z in zip(*outs_p)]
    swa_k_s, swa_v_s, shift_s, wkv_s, conv_s, h_s = [jnp.stack(z) for z in zip(*outs_s)]
    return (yp, ys, swa_k_p, swa_v_p, shift_p, wkv_p, conv_p, h_p,
            swa_k_s, swa_v_s, shift_s, wkv_s, conv_s, h_s)


_drawn_inputs = setup_inputs


def setup_inputs(seed=0):
    import zlib

    import numpy as np

    out = dict(_drawn_inputs(seed))
    spreads = {}
    factors = {'norm_post': 2.876,
     'attn_sinks': 8.0,
     'rwkv_lnx_w': 3.324,
     'rwkv_lnx_b': 8.0,
     'lru_gate_a_b': 8.0,
     'lru_gate_x_b': 6.383}
    for name, (base, spread) in spreads.items():
        noise = np.random.default_rng([zlib.crc32(name.encode()), seed]).standard_normal(out[name].shape)
        drawn = base * np.exp(spread * noise) if base else spread * noise
        out[name] = jnp.asarray(drawn.astype(out[name].dtype))
    for name, factor in factors.items():
        out[name] = (out[name] * factor).astype(out[name].dtype)
    return out
```

```python
from contextlib import ExitStack

import numpy as np

import concourse.bass as bass
from concourse import mybir

ALU = mybir.AluOpType
ACT = mybir.ActivationFunctionType
F32 = mybir.dt.float32
BF16 = mybir.dt.bfloat16
AX_X = mybir.AxisListType.X

P = 128
D = 1024
KC = D // P
SEQ = 2048
NT = SEQ // P
DEPTH = 2
B = 8
HD = 64
HALF = HD // 2
HEADS = 8
KV = 2
CH = 64
NCH = P // CH
PAIRS = 2
U = PAIRS * NCH
LORA = 32
SHIFT = 832
PAST = 2048
SCALE = HD ** -0.5
EPS = 1e-6
LNX_EPS = 64e-5
LRU_C = 8.0
DECAY = float(np.exp(-0.5))
NEG = -1e30
PIN = 2880

C_R, C_K, C_V, C_WA, C_KA, C_Q, C_XC, C_VA, C_GB, C_GC, C_GA = (
    0, 256, 512, 768, 832, 960, 1472, 1728, 1856, 2112, 2368)

PRM = {}
for _name, _n in (("npre", 8), ("npost", 8), ("bmod", 24), ("mu", 7), ("w0", 2), ("a0", 2), ("kk", 2),
                  ("ka", 2), ("rk", 2), ("lnw", 2), ("lnb", 2), ("cw", 8), ("cb", 2), ("gab", 2),
                  ("gxb", 2), ("lam", 2), ("sink", 8), ("dsink", 1)):
    PRM[_name] = (sum(n for _, n in PRM.values()), _n)
NPRM = sum(n for _, n in PRM.values())

CST = {}
for _name, _n in (("ident", 128), ("ones", 128), ("mst", 128), ("ms", 128), ("mit", 128), ("reset", 256)):
    CST[_name] = (sum(n for _, n in CST.values()), _n)
NCST = sum(n for _, n in CST.values())
DCST = {}
for _name, _n in (("perm", 128), ("stack", 64), ("rowb", 8), ("cos", 1), ("sin", 1)):
    DCST[_name] = (sum(n for _, n in DCST.values()), _n)
NDCST = sum(n for _, n in DCST.values())


def DONE(n):
    return n + 2


def BEFORE(n):
    return n + 1


def STEP(n, k, per):
    return n * per + (per + k)


class Link:

    def __init__(self, eng, sem, per):
        self.eng, self.sem, self.per, self.k, self.base = eng, sem, per, 0, 0

    def start(self, n):
        self.k, self.base = 0, n * self.per

    def __call__(self, ins):
        self.k += 1
        ins.then_inc(self.sem, 1)
        self.eng.wait_ge(self.sem, self.base + self.k)

    def end(self):
        assert self.k == self.per, (self.sem, self.k, self.per)


def over(ap, axis, count):
    v = ap.unsqueeze(axis)
    shape = list(v.shape)
    shape[axis] = count
    return v.to_broadcast(shape)


TILE_SEMS = """x_squared rms_root xn_ready xT_lo xT_hi hT_lo hT_hi
 rk_mm vwk_mm rk_out vwk_out rkT_mm vwT_mm pB_ready q_mm q_out xs_ready carried tw_ready lora_mm vbT_mm vst_ready
 sq_ready kksum_mm sgw_ready a_ready kknorm cum_ready exps_ready bonus_in bd_ready bonus_mm bonus_out
 g1T_mm g1_mm g2T_mm g3T_mm g4T_mm ntn_ready g_ready btT_mm bt_out
 xv_mm xv_out xcT_mm xcb_ready conv_ready lru_mm gates_ready lru_exps lru_t lru_root h_ready yC_ready
 gbc_mm gbc_out gbcT_mm gates_T ga_mm ga_out
 rope_ready qT_mm kT_mm qT_ready kT_ready qbd
 s0_mm s1_mm neg0 neg1 es0 es1 exp0 exp1 pT0_mm pT1_mm pT0_act pT0_dve pT1_act pT1_dve pv_mm yA_tm yAT_mm yA_ready window_moved
 u_out y_mm y_sq y_root yn_ready ynT_mm yB_ready ytm_ready
 s_mm o0_mm o1_mm o_squared o_root o_ready""".split()
TILE_STEPS = {"inv_mm": 5, "inv_act": 5, "inv_dve": 4, "q_mm5": 5, "q_dve": 4, "rh_ready": 2, "rh_mm": 2, "u_mm": 2,
              "u_act": 2, "s_ready": 2}


ACT_SEMS = """rms_root hT_lo x_squared rk_out vwk_out pB_ready q_out xv_out tw_ready sgw_ready a_ready xcb_ready kknorm
 exps_ready gbc_out inv_act bt_out gates_T gates_ready lru_exps qT_ready kT_ready lru_root ga_out es0 es1 exp0 exp1
 u_act pT0_act pT1_act y_sq y_root yA_ready o_squared o_root""".split()
PE_SEMS = [k for k in TILE_SEMS + list(TILE_STEPS) if k.endswith("_mm") or k in ("xT_lo", "xT_hi", "q_mm5")]
DVE_SEMS = [k for k in TILE_SEMS + list(TILE_STEPS) if k not in PE_SEMS and k not in ACT_SEMS]
PE_STEPS = """ssq_mm proj_mm perm_mm lora_mm kk_mm lru_mm bonus_mm sa_mm vb_mm sr_mm s_mm mean_mm var_mm pt_mm pv_mm o_mm
 ossq_mm""".split()
ACT_STEPS = """root silu tw sig w kknorm gates lru_exps lru_root exp yroot oroot""".split()
DVE_STEPS = """sq ms h proj xs u kksq bonus_in skk vdiag bonus qrows s_new sr y neg ysq lru_t var pd h_new pt ys osq oms""".split()
SAMPLE_SEMS = ("pe", "act", "dve", "x_s", "in_small", "kv_in", "stored")


def AT(step, l):
    steps = next(x for x in (PE_STEPS, ACT_STEPS, DVE_STEPS) if step in x)
    return l * len(steps) + steps.index(step) + 1


DCHUNKS = [(128 * j, 128) for j in range(6)] + [(C_WA, 64), (C_KA, 128)] + [(C_Q + 128 * j, 128) for j in range(4)] + \
    [(C_XC, 128), (C_XC + 128, 128), (C_VA, 128), (C_GB, 128), (C_GB + 128, 128), (C_GC, 128), (C_GC + 128, 128)] + \
    [(C_GA + 128 * j, 128) for j in range(4)]
DVE_T, DVE_L, DVE_D, YVAR, OVAR = 43, 13, 49, 34, 41


def program(nc, d):
    with ExitStack() as ctx:
        def sb(name, shape, dt=F32):
            return ctx.enter_context(nc.sbuf_tensor(name, shape, dt))

        def sem(name):
            return ctx.enter_context(nc.semaphore(name))

        Win = sb("w_in", [P, KC, PIN])
        Wout = sb("w_out", [P, KC, D])
        prm = sb("prm", [P, NPRM])
        cst = sb("cst", [P, NCST])
        lora = sb("lora", [2 * LORA, 4 * P])
        gatew = sb("gatew", [P, 4, P])
        mod = sb("mod", [P, 24, 1 + B])
        gs = sb("gs", [P, KC, 1 + B])
        gpc = sb("gpc", [P, KC, 1 + B])
        gp = sb("gp", [P, D])
        cT = sb("cT", [P, KC, 1 + B])
        spc = sb("spc", [P, 12, 2])
        identb = sb("identb", [P, P], BF16)
        mk = sb("mk", [P, 2 * P], BF16)
        mkprev = sb("mkprev", [P, 2, P], BF16)
        xa = sb("xa", [P, D])
        hT = sb("hT", [P, KC, P])
        stA = sb("stA", [P, 512])
        stB = sb("stB", [P, 512])
        qk = sb("qk", [P, 640])
        rope = sb("rope", [P, 64])
        pB = sb("pB", [P, 7, P + 1])
        xs = sb("xs", [P, 7, P])
        yT = sb("yT", [P, KC, P])
        kT = sb("kT", [P, 2 * P])
        Vt = sb("Vt", [P, 2, P])
        RA = sb("RA", [P, 2048])
        RB = sb("RB", [P, 1024])
        small = sb("small", [P, 64])
        tw = sb("tw", [2 * LORA, P])
        W1 = sb("W1", [P, 4, 256])
        W2 = sb("W2", [P, 4, 256])
        Ep = sb("Ep", [P, 256])
        kap = sb("kap", [P, U, P])
        bti = sb("bti", [P, U, P])
        kti = sb("kti", [P, U, P])
        rti = sb("rti", [P, U, P])
        Vst = sb("Vst", [P, U, HD])
        G = sb("G", [P, 3, 512])
        Q = sb("Q", [P, U, CH])
        RH = sb("RH", [P, PAIRS, HD])
        Ub = sb("Ub", [P, PAIRS, HD])
        S = sb("S", [P, 2, PAIRS, HD])
        bonv = sb("bonv", [P, 256])
        xcb = sb("xcb", [P, 2, P + 3])
        hcar = sb("hcar", [P, 2])
        flag = sb("flag", [P, 1])
        xsT = sb("xsT", [P, KC, B])

        sgw, cum, cx, Em = (W1[:, k, :] for k in range(4))
        Ex = cx
        Nbd = W1[:, 0:2, :].rearrange("p a (b c) -> p (a b) c", c=P)
        NTbd = W1[:, 2:4, :].rearrange("p a (b c) -> p (a b) c", c=P)
        Qbd = NTbd
        av, kkv, kmod, tmp = (W2[:, k, :] for k in range(4))
        btk = W2[:, 0:2, :].rearrange("p a (b c) -> p (a b) c", c=P)
        ktk = W2[:, 2:4, :].rearrange("p a (b c) -> p (a b) c", c=P)
        ytm = W2[:, 0, :].rearrange("p (u v) -> p u v", v=HD)
        qT = stA[:, :].rearrange("p (c t) -> p c t", c=4)
        G2T, G3T, G4T = (G[:, k, :].rearrange("p (u c) -> p u c", c=P) for k in range(3))
        xr = G[:, 0:2, :].rearrange("p a b -> p (a b)")
        xn = RA[:, 0:1024]
        ob = RA[:, 1024:2048]
        lu, lgr, lgi, lth, laa, la2, lh = (RA[:, 256 * k:256 * k + 256].rearrange("p (c t) -> p c t", c=2)
                                           for k in range(7))
        Pm = RA[:, :].rearrange("p (j s k) -> p j s k", j=2, k=256)
        PT = RB[:, :].rearrange("p (f s q) -> p f s q", f=2, q=P)
        rot = RB[:, 0:640]


        s = {k: sem("s_" + k) for k in TILE_SEMS + list(TILE_STEPS)}
        smp = {k: sem("d_" + k) for k in SAMPLE_SEMS}
        L = {k: sem("l_" + k) for k in (
            "const", "prm", "win", "wout", "wmod0", "wmod1", "wmod2", "mod_mm", "silu_c", "mod_out", "gpc", "gp_mm",
            "gp_out", "sp1", "sp2", "sp3", "cleared", "cast", "state", "x_in", "rope_in", "xr_in", "y_out",
            "dve_t", "act_t", "dve_l", "act_l", "zeros", "layer_end", "dve_d")}

        at = [0]

        def view(n, *shape):
            v = RA[:, at[0]:at[0] + n]
            at[0] += n
            if len(shape) == 2:
                v = v.rearrange("p (a b) -> p a b", b=shape[1])
            elif len(shape) == 3:
                v = v.rearrange("p (a b c) -> p a b c", b=shape[1], c=shape[2])
            return v

        KTs = view(B * (P + 1), B, P + 1)
        dcst = view(NDCST)
        dshift = view(7 * B, 7, B)
        dconv = view(6 * B, 2, 3, B)
        dcnew = view(6 * B, 2, 3, B)
        dh0 = view(2 * B, 2, B)
        pj = view(23 * B, 23, B)
        dx = view(7 * B, 7, B)
        du, dv1, dkr, dkm, da, dw, dgr, dgi, dth, daa = (view(2 * B, 2, B) for _ in range(10))
        dq1, dq2, dkk, dyv, dbv = (view(2 * B) for _ in range(5))
        Vc = RB[:, :].rearrange("p (b c) -> p b c", b=B)
        dS = W1[:, :, :].rearrange("p a b -> p (a b)")
        dT1 = W2[:, :, :].rearrange("p a b -> p (a b)")
        dT2 = xa[:, :]
        dsq = stA[:, 0:64].rearrange("p (c b) -> p c b", b=B)
        dh = stA[:, 64:128].rearrange("p (c b) -> p c b", b=B)
        dsg = stA[:, 128:192].rearrange("p (c b) -> p c b", b=B)
        drq = stA[:, 192:232].rearrange("p (c b) -> p c b", b=B)
        dtw = stA[:, 232:240]
        dr1, dr2, dm = stA[:, 240:248], stA[:, 248:256], stA[:, 256:264]
        Pd = stA[:, 264:393]
        dg64 = stA[:, 393:457]
        ys = yT[:, 0, 0:64].rearrange("p (c b) -> p c b", b=B)
        PTd = yT[:, 1, 0:64]
        Pnd = yT[:, 2, 0:64]
        Vnd = yT[:, 3, :]
        kkr = bonv[:, :]

        def dcon(name):
            o, n = DCST[name]
            return dcst[:, o:o + n]

        wmod = [v.rearrange("p (k c) -> p k c", c=P) for v in (RA[:, 0:1024], RA[:, 1024:2048], RB[:, :])]
        wmod_in = [L["wmod0"], L["wmod1"], L["wmod2"]]

        def par(name, rows=P):
            o, n = PRM[name]
            return prm[0:rows, o:o + n]

        def con(name):
            o, n = CST[name]
            return cst[:, o:o + n]

        ident = con("ident")
        ones = con("ones")

        PS = {k: ctx.enter_context(nc.psum_tensor(k, [P, 512], F32))
              for k in ("G0", "G1", "M0", "M1", "M2", "M3", "M4", "M5")}
        G0, G1, M0, M1, M2, M3, M4, M5 = PS["G0"], PS["G1"], PS["M0"], PS["M1"], PS["M2"], PS["M3"], PS["M4"], PS["M5"]
        block = ctx.enter_context(nc.Block())

        @block.sync
        def _(sp):
            sp.sem_inc(L["y_out"], 16)
            sp.sem_inc(L["state"], 16)
            sp.dma_start(cst[:, :], d["cst"]).then_inc(L["const"], 16)
            sp.dma_start(cT[:, :, :], d["cT"]).then_inc(L["const"], 16)
            sp.dma_start(RB[:, 0:384], d["masks"]).then_inc(L["const"], 16)
            sp.dma_start(xsT[:, :, :], d["x_s"]).then_inc(smp["x_s"], 16)
            for l in range(DEPTH):
                src = d["x_prompt"] if l == 0 else d["x_mid"]
                dst = d["y_prompt"] if l == DEPTH - 1 else d["x_mid"]

                def rows(x, i):
                    return x[bass.ds(i * P, P), :]

                def load(i, n):
                    sp.dma_start(xa[:, :], rows(src, i)).then_inc(L["x_in"], 16)
                    sp.wait_ge(s["rope_ready"], BEFORE(n))
                    sp.dma_start(rope[:, :], d["rope"][i]).then_inc(L["rope_in"], 16)

                def residual_and_store(i, n):
                    sp.wait_ge(s["y_mm"], DONE(n))
                    sp.dma_start(xr, rows(src, i)).then_inc(L["xr_in"], 16)
                    sp.wait_ge(s["o_ready"], DONE(n))
                    sp.dma_start(rows(dst, i), ob).then_inc(L["y_out"], 16)

                sp.wait_ge(L["layer_end"], l + 1)
                load(0, l * NT)
                with sp.Fori(0, NT - 1) as i:
                    n = l * NT + i
                    sp.wait_ge(s["xn_ready"], DONE(n))
                    load(i + 1, n + 1)
                    residual_and_store(i, n)
                residual_and_store(NT - 1, l * NT + NT - 1)
                for out, carry in ((d["k_p"], kT[:, 0:P]), (d["v_p"], Vt[:, 0, :]), (d["shift_p"], pB[:, :, 0]),
                                   (d["wkv_p"], S[:, 0, :, :]), (d["conv_p"], xcb[:, :, 0:3]), (d["h_p"], hcar[:, :])):
                    sp.dma_start(out[l], carry, allow_slow_non_contiguous=out is d["shift_p"]).then_inc(L["state"], 16)
                sp.wait_ge(L["y_out"], (l + 1) * NT * 16 + 16)
                for buf, x in ((dcst, d["dcst"]), (dshift, d["shift_s"][l]), (dconv, d["conv_s"][l]), (dh0, d["h_s"][l])):
                    sp.dma_start(buf, x).then_inc(smp["in_small"], 16)
                for k in range(4):
                    sp.dma_start(KTs[:, 2 * k:2 * k + 2, 0:P], d["kc"][l][:, 2 * k:2 * k + 2, :]).then_inc(smp["kv_in"], 16)
                sp.dma_start(Vc, d["vc"][l]).then_inc(smp["kv_in"], 16)
                sp.dma_start(dS, d["wkv_s"][l]).then_inc(smp["kv_in"], 16)
                sp.wait_ge(smp["dve"], AT("u", l))
                sp.wait_ge(smp["dve"], AT("qrows", l))
                sp.dma_start(d["ko_s"][l], drq[:, 0, :]).then_inc(smp["stored"], 16)
                sp.dma_start(d["vo_s"][l], pj[:, 14, :]).then_inc(smp["stored"], 16)
                sp.dma_start(d["shifto_s"][l], pj[:, 0:7, :]).then_inc(smp["stored"], 16)
                sp.dma_start(d["convo_s"][l], dcnew).then_inc(smp["stored"], 16)
                sp.wait_ge(smp["dve"], AT("s_new", l))
                sp.dma_start(d["wkvo_s"][l], dS).then_inc(smp["stored"], 16)
                sp.wait_ge(smp["dve"], AT("h_new", l))
                sp.dma_start(d["ho_s"][l], dh0).then_inc(smp["stored"], 16)
            sp.wait_ge(L["layer_end"], DEPTH + 1)
            sp.dma_start(d["y_s"], xsT[:, :, :]).then_inc(smp["x_s"], 16)
            sp.wait_ge(smp["x_s"], 32)
            sp.wait_ge(L["state"], DEPTH * 96 + 16)
            sp.wait_ge(smp["stored"], DEPTH * 96)
            sp.wait_ge(L["y_out"], DEPTH * NT * 16 + 16)

        @block.tensor
        def _(pe):
            for name in PE_SEMS:
                pe.sem_inc(s[name], TILE_STEPS.get(name, 1))
            mm = nc.tensor.matmul

            def T(out, in_, rows=P):
                return nc.tensor.transpose(out, in_, ident[0:rows, 0:rows])

            def fill(out, col, width, ks):
                for k in ks:
                    last = mm(out[:, 0:width], hT[:, k, :], Win[:, k, col:col + width], start=k == 0, stop=k == KC - 1)
                return last

            with pe.Fori(0, DEPTH) as l:
                pe.wait_ge(L["silu_c"], 1)
                pe.wait_ge(L["const"], 48)
                pe.wait_ge(L["layer_end"], l + 1)
                for q in range(24):
                    pe.wait_ge(wmod_in[q % 3], (l * 8 + (q // 3 + 1)) * 16)
                    for k in range(KC):
                        last = mm(M0[:, 9 * q:9 * q + 9], wmod[q % 3][:, k, :], cT[:, k, :], start=k == 0,
                                  stop=k == KC - 1)
                    last.then_inc(L["mod_mm"], 1)
                pe.wait_ge(L["gpc"], l + 1)
                for k in range(KC):
                    last = mm((M1 if k < 4 else M2)[:, P * (k % 4):P * (k % 4) + P],
                              gpc[:, k, 0:1].to_broadcast([P, P]), ident, start=True, stop=True)
                last.then_inc(L["gp_mm"], 1)
                with pe.Fori(0, NT) as i:
                    n = l * NT + i
                    pe.wait_ge(s["xn_ready"], DONE(n))
                    pe.wait_ge(s["pT1_act"], BEFORE(n))
                    pe.wait_ge(s["pT1_dve"], BEFORE(n))
                    pe.wait_ge(L["mod_out"], l + 1)
                    for k in range(4):
                        last = T(M0[:, P * k:P * k + P], xn[:, P * k:P * k + P])
                    last.then_inc(s["xT_lo"], 1)
                    pe.wait_ge(L["gp_out"], l + 1)
                    for k in range(4, 8):
                        last = T(M1[:, P * (k - 4):P * (k - 4) + P], xn[:, P * k:P * k + P])
                    last.then_inc(s["xT_hi"], 1)
                    pe.wait_ge(s["hT_lo"], DONE(n))
                    pe.wait_ge(s["hT_hi"], DONE(n))
                    pe.wait_ge(s["o_ready"], BEFORE(n))
                    pe.wait_ge(L["win"], (l + 1) * 16)
                    fill(G0, C_R, 512, range(KC)).then_inc(s["rk_mm"], 1)
                    fill(G1, C_V, 448, range(KC)).then_inc(s["vwk_mm"], 1)
                    pe.wait_ge(s["rk_out"], DONE(n))
                    pe.wait_ge(s["ytm_ready"], BEFORE(n))
                    for k in range(4):
                        last = T(M2[:, P * k:P * k + P], stA[:, P * k:P * k + P])
                    last.then_inc(s["rkT_mm"], 1)
                    fill(G0, C_Q, 512, range(KC)).then_inc(s["q_mm"], 1)
                    pe.wait_ge(s["vwk_out"], DONE(n))
                    pe.wait_ge(s["yB_ready"], BEFORE(n))
                    T(M3[:, 0:P], stB[:, 0:P])
                    T(M3[:, P:2 * P], stB[:, P:2 * P])
                    T(M3[0:64, 2 * P:3 * P], stB[:, 256:320]).then_inc(s["vwT_mm"], 1)
                    fill(G1, C_XC, 384, range(KC)).then_inc(s["xv_mm"], 1)
                    pe.wait_ge(s["xs_ready"], DONE(n))
                    T(M1[:, 0:P], xs[:, 4, :])
                    T(M1[:, P:2 * P], xs[:, 5, :]).then_inc(s["vbT_mm"], 1)
                    pe.wait_ge(s["tw_ready"], DONE(n))
                    for k in range(4):
                        last = mm(M0[:, P * k:P * k + P], lora[:, P * k:P * k + P], tw[:, :], start=True, stop=True)
                    last.then_inc(s["lora_mm"], 1)
                    pe.wait_ge(s["sq_ready"], DONE(n))
                    pe.wait_ge(s["pB_ready"], DONE(n))
                    mm(M2[:, 0:256], ones, tmp, start=True, stop=True).then_inc(s["kksum_mm"], 1)
                    pe.wait_ge(s["xv_out"], DONE(n))
                    pe.wait_ge(s["yA_ready"], BEFORE(n))
                    T(M4[:, 0:P], stA[:, 0:P])
                    T(M4[:, P:2 * P], stA[:, P:2 * P]).then_inc(s["xcT_mm"], 1)
                    pe.wait_ge(s["q_out"], DONE(n))
                    fill(G0, C_GB, 512, range(KC)).then_inc(s["gbc_mm"], 1)
                    pe.wait_ge(s["bonus_in"], DONE(n))
                    pe.wait_ge(s["kknorm"], DONE(n))
                    mm(M2[:, 256:512], ones, bonv[:, :], start=True, stop=True).then_inc(s["bonus_mm"], 1)
                    pe.wait_ge(s["bd_ready"], DONE(n))
                    pe.wait_ge(s["a_ready"], DONE(n))
                    pe.wait_ge(s["vst_ready"], DONE(n))
                    pe.wait_ge(s["xcb_ready"], DONE(n))
                    pe.wait_ge(s["s_ready"], STEP(n, 0, 2))

                    def gram(out, a, b):
                        for u in range(U):
                            last = mm(out[:, P * u:P * u + P], a[:, u, :], b[:, u, :], start=True, stop=True)
                        return last

                    gram(M0, bti, kap).then_inc(s["g1T_mm"], 1)
                    gram(M1, kap, bti).then_inc(s["g1_mm"], 1)
                    gram(M3, kti, kap).then_inc(s["g2T_mm"], 1)
                    gram(M4, bti, rti).then_inc(s["g3T_mm"], 1)
                    gram(M5, kti, rti).then_inc(s["g4T_mm"], 1)
                    pe.wait_ge(s["ntn_ready"], DONE(n))

                    def squares(level):
                        for u in range(U):
                            last = mm(M0[:, P * u:P * u + P], NTbd[:, u, :], Nbd[:, u, :], start=True, stop=True)
                        if level < 5:
                            for u in range(U):
                                last = mm(M1[:, P * u:P * u + P], Nbd[:, u, :], NTbd[:, u, :], start=True, stop=True)
                        last.then_inc(s["inv_mm"], 1)

                    def multiply(level):
                        pe.wait_ge(s["inv_act"], STEP(n, level, 5))
                        if level > 1:
                            pe.wait_ge(s["q_dve"], STEP(n, level - 1, 4))
                        for u in range(U):
                            last = mm(M2[:, CH * u:CH * u + CH], Nbd[:, u, :], Q[:, u, :], start=True, stop=True)
                        last.then_inc(s["q_mm5"], 1)

                    squares(1)
                    pe.wait_ge(s["g_ready"], DONE(n))
                    for u in range(U):
                        T(M3[:, P * u:P * u + P], bti[:, u, :])
                    for u in range(U):
                        last = T(M4[:, P * u:P * u + P], kti[:, u, :])
                    last.then_inc(s["btT_mm"], 1)
                    fill(G1, C_GA, 512, range(0, 2))
                    pe.wait_ge(s["bonus_out"], DONE(n))
                    multiply(1)
                    pe.wait_ge(s["inv_dve"], STEP(n, 1, 4))
                    squares(2)
                    pe.wait_ge(s["conv_ready"], DONE(n))
                    pe.wait_ge(s["bt_out"], DONE(n))
                    for k in range(4):
                        last = mm(M3[:, P * k:P * k + P], gatew[:, k, :], lu[:, k % 2, :], start=True, stop=True)
                    last.then_inc(s["lru_mm"], 1)
                    pe.wait_ge(s["gbc_out"], DONE(n))
                    for k in range(4):
                        last = T(M4[:, P * k:P * k + P], stA[:, P * k:P * k + P])
                    last.then_inc(s["gbcT_mm"], 1)
                    fill(G1, C_GA, 512, range(2, 4))
                    multiply(2)
                    pe.wait_ge(s["inv_dve"], STEP(n, 2, 4))
                    squares(3)
                    fill(G1, C_GA, 512, range(4, 6))
                    pe.wait_ge(s["rope_ready"], DONE(n))
                    pe.wait_ge(s["gates_ready"], DONE(n))
                    for k in range(4):
                        last = T(M3[:, P * k:P * k + P], qk[:, P * k:P * k + P])
                    last.then_inc(s["qT_mm"], 1)
                    pe.wait_ge(s["gates_T"], DONE(n))
                    T(M4[:, 0:P], qk[:, 512:640]).then_inc(s["kT_mm"], 1)
                    multiply(3)
                    pe.wait_ge(s["inv_dve"], STEP(n, 3, 4))
                    squares(4)
                    fill(G1, C_GA, 512, range(6, 8)).then_inc(s["ga_mm"], 1)

                    def scores(j, ma, mb):
                        for g, m in ((0, ma), (1, mb)):
                            mm(m[:, :].rearrange("p (c k) -> p c k", c=2), identb[:, :], over(mk[:, :], 1, 2),
                               start=True, stop=False, skip_group_check=True)
                            for c in range(2):
                                last = mm(m[:, 256 * c:256 * c + 256], qT[HD * g:HD * g + HD, 2 * j + c, :],
                                          kT[HD * g:HD * g + HD, :], start=False, stop=True, skip_group_check=True)
                        return last

                    pe.wait_ge(s["qT_ready"], DONE(n))
                    pe.wait_ge(s["kT_ready"], DONE(n))
                    scores(0, M3, M4).then_inc(s["s0_mm"], 1)
                    multiply(4)
                    pe.wait_ge(s["inv_dve"], STEP(n, 4, 4))
                    squares(5)
                    multiply(5)
                    scores(1, M0, M1).then_inc(s["s1_mm"], 1)

                    def probs(j, ma, mb):
                        for f, m in ((0, ma), (1, mb)):
                            for k in range(4):
                                last = T(m[:, P * k:P * k + P], Pm[:, j, k, P * f:P * f + P])
                        return last

                    def values(j):
                        for k in range(4):
                            g = k % 2
                            for f in range(2):
                                last = mm(G0[:, HD * (4 * j + k):HD * (4 * j + k) + HD], PT[:, f, k, :],
                                          Vt[:, f, HD * g:HD * g + HD], start=f == 0, stop=f == 1)
                        return last

                    def chunk(m):
                        prev, new = S[:, m % 2], S[:, (m + 1) % 2]
                        for p in range(PAIRS):
                            u = NCH * p + m
                            mm(M5[:, HD * p:HD * p + HD], kap[:, u, :], prev[:, p, :], start=True, stop=False)
                            last = mm(M5[:, HD * p:HD * p + HD], G2T[:, u, :], Vst[:, u, :], start=False, stop=True)
                        last.then_inc(s["rh_mm"], 1)
                        pe.wait_ge(s["rh_ready"], STEP(n, m + 1, 2))
                        for p in range(PAIRS):
                            u = NCH * p + m
                            last = mm(M5[:, P + HD * p:P + HD * p + HD], Qbd[:, u, :], RH[:, p, :], start=True, stop=True)
                        last.then_inc(s["u_mm"], 1)

                    def chunk_end(m):
                        prev = S[:, m % 2]
                        pe.wait_ge(s["u_act"], STEP(n, m + 1, 2))
                        for p in range(PAIRS):
                            u = NCH * p + m
                            o = M2[:, HD * u:HD * u + HD]
                            mm(o, rti[:, u, :], prev[:, p, :], start=True, stop=False)
                            mm(o, G3T[:, u, :], Ub[:, p, :], start=False, stop=False)
                            mm(o, G4T[:, u, :], Vst[:, u, :], start=False, stop=True)
                        for p in range(PAIRS):
                            u = NCH * p + m
                            o = M5[:, 256 + HD * p:256 + HD * p + HD]
                            mm(o, ident, prev[:, p, :], start=True, stop=False)
                            mm(o, btk[:, u, :], Ub[:, p, :], start=False, stop=False)
                            last = mm(o, ktk[:, u, :], Vst[:, u, :], start=False, stop=True)
                        return last

                    pe.wait_ge(s["bt_out"], DONE(n))
                    pe.wait_ge(L["zeros"], l + 1)
                    pe.wait_ge(s["qbd"], DONE(n))
                    chunk(0)
                    pe.wait_ge(s["exp0"], DONE(n))
                    probs(0, M3, M4).then_inc(s["pT0_mm"], 1)
                    chunk_end(0).then_inc(s["s_mm"], 1)
                    pe.wait_ge(s["pT0_act"], DONE(n))
                    pe.wait_ge(s["pT0_dve"], DONE(n))
                    pe.wait_ge(s["gbc_out"], DONE(n))
                    values(0)
                    pe.wait_ge(s["s_ready"], STEP(n, 1, 2))
                    chunk(1)
                    pe.wait_ge(s["exp1"], DONE(n))
                    probs(1, M0, M1).then_inc(s["pT1_mm"], 1)
                    chunk_end(1).then_inc(s["y_mm"], 1)
                    pe.wait_ge(s["pT1_act"], DONE(n))
                    pe.wait_ge(s["pT1_dve"], DONE(n))
                    values(1).then_inc(s["pv_mm"], 1)
                    pe.wait_ge(s["yA_tm"], DONE(n))
                    pe.wait_ge(s["yn_ready"], DONE(n))
                    for k in range(4):
                        last = T(M4[:, P * k:P * k + P], stA[:, P * k:P * k + P])
                    last.then_inc(s["yAT_mm"], 1)
                    for u in range(U):
                        last = T(M3[0:HD, P * u:P * u + P], ytm[:, u, :])
                    last.then_inc(s["ynT_mm"], 1)
                    pe.wait_ge(s["yC_ready"], DONE(n))
                    pe.wait_ge(s["ga_out"], DONE(n))
                    pe.wait_ge(L["wout"], (l + 1) * 16)
                    pe.wait_ge(s["yA_ready"], DONE(n))
                    pe.wait_ge(s["yB_ready"], DONE(n))
                    for h, o in ((0, G1), (1, G0)):
                        for k in range(KC):
                            last = mm(o[:, :], yT[:, k, :], Wout[:, k, 512 * h:512 * h + 512], start=k == 0,
                                      stop=k == KC - 1)
                        last.then_inc(s["o1_mm"] if h else s["o0_mm"], 1)

                one = con("reset")[:, 1:2].to_broadcast([P, P])
                pe.wait_ge(s["o1_mm"], BEFORE((l + 1) * NT))
                pe.wait_ge(smp["dve"], AT("sq", l))
                for k in range(KC):
                    last = mm(M0[:, 0:B], one, dsq[:, k, :], start=k == 0, stop=k == KC - 1)
                last.then_inc(smp["pe"], 1)
                pe.wait_ge(smp["dve"], AT("h", l))
                for j, (col, width) in enumerate(DCHUNKS):
                    for k in range(KC):
                        last = mm(M1[0:width, B * j:B * j + B], Win[:, k, col:col + width], dh[:, k, :],
                                  start=k == 0, stop=k == KC - 1)
                last.then_inc(smp["pe"], 1)
                pe.wait_ge(smp["dve"], AT("proj", l))
                mm(M5[:, 0:5 * B], dcon("perm"), pj[:, 7:12, :], start=True, stop=True).then_inc(smp["pe"], 1)
                pe.wait_ge(smp["act"], AT("tw", l))
                for k in range(4):
                    last = mm(M0[:, B * k:B * k + B], lora[:, P * k:P * k + P], dtw[0:64, :], start=True, stop=True)
                last.then_inc(smp["pe"], 1)
                pe.wait_ge(smp["dve"], AT("kksq", l))
                mm(M2[:, 0:16], ones, dq1[:, :], start=True, stop=True).then_inc(smp["pe"], 1)
                pe.wait_ge(smp["dve"], AT("u", l))
                for k in range(4):
                    last = mm(M3[:, B * k:B * k + B], gatew[:, k, :], du[:, k % 2, :], start=True, stop=True)
                last.then_inc(smp["pe"], 1)
                pe.wait_ge(smp["dve"], AT("bonus_in", l))
                mm(M4[:, 0:16], ones, dq2[:, :], start=True, stop=True).then_inc(smp["pe"], 1)
                pe.wait_ge(smp["dve"], AT("skk", l))
                pe.wait_ge(smp["act"], AT("gates", l))
                pe.wait_ge(smp["act"], AT("kknorm", l))
                mm(M2[:, :], ones, dT1[:, 0:512], start=True, stop=True)
                mm(M3[:, :], ones, dT1[:, 512:1024], start=True, stop=True).then_inc(smp["pe"], 1)
                pe.wait_ge(smp["dve"], AT("vdiag", l))
                pe.wait_ge(smp["dve"], AT("qrows", l))
                mm(M4[:, :], ones, dT2[:, 0:512], start=True, stop=True)
                mm(M5[:, :], ones, dT2[:, 512:1024], start=True, stop=True).then_inc(smp["pe"], 1)
                pe.wait_ge(smp["dve"], AT("sr", l))
                mm(M2[:, :], ones, dT1[:, 0:512], start=True, stop=True)
                mm(M3[:, :], ones, dT1[:, 512:1024], start=True, stop=True).then_inc(smp["pe"], 1)
                pe.wait_ge(smp["dve"], AT("qrows", l))
                pe.wait_ge(smp["kv_in"], (l + 1) * 96)
                for b in range(B):
                    last = mm(M4[0:64, 0:P + 1], stB[:, 64 * b:64 * b + 64], KTs[:, b, :], start=b == 0, stop=b == B - 1)
                last.then_inc(smp["pe"], 1)
                pe.wait_ge(smp["dve"], AT("y", l))
                mm(M0[:, 0:16], ones, dyv[:, :], start=True, stop=True).then_inc(smp["pe"], 1)
                pe.wait_ge(smp["dve"], AT("ysq", l))
                mm(M0[:, 16:32], ones, dq1[:, :], start=True, stop=True).then_inc(smp["pe"], 1)
                pe.wait_ge(smp["dve"], AT("pd", l))
                T(M1[0:8, 64:64 + P], pj[:, 14, :])
                mm(M1[0:8, 0:64], dcon("rowb")[0:64, :], dg64[0:64, :], start=True, stop=True)
                T(M5[:, 0:64], Pd[0:64, 0:P], 64).then_inc(smp["pe"], 1)
                pe.wait_ge(smp["dve"], AT("pt", l))
                mm(M2[:, 0:64], Vnd[0:8, :], Pnd[0:8, :], start=True, stop=False, skip_group_check=True)
                for b in range(B):
                    last = mm(M2[:, 8 * b:8 * b + 8], Vc[:, b, :], PTd[:, 8 * b:8 * b + 8], start=False, stop=True,
                              skip_group_check=True)
                last.then_inc(smp["pe"], 1)
                pe.wait_ge(smp["dve"], AT("ys", l))
                for m in range(KC):
                    for k in range(KC):
                        last = mm(M3[:, B * m:B * m + B], Wout[:, k, P * m:P * m + P], ys[:, k, :], start=k == 0,
                                  stop=k == KC - 1)
                last.then_inc(smp["pe"], 1)
                pe.wait_ge(smp["dve"], AT("osq", l))
                for k in range(KC):
                    last = mm(M4[:, 0:B], one, dsq[:, k, :], start=k == 0, stop=k == KC - 1)
                last.then_inc(smp["pe"], 1)

        @block.scalar
        def _(act):
            for name in ACT_SEMS:
                act.sem_inc(s[name], TILE_STEPS.get(name, 1))
            A = nc.scalar.activation
            link = Link(act, L["act_t"], 1)
            act.wait_ge(L["const"], 48)
            A(cT[:, :, :], cT[:, :, :], ACT.Silu).then_inc(L["silu_c"], 1)
            A(identb[:, :], ident, ACT.Copy).then_inc(L["cast"], 1)
            A(mkprev[:, :, :], RB[:, 0:256].rearrange("p (a b) -> p a b", a=2), ACT.Copy).then_inc(L["cast"], 1)
            A(mk[:, P:2 * P], RB[:, 256:384], ACT.Copy).then_inc(L["cast"], 1)
            with act.Fori(0, DEPTH) as l:
                act.wait_ge(s["o1_mm"], BEFORE(l * NT))
                act.wait_ge(L["layer_end"], l + 1)
                act.dma_start(prm[:, :], d["prm"][l]).then_inc(L["prm"], 16)
                act.dma_start(lora[:, :], d["lora"][l]).then_inc(L["prm"], 16)
                act.dma_start(gatew[:, :, :], d["gatew"][l]).then_inc(L["prm"], 16)
                act.wait_ge(L["cast"], 3)
                act.wait_ge(L["y_out"], l * NT * 16 + 16)
                for q in range(24):
                    if q >= 3:
                        act.wait_ge(L["mod_mm"], l * 24 + (q - 2))
                    act.dma_start(wmod[q % 3], d["w_mod"][l, q]).then_inc(wmod_in[q % 3], 16)
                act.dma_start(Win[:, :, :], d["w_in"][l]).then_inc(L["win"], 16)
                act.dma_start(Wout[:, :, :], d["w_out"][l]).then_inc(L["wout"], 16)
                act.wait_ge(L["sp1"], l + 1)
                A(spc[:, 1, :], spc[:, 0, :], ACT.Exp, scale=-1.0).then_inc(L["sp2"], 1)
                act.wait_ge(L["sp1"], l + 1)
                act.wait_ge(L["sp3"], 2 * l + 1)
                A(spc[:, 5, :], spc[:, 2, :], ACT.Ln).then_inc(L["sp2"], 1)
                with act.Fori(0, NT) as i:
                    n = l * NT + i
                    act.wait_ge(L["x_in"], (n + 1) * 16)
                    act.wait_ge(s["pv_mm"], BEFORE(n))
                    act.wait_ge(s["o_root"], BEFORE(n))
                    act.wait_ge(L["mod_mm"], (l + 1) * 24)
                    A(RB[:, :], xa[:, :], ACT.Square, accum_out=small[:, 0:1]).then_inc(s["x_squared"], 1)
                    act.wait_ge(s["rms_root"], BEFORE(n))
                    act.wait_ge(L["dve_t"], n * DVE_T + 1)
                    A(small[:, 2:3], small[:, 1:2], ACT.Sqrt).then_inc(s["rms_root"], 1)
                    act.wait_ge(s["xT_lo"], DONE(n))
                    act.wait_ge(L["mod_out"], l + 1)
                    for k in range(4):
                        last = A(hT[:, k, :], M0[:, P * k:P * k + P], ACT.Identity, bias=mod[:, k, 0:1],
                                 scale=gs[:, k, 0:1])
                    last.then_inc(s["hT_lo"], 1)
                    act.wait_ge(s["rk_mm"], DONE(n))
                    A(stA[:, :], G0[:, :], ACT.Copy).then_inc(s["rk_out"], 1)
                    act.wait_ge(s["vwk_mm"], DONE(n))
                    act.wait_ge(s["yA_tm"], BEFORE(n))
                    A(stB[:, 0:320], G1[:, 0:320], ACT.Copy)
                    A(qk[:, 512:640], G1[:, 320:448], ACT.Copy).then_inc(s["vwk_out"], 1)
                    act.wait_ge(s["rkT_mm"], DONE(n))
                    act.wait_ge(s["carried"], BEFORE(n))
                    act.wait_ge(L["zeros"], l + 1)
                    A(pB[:, 0:4, 1:P + 1], M2[:, :].rearrange("p (c t) -> p c t", c=4), ACT.Copy)
                    act.wait_ge(s["vwT_mm"], DONE(n))
                    A(pB[:, 4:6, 1:P + 1], M3[:, 0:256].rearrange("p (c t) -> p c t", c=2), ACT.Copy)
                    A(pB[0:64, 6, 1:P + 1], M3[0:64, 256:384], ACT.Copy).then_inc(s["pB_ready"], 1)
                    act.wait_ge(s["q_mm"], DONE(n))
                    A(qk[:, 0:512], G0[:, :], ACT.Copy).then_inc(s["q_out"], 1)
                    act.wait_ge(s["xv_mm"], DONE(n))
                    act.wait_ge(s["window_moved"], BEFORE(n))
                    A(stA[:, 0:256], G1[:, 0:256], ACT.Copy)
                    A(Vt[:, 1, :], G1[:, 256:384], ACT.Copy).then_inc(s["xv_out"], 1)
                    act.wait_ge(s["xs_ready"], DONE(n))
                    A(tw[0:32, :], xs[0:32, 6, :], ACT.Tanh)
                    A(tw[32:64, :], xs[32:64, 6, :], ACT.Copy).then_inc(s["tw_ready"], 1)
                    act.wait_ge(s["lora_mm"], DONE(n))
                    act.wait_ge(s["y_mm"], BEFORE(n))
                    for p in range(PAIRS):
                        last = A(sgw[:, P * p:P * p + P], M0[:, P * p:P * p + P], ACT.Sigmoid, bias=par("w0")[:, p:p + 1])
                    last.then_inc(s["sgw_ready"], 1)
                    for p in range(PAIRS):
                        last = A(av[:, P * p:P * p + P], M0[:, 256 + P * p:256 + P * p + P], ACT.Sigmoid,
                                 bias=par("a0")[:, p:p + 1])
                    last.then_inc(s["a_ready"], 1)
                    act.wait_ge(s["xcT_mm"], DONE(n))
                    act.wait_ge(s["conv_ready"], BEFORE(n))
                    A(xcb[:, :, 3:P + 3], M4[:, 0:256].rearrange("p (c t) -> p c t", c=2), ACT.Copy)\
                        .then_inc(s["xcb_ready"], 1)
                    act.wait_ge(s["kksum_mm"], DONE(n))
                    A(kkv, M2[:, 0:256], ACT.Sqrt).then_inc(s["kknorm"], 1)
                    act.wait_ge(s["cum_ready"], DONE(n))
                    A(Em, cum, ACT.Exp, scale=DECAY)
                    A(Ep[:, :], cum, ACT.Exp, scale=-DECAY)
                    A(Ex, cx, ACT.Exp, scale=-DECAY).then_inc(s["exps_ready"], 1)
                    act.wait_ge(s["gbc_mm"], DONE(n))
                    A(stA[:, :], G0[:, :], ACT.Silu).then_inc(s["gbc_out"], 1)
                    def power(level):
                        act.wait_ge(s["inv_mm"], STEP(n, level, 5))
                        if level > 1:
                            act.wait_ge(s["q_mm5"], STEP(n, level - 1, 5))
                        A(Nbd, M0[:, :].rearrange("p (u c) -> p u c", c=P), ACT.Copy).then_inc(s["inv_act"], 1)
                    power(1)
                    act.wait_ge(s["btT_mm"], DONE(n))
                    A(btk, M3[:, :].rearrange("p (u c) -> p u c", c=P), ACT.Copy)
                    A(ktk, M4[:, :].rearrange("p (u c) -> p u c", c=P), ACT.Copy).then_inc(s["bt_out"], 1)
                    power(2)
                    act.wait_ge(s["gbcT_mm"], DONE(n))
                    act.wait_ge(s["o1_mm"], BEFORE(n))
                    A(yT[:, 4:8, :], M4[:, :].rearrange("p (c t) -> p c t", c=4), ACT.Copy).then_inc(s["gates_T"], 1)
                    act.wait_ge(s["lru_mm"], DONE(n))
                    for c in range(2):
                        A(lgr[:, c, :], M3[:, P * c:P * c + P], ACT.Sigmoid, bias=par("gab")[:, c:c + 1])
                        last = A(lgi[:, c, :], M3[:, 256 + P * c:256 + P * c + P], ACT.Sigmoid, bias=par("gxb")[:, c:c + 1])
                    last.then_inc(s["gates_ready"], 1)
                    act.wait_ge(s["gates_ready"], DONE(n))
                    act.wait_ge(L["y_out"], n * 16 + 16)
                    power(3)
                    for c in range(2):
                        A(lth[:, c, :], lgr[:, c, :], ACT.Tanh, scale=spc[:, 9, c:c + 1])
                        last = A(laa[:, c, :], lgr[:, c, :], ACT.Exp, scale=spc[:, 9, c:c + 1])
                    link.start(n)
                    link(last)
                    link.end()
                    A(la2, laa, ACT.Square).then_inc(s["lru_exps"], 1)
                    act.wait_ge(s["qT_mm"], DONE(n))
                    A(qT[:, :, :], M3[:, :].rearrange("p (c t) -> p c t", c=4), ACT.Copy).then_inc(s["qT_ready"], 1)
                    act.wait_ge(s["kT_mm"], DONE(n))
                    A(kT[:, P:2 * P], M4[:, 0:P], ACT.Copy).then_inc(s["kT_ready"], 1)
                    power(4)
                    act.wait_ge(s["lru_t"], DONE(n))
                    A(lth, lth, ACT.Sqrt, scale=-1.0).then_inc(s["lru_root"], 1)
                    act.wait_ge(s["ga_mm"], DONE(n))
                    A(stB[:, :], G1[:, :], ACT.Silu).then_inc(s["ga_out"], 1)
                    power(5)

                    def exps(j, ma, mb, neg, es, done):
                        act.wait_ge(neg, DONE(n))
                        if j == 0:
                            act.wait_ge(s["yC_ready"], DONE(n))
                        A(small[:, 40 + 4 * j:44 + 4 * j], small[:, 32 + 4 * j:36 + 4 * j], ACT.Exp).then_inc(es, 1)
                        for k in range(4):
                            m = mb if k % 2 else ma
                            last = A(Pm[:, j, k, :], m[:, 256 * (k // 2):256 * (k // 2) + 256], ACT.Exp,
                                     bias=small[:, 16 + 4 * j + k:17 + 4 * j + k], scale=SCALE,
                                     accum_out=small[:, 24 + 4 * j + k:25 + 4 * j + k])
                        last.then_inc(done, 1)

                    exps(0, M3, M4, s["neg0"], s["es0"], s["exp0"])
                    act.wait_ge(s["u_mm"], STEP(n, 1, 2))
                    A(Ub[:, :, :], M5[:, P:2 * P].rearrange("p (a b) -> p a b", a=2), ACT.Copy).then_inc(s["u_act"], 1)
                    act.wait_ge(s["pT0_mm"], DONE(n))
                    A(PT[:, 0, :, :], M3[:, :].rearrange("p (k q) -> p k q", k=4), ACT.Copy).then_inc(s["pT0_act"], 1)
                    exps(1, M0, M1, s["neg1"], s["es1"], s["exp1"])
                    act.wait_ge(s["u_mm"], STEP(n, 2, 2))
                    A(Ub[:, :, :], M5[:, P:2 * P].rearrange("p (a b) -> p a b", a=2), ACT.Copy).then_inc(s["u_act"], 1)
                    act.wait_ge(s["pT1_mm"], DONE(n))
                    A(PT[:, 0, :, :], M0[:, :].rearrange("p (k q) -> p k q", k=4), ACT.Copy).then_inc(s["pT1_act"], 1)
                    act.wait_ge(s["ytm_ready"], DONE(n))
                    A(Q[:, :, :], ytm[:, :, :], ACT.Square).then_inc(s["y_sq"], 1)
                    act.wait_ge(L["dve_t"], n * DVE_T + YVAR)
                    A(small[:, 56:60], small[:, 52:56], ACT.Sqrt).then_inc(s["y_root"], 1)
                    act.wait_ge(s["yAT_mm"], DONE(n))
                    A(yT[:, 0:4, :], M4[:, :].rearrange("p (c t) -> p c t", c=4), ACT.Copy).then_inc(s["yA_ready"], 1)
                    act.wait_ge(s["o0_mm"], DONE(n))
                    A(RB[:, 0:512], G1[:, :], ACT.Square, accum_out=small[:, 3:4])
                    act.wait_ge(s["o1_mm"], DONE(n))
                    A(RB[:, 512:1024], G0[:, :], ACT.Square, accum_out=small[:, 4:5]).then_inc(s["o_squared"], 1)
                    act.wait_ge(L["dve_t"], n * DVE_T + OVAR)
                    A(small[:, 6:7], small[:, 5:6], ACT.Sqrt).then_inc(s["o_root"], 1)

                act.wait_ge(smp["dve"], AT("ms", l))
                A(dr2[:, :], dr1[:, :], ACT.Sqrt).then_inc(smp["act"], 1)
                act.wait_ge(smp["dve"], AT("proj", l))
                A(dsg[:, :, :], pj[:, 15:23, :], ACT.Silu).then_inc(smp["act"], 1)
                act.wait_ge(smp["dve"], AT("xs", l))
                A(dtw[0:32, :], dx[0:32, 6, :], ACT.Tanh)
                A(dtw[32:64, :], dx[32:64, 6, :], ACT.Copy).then_inc(smp["act"], 1)
                act.wait_ge(smp["pe"], AT("lora_mm", l))
                for p in range(PAIRS):
                    A(dw[:, p, :], M0[:, B * p:B * p + B], ACT.Sigmoid, bias=par("w0")[:, p:p + 1])
                    last = A(da[:, p, :], M0[:, 16 + B * p:16 + B * p + B], ACT.Sigmoid, bias=par("a0")[:, p:p + 1])
                last.then_inc(smp["act"], 1)
                act.wait_ge(smp["act"], AT("sig", l))
                A(dw[:, :, :], dw[:, :, :], ACT.Exp, scale=-DECAY).then_inc(smp["act"], 1)
                act.wait_ge(smp["pe"], AT("kk_mm", l))
                A(dkk[:, :], M2[:, 0:16], ACT.Sqrt).then_inc(smp["act"], 1)
                act.wait_ge(smp["pe"], AT("lru_mm", l))
                for c in range(2):
                    A(dgr[:, c, :], M3[:, B * c:B * c + B], ACT.Sigmoid, bias=par("gab")[:, c:c + 1])
                    last = A(dgi[:, c, :], M3[:, 16 + B * c:16 + B * c + B], ACT.Sigmoid, bias=par("gxb")[:, c:c + 1])
                last.then_inc(smp["act"], 1)
                act.wait_ge(smp["act"], AT("gates", l))
                for c in range(2):
                    A(dth[:, c, :], dgr[:, c, :], ACT.Tanh, scale=spc[:, 9, c:c + 1])
                    last = A(daa[:, c, :], dgr[:, c, :], ACT.Exp, scale=spc[:, 9, c:c + 1])
                last.then_inc(smp["act"], 1)
                act.wait_ge(smp["dve"], AT("lru_t", l))
                A(dth[:, :, :], dth[:, :, :], ACT.Sqrt, scale=-1.0).then_inc(smp["act"], 1)
                act.wait_ge(smp["dve"], AT("neg", l))
                A(dm[0:64, 5:6], dm[0:64, 3:4], ACT.Exp)
                A(Pd[0:64, :], M4[0:64, 0:P + 1], ACT.Exp, bias=dm[0:64, 2:3], scale=SCALE,
                  accum_out=dm[0:64, 4:5]).then_inc(smp["act"], 1)
                act.wait_ge(smp["dve"], AT("var", l))
                A(dq2[:, :], dq1[:, :], ACT.Sqrt).then_inc(smp["act"], 1)
                act.wait_ge(smp["dve"], AT("oms", l))
                A(dr2[:, :], dr1[:, :], ACT.Sqrt).then_inc(smp["act"], 1)

        @block.vector
        def _(dve):
            for name in DVE_SEMS:
                dve.sem_inc(s[name], TILE_STEPS.get(name, 1))
            tt, stt, ts = nc.vector.tensor_tensor, nc.vector.scalar_tensor_tensor, nc.vector.tensor_scalar
            cp, red, rcp, ms = nc.vector.tensor_copy, nc.vector.tensor_reduce, nc.vector.reciprocal, nc.vector.memset
            dve.wait_ge(L["const"], 48)
            for t in (kap, bti, kti, rti):
                ms(t[:, :, :], 0.0)
            ms(pB[:, :, :], 0.0)
            ms(xs[:, :, :], 0.0).then_inc(L["cleared"], 1)
            dve.wait_ge(L["cleared"], 1)
            dve.wait_ge(L["cast"], 3)
            link = Link(dve, L["dve_t"], DVE_T)
            ll = Link(dve, L["dve_l"], DVE_L)
            dl = Link(dve, L["dve_d"], DVE_D)
            dve.sem_inc(L["layer_end"], 1)
            with dve.Fori(0, DEPTH) as l:
                ll.start(l)
                dve.wait_ge(L["state"], l * 96 + 16)
                ms(pB[:, :, 0:1], 0.0)
                ms(kT[:, 0:P], 0.0)
                ms(Vt[:, 0, :], 0.0)
                ms(S[:, 0, :, :], 0.0)
                ms(xcb[:, :, 0:3], 0.0)
                ms(hcar[:, :], 0.0)
                ms(flag[:, :], 1.0)
                cp(mk[:, 0:P], mkprev[:, 0, :]).then_inc(L["zeros"], 1)
                dve.wait_ge(L["zeros"], l + 1)
                dve.wait_ge(L["prm"], (l + 1) * 48)
                lam = par("lam")
                ll(ts(spc[:, 10, :], lam, -1.0, None, ALU.mult))
                tt(spc[:, 0, :], lam, spc[:, 10, :], ALU.max).then_inc(L["sp1"], 1)
                dve.wait_ge(L["sp2"], 2 * l + 1)
                ll(ts(spc[:, 2, :], spc[:, 1, :], 1.0, None, ALU.add))
                ll(ts(spc[:, 3, :], spc[:, 2, :], -1.0, None, ALU.add))
                ts(spc[:, 4, :], spc[:, 3, :], 0.0, None, ALU.is_equal).then_inc(L["sp3"], 1)
                dve.wait_ge(L["sp3"], 2 * l + 1)
                ll(tt(spc[:, 3, :], spc[:, 3, :], spc[:, 4, :], ALU.add))
                ll(rcp(spc[:, 6, :], spc[:, 3, :]))
                ll(tt(spc[:, 6, :], spc[:, 6, :], spc[:, 1, :], ALU.mult))
                dve.wait_ge(L["sp2"], 2 * l + 2)
                ll(tt(spc[:, 6, :], spc[:, 6, :], spc[:, 5, :], ALU.mult))
                ll(tt(spc[:, 7, :], spc[:, 4, :], spc[:, 1, :], ALU.mult))
                ll(tt(spc[:, 6, :], spc[:, 6, :], spc[:, 7, :], ALU.add))
                ll(ts(spc[:, 8, :], spc[:, 10, :], 0.0, None, ALU.max))
                ll(tt(spc[:, 8, :], spc[:, 8, :], spc[:, 6, :], ALU.add))
                ts(spc[:, 9, :], spc[:, 8, :], -LRU_C, None, ALU.mult).then_inc(L["sp3"], 1)
                dve.wait_ge(L["sp3"], 2 * l + 2)
                dve.wait_ge(L["mod_mm"], (l + 1) * 24)
                ll(tt(mod[:, :, :], M0[:, 0:216].rearrange("p (q b) -> p q b", q=24), over(par("bmod"), 2, 9), ALU.add))
                ll(ts(gs[:, :, :], mod[:, 8:16, :], 1.0, None, ALU.add))
                tt(gs[:, :, :], gs[:, :, :], over(par("npre"), 2, 9), ALU.mult).then_inc(L["mod_out"], 1)
                tt(gpc[:, :, :], mod[:, 16:24, :], over(par("npost"), 2, 9), ALU.mult).then_inc(L["gpc"], 1)
                dve.wait_ge(L["gp_mm"], l + 1)
                cp(gp[:, 0:512], M1[:, :])
                cp(gp[:, 512:1024], M2[:, :]).then_inc(L["gp_out"], 1)
                ll.end()
                with dve.Fori(0, NT) as i:
                    n = l * NT + i
                    link.start(n)
                    dve.wait_ge(L["gp_out"], l + 1)
                    dve.wait_ge(s["x_squared"], DONE(n))
                    link(ts(small[:, 1:2], small[:, 0:1], 1.0 / D, EPS, ALU.mult, ALU.add))
                    assert link.k == 1
                    dve.wait_ge(s["rms_root"], DONE(n))
                    link(rcp(small[:, 7:8], small[:, 2:3]))
                    ts(xn, xa[:, :], small[:, 7:8], None, ALU.mult).then_inc(s["xn_ready"], 1)
                    dve.wait_ge(s["xT_hi"], DONE(n))
                    for k in range(4, 8):
                        last = ts(hT[:, k, :], M1[:, P * (k - 4):P * (k - 4) + P], gs[:, k, 0:1], mod[:, k, 0:1],
                                  ALU.mult, ALU.add)
                    last.then_inc(s["hT_hi"], 1)
                    dve.wait_ge(s["pB_ready"], DONE(n))
                    dve.wait_ge(s["bonus_out"], BEFORE(n))
                    tt(xs[:, 0:6, :], pB[:, 0:6, 0:P], pB[:, 0:6, 1:P + 1], ALU.subtract)
                    link(tt(xs[0:64, 6, :], pB[0:64, 6, 0:P], pB[0:64, 6, 1:P + 1], ALU.subtract))
                    mu = par("mu")
                    link(tt(xs[:, :, :], xs[:, :, :], over(mu, 2, P), ALU.mult))
                    tt(xs[:, 0:6, :], xs[:, 0:6, :], pB[:, 0:6, 1:P + 1], ALU.add)
                    tt(xs[0:64, 6, :], xs[0:64, 6, :], pB[0:64, 6, 1:P + 1], ALU.add).then_inc(s["xs_ready"], 1)
                    dve.wait_ge(s["xs_ready"], DONE(n))
                    cp(pB[:, :, 0:1], pB[:, :, P:P + 1]).then_inc(s["carried"], 1)
                    xsk = xs[:, 2:4, :].rearrange("p c t -> p (c t)")
                    xsr = xs[:, 0:2, :].rearrange("p c t -> p (c t)")
                    xsv = xs[:, 4:6, :].rearrange("p c t -> p (c t)")
                    dve.wait_ge(s["y_mm"], BEFORE(n))
                    link(tt(kkr.rearrange("p (c t) -> p c t", c=2), xs[:, 2:4, :], over(par("kk"), 2, P), ALU.mult))
                    tt(tmp, kkr, kkr, ALU.mult).then_inc(s["sq_ready"], 1)
                    dve.wait_ge(s["vbT_mm"], DONE(n))
                    vv = Vst[:, :, :].rearrange("p (a m) v -> p a m v", m=NCH)
                    mv = M1[:, 0:256].rearrange("p (a h v) -> p a h v", a=PAIRS, h=2)
                    for m in range(NCH):
                        for h in range(2):
                            last = cp(vv[HD * h:HD * h + HD, :, m, :], mv[CH * m:CH * m + CH, :, h, :])
                    last.then_inc(s["vst_ready"], 1)
                    dve.wait_ge(s["sgw_ready"], DONE(n))
                    link(nc.vector.tensor_tensor_scan(cum, con("reset"), sgw, 0.0, ALU.mult, ALU.add))
                    tt(cx, cum, sgw, ALU.subtract).then_inc(s["cum_ready"], 1)
                    dve.wait_ge(s["kknorm"], DONE(n))
                    link(ts(kkv, kkv, 1e-12, None, ALU.max))
                    link(rcp(kkv, kkv))
                    link(tt(kkv, kkr, kkv, ALU.mult))
                    dve.wait_ge(s["a_ready"], DONE(n))
                    v3 = lambda t: t.rearrange("p (c t) -> p c t", c=2)
                    link(stt(v3(kmod), v3(av), -1.0, over(par("ka"), 2, P), ALU.add, ALU.mult))
                    link(stt(kmod, kmod, 1.0, xsk, ALU.add, ALU.mult))
                    link(tt(av, av, kkv, ALU.mult))
                    link(tt(v3(bonv[:, :]), xs[:, 0:2, :], over(par("rk"), 2, P), ALU.mult))
                    tt(bonv[:, :], bonv[:, :], kmod, ALU.mult).then_inc(s["bonus_in"], 1)
                    dve.wait_ge(s["exps_ready"], DONE(n))
                    for h in range(2):
                        r = slice(HD * h, HD * h + HD)
                        v4 = lambda t: t[r, :].rearrange("p (u c) -> p u c", c=CH)
                        tt(kap[r, :, r], v4(kkv), v4(Ex), ALU.mult)
                        tt(bti[r, :, r], v4(av), v4(Em), ALU.mult)
                        tt(kti[r, :, r], v4(kmod), v4(Em), ALU.mult)
                        last = tt(rti[r, :, r], v4(xsr), v4(Ep), ALU.mult)
                    last.then_inc(s["bd_ready"], 1)
                    dve.wait_ge(s["bd_ready"], DONE(n))
                    dve.wait_ge(s["q_out"], DONE(n))
                    dve.wait_ge(s["vwk_out"], DONE(n))
                    dve.wait_ge(L["rope_in"], (n + 1) * 16)
                    q4 = qk[:, :].rearrange("p (h a f) -> p h a f", a=2, f=HALF)
                    r4 = rot.rearrange("p (h a f) -> p h a f", a=2, f=HALF)
                    tt(r4[:, :, 0, :], q4[:, :, 1, :], over(rope[:, 32:64], 1, 10), ALU.mult)
                    link(tt(r4[:, :, 1, :], q4[:, :, 0, :], over(rope[:, 32:64], 1, 10), ALU.mult))
                    link(tt(qk[:, :].rearrange("p (h f) -> p h f", f=HALF),
                            qk[:, :].rearrange("p (h f) -> p h f", f=HALF), over(rope[:, 0:32], 1, 20), ALU.mult))
                    tt(q4[:, :, 0, :], q4[:, :, 0, :], r4[:, :, 0, :], ALU.subtract)
                    tt(q4[:, :, 1, :], q4[:, :, 1, :], r4[:, :, 1, :], ALU.add).then_inc(s["rope_ready"], 1)
                    u3 = lambda m: m[:, :].rearrange("p (u c) -> p u c", c=P)
                    dve.wait_ge(s["g1T_mm"], DONE(n))
                    stt(NTbd, u3(M0), -1.0, over(con("mst"), 1, U), ALU.mult, ALU.mult)
                    dve.wait_ge(s["g1_mm"], DONE(n))
                    stt(Nbd, u3(M1), -1.0, over(con("ms"), 1, U), ALU.mult, ALU.mult).then_inc(s["ntn_ready"], 1)
                    dve.wait_ge(s["ntn_ready"], DONE(n))
                    for h in range(2):
                        r = slice(HD * h, HD * h + HD)
                        last = tt(Q[r, :, :], NTbd[r, :, r], over(ident[r, r], 1, U), ALU.add)
                    link(last)
                    dve.wait_ge(s["o_ready"], BEFORE(n))
                    dve.wait_ge(s["g2T_mm"], DONE(n))
                    tt(G2T, u3(M3), over(con("mst"), 1, U), ALU.mult)
                    dve.wait_ge(s["g3T_mm"], DONE(n))
                    tt(G3T, u3(M4), over(con("mit"), 1, U), ALU.mult)
                    dve.wait_ge(s["g4T_mm"], DONE(n))
                    tt(G4T, u3(M5), over(con("mit"), 1, U), ALU.mult).then_inc(s["g_ready"], 1)
                    dve.wait_ge(s["bonus_mm"], DONE(n))
                    tt(bonv[:, :], M2[:, 256:512], xsv, ALU.mult).then_inc(s["bonus_out"], 1)

                    def power_T(level):
                        dve.wait_ge(s["inv_mm"], STEP(n, level, 5))
                        cp(NTbd, u3(M1)).then_inc(s["inv_dve"], 1)

                    def product(level):
                        dve.wait_ge(s["q_mm5"], STEP(n, level, 5))
                        tt(Q[:, :, :], Q[:, :, :], M2[:, 0:256].rearrange("p (u c) -> p u c", c=CH), ALU.add)\
                            .then_inc(s["q_dve"], 1)

                    power_T(1)
                    dve.wait_ge(s["xcb_ready"], DONE(n))
                    cw, cb = par("cw"), par("cb")
                    for c in range(2):
                        last = ts(lu[:, c, :], xcb[:, c, 0:P], cw[:, c:c + 1], cb[:, c:c + 1], ALU.mult, ALU.add)
                    link(last)
                    for t in range(1, 4):
                        for c in range(2):
                            last = stt(lu[:, c, :], xcb[:, c, t:t + P], cw[:, 2 * t + c:2 * t + c + 1], lu[:, c, :],
                                       ALU.mult, ALU.add)
                        link(last)
                    cp(xcb[:, :, 0:3], xcb[:, :, P:P + 3]).then_inc(s["conv_ready"], 1)
                    product(1)
                    power_T(2)
                    product(2)
                    power_T(3)
                    dve.wait_ge(s["lru_exps"], DONE(n))
                    stt(lth, la2, 1.0, lth, ALU.add, ALU.mult).then_inc(s["lru_t"], 1)
                    product(3)
                    power_T(4)
                    dve.wait_ge(s["lru_root"], DONE(n))
                    ts(lth[:, :, 0:1], lth[:, :, 0:1], flag[:, 0:1], None, ALU.max)
                    link(tt(la2, lgi, lu, ALU.mult))
                    tt(la2, la2, lth, ALU.mult)
                    link(ms(flag[:, :], 0.0))
                    for c in range(2):
                        last = nc.vector.tensor_tensor_scan(lh[:, c, :], laa[:, c, :], la2[:, c, :], hcar[:, c:c + 1],
                                                            ALU.mult, ALU.add)
                    link(last)
                    cp(hcar[:, :].unsqueeze(2), lh[:, :, P - 1:P])
                    dve.wait_ge(s["gates_T"], DONE(n))
                    tt(yT[:, 6:8, :], yT[:, 6:8, :], lh, ALU.mult).then_inc(s["yC_ready"], 1)

                    def maxima(j, ma, mb, ready, neg):
                        dve.wait_ge(ready, DONE(n))
                        mx = small[:, 8 + 4 * j:12 + 4 * j].rearrange("p (c g) -> p c g", g=2)
                        for g, m in ((0, ma), (1, mb)):
                            last = red(mx[:, :, g], m[:, :].rearrange("p (c k) -> p c k", c=2), AX_X, ALU.max)
                        link(last)
                        m4, sk = small[:, 8 + 4 * j:12 + 4 * j], par("sink")[:, 4 * j:4 * j + 4]
                        link(stt(m4, m4, SCALE, sk, ALU.mult, ALU.max))
                        ts(small[:, 16 + 4 * j:20 + 4 * j], m4, -1.0, None, ALU.mult)
                        tt(small[:, 32 + 4 * j:36 + 4 * j], sk, m4, ALU.subtract).then_inc(neg, 1)

                    maxima(0, M3, M4, s["s0_mm"], s["neg0"])
                    product(4)
                    dve.wait_ge(s["q_mm5"], STEP(n, 5, 5))
                    link(ms(Qbd, 0.0))
                    for h in range(2):
                        r = slice(HD * h, HD * h + HD)
                        last = tt(Qbd[r, :, r], Q[r, :, :], M2[r, 0:256].rearrange("p (u c) -> p u c", c=CH), ALU.add)
                    last.then_inc(s["qbd"], 1)

                    def rhs(m):
                        dve.wait_ge(s["rh_mm"], STEP(n, m + 1, 2))
                        ts(RH[:, :, :], M5[:, 0:P].rearrange("p (a b) -> p a b", a=2), -1.0, None, ALU.mult)\
                            .then_inc(s["rh_ready"], 1)

                    def state(m, ready, value):
                        dve.wait_ge(ready, value)
                        pend = Ep[:, :].rearrange("p (a t) -> p a t", a=2)[:, :, CH * m + CH - 1:CH * m + CH]
                        tt(S[:, (m + 1) % 2, :, :], M5[:, 256:384].rearrange("p (a b) -> p a b", a=2),
                           pend.to_broadcast([P, 2, HD]), ALU.mult).then_inc(s["s_ready"], 1)

                    rhs(0)
                    maxima(1, M0, M1, s["s1_mm"], s["neg1"])
                    dve.wait_ge(s["pT0_mm"], DONE(n))
                    cp(PT[:, 1, :, :], M4[:, :].rearrange("p (k q) -> p k q", k=4)).then_inc(s["pT0_dve"], 1)
                    state(0, s["s_mm"], DONE(n))
                    rhs(1)
                    dve.wait_ge(s["pT1_mm"], DONE(n))
                    cp(PT[:, 1, :, :], M1[:, :].rearrange("p (k q) -> p k q", k=4)).then_inc(s["pT1_dve"], 1)
                    state(1, s["y_mm"], DONE(n))
                    link(red(small[:, 48:52], M2[:, 0:256].rearrange("p (u v) -> p u v", v=HD), AX_X, ALU.add))
                    link(ts(small[:, 48:52], small[:, 48:52], -1.0 / HD, None, ALU.mult))
                    tt(ytm[:, :, :], M2[:, 0:256].rearrange("p (u v) -> p u v", v=HD), over(small[:, 48:52], 2, HD),
                       ALU.add).then_inc(s["ytm_ready"], 1)
                    dve.wait_ge(s["exp1"], DONE(n))
                    link(tt(small[:, 24:32], small[:, 24:32], small[:, 40:48], ALU.add))
                    link(rcp(small[:, 24:32], small[:, 24:32]))
                    dve.wait_ge(s["y_sq"], DONE(n))
                    link(red(small[:, 52:56], Q[:, :, :], AX_X, ALU.add))
                    link(ts(small[:, 52:56], small[:, 52:56], 1.0 / HD, LNX_EPS, ALU.mult, ALU.add))
                    assert link.k == YVAR, link.k
                    dve.wait_ge(s["pv_mm"], DONE(n))
                    dve.wait_ge(s["gbcT_mm"], DONE(n))
                    link(tt(stA[:, :].rearrange("p (k v) -> p k v", v=HD), G0[:, :].rearrange("p (k v) -> p k v", v=HD),
                            over(small[:, 24:32], 2, HD), ALU.mult))
                    dve.wait_ge(s["ga_out"], DONE(n))
                    tt(stA[:, :], stA[:, :], stB[:, :], ALU.mult).then_inc(s["yA_tm"], 1)
                    dve.wait_ge(s["y_root"], DONE(n))
                    link(rcp(small[:, 56:60], small[:, 56:60]))
                    tt(ytm[:, :, :], ytm[:, :, :], over(small[:, 56:60], 2, HD), ALU.mult).then_inc(s["yn_ready"], 1)
                    cp(kT[:, 0:P], kT[:, P:2 * P])
                    cp(Vt[:, 0, :], Vt[:, 1, :])
                    cp(mk[:, 0:P], mkprev[:, 1, :]).then_inc(s["window_moved"], 1)
                    dve.wait_ge(s["ynT_mm"], DONE(n))
                    yb = Ep
                    for h in range(2):
                        last = cp(yb[HD * h:HD * h + HD, :].rearrange("p (u t) -> p u t", t=CH),
                                  M3[0:HD, :].rearrange("p (u k) -> p u k", k=P)[:, :, CH * h:CH * h + CH])
                    link(last)
                    for p in range(PAIRS):
                        last = ts(yb[:, P * p:P * p + P], yb[:, P * p:P * p + P], par("lnw")[:, p:p + 1],
                                  par("lnb")[:, p:p + 1], ALU.mult, ALU.add)
                    link(last)
                    link(tt(yb[:, :], yb[:, :], bonv[:, :], ALU.add))
                    tt(yT[:, 4:6, :], yT[:, 4:6, :], yb[:, :].rearrange("p (c t) -> p c t", c=2), ALU.mult)\
                        .then_inc(s["yB_ready"], 1)
                    dve.wait_ge(s["o_squared"], DONE(n))
                    link(tt(small[:, 5:6], small[:, 3:4], small[:, 4:5], ALU.add))
                    link(ts(small[:, 5:6], small[:, 5:6], 1.0 / D, EPS, ALU.mult, ALU.add))
                    assert link.k == OVAR, link.k
                    dve.wait_ge(s["o_root"], DONE(n))
                    link(rcp(small[:, 60:61], small[:, 6:7]))
                    stt(ob[:, 0:512], G1[:, :], small[:, 60:61], gp[:, 0:512], ALU.mult, ALU.mult)
                    link(stt(ob[:, 512:1024], G0[:, :], small[:, 60:61], gp[:, 512:1024], ALU.mult, ALU.mult))
                    dve.wait_ge(L["xr_in"], (n + 1) * 16)
                    tt(ob, ob, xr, ALU.add).then_inc(s["o_ready"], 1)
                    link.end()
                dve.wait_ge(s["o_ready"], BEFORE((l + 1) * NT))

                dl.start(l)
                dve.wait_ge(smp["in_small"], (l + 1) * 64)

                def signal(ins, step):
                    ins.then_inc(smp["dve"], 1)
                    dve.wait_ge(smp["dve"], AT(step, l))

                signal(tt(dsq[:, :, :], xsT[:, :, :], xsT[:, :, :], ALU.mult), "sq")
                dve.wait_ge(smp["pe"], AT("ssq_mm", l))
                signal(ts(dr1[:, :], M0[:, 0:B], 1.0 / D, EPS, ALU.mult, ALU.add), "ms")
                dve.wait_ge(smp["act"], AT("root", l))
                dl(rcp(dr2[:, :], dr2[:, :]))
                dl(tt(dh[:, :, :], xsT[:, :, :], over(dr2[:, :], 1, KC), ALU.mult))
                dl(tt(dh[:, :, :], dh[:, :, :], gs[:, :, 1:1 + B], ALU.mult))
                signal(tt(dh[:, :, :], dh[:, :, :], mod[:, 0:8, 1:1 + B], ALU.add), "h")
                dve.wait_ge(smp["pe"], AT("proj_mm", l))
                dl(ms(pj[:, 6, :], 0.0))
                cp(pj[0:64, 6, :], M1[0:64, 6 * B:7 * B])
                cp(pj[:, 0:6, :], M1[:, 0:6 * B].rearrange("p (c b) -> p c b", b=B))
                signal(cp(pj[:, 7:23, :], M1[:, 7 * B:23 * B].rearrange("p (c b) -> p c b", b=B)), "proj")
                dl(tt(dx[:, :, :], dshift[:, :, :], pj[:, 0:7, :], ALU.subtract))
                dl(tt(dx[:, :, :], dx[:, :, :], over(par("mu"), 2, B), ALU.mult))
                signal(tt(dx[:, :, :], dx[:, :, :], pj[:, 0:7, :], ALU.add), "xs")
                cw, cb = par("cw"), par("cb")
                dl(tt(du[:, :, :], pj[:, 12:14, :], over(cw[:, 6:8], 2, B), ALU.mult))
                for k in range(3):
                    dl(tt(dv1[:, :, :], dconv[:, :, k, :], over(cw[:, 2 * k:2 * k + 2], 2, B), ALU.mult))
                    dl(tt(du[:, :, :], du[:, :, :], dv1[:, :, :], ALU.add))
                dl(tt(du[:, :, :], du[:, :, :], over(cb, 2, B), ALU.add))
                cp(dcnew[:, :, 0:2, :], dconv[:, :, 1:3, :])
                signal(cp(dcnew[:, :, 2, :], pj[:, 12:14, :]), "u")
                f2 = lambda v: v.rearrange("p c b -> p (c b)")
                dl(tt(dkr[:, :, :], dx[:, 2:4, :], over(par("kk"), 2, B), ALU.mult))
                signal(tt(dq1[:, :], f2(dkr[:, :, :]), f2(dkr[:, :, :]), ALU.mult), "kksq")
                dve.wait_ge(smp["act"], AT("w", l))
                dl(stt(dkm[:, :, :], da[:, :, :], -1.0, over(par("ka"), 2, B), ALU.add, ALU.mult))
                dl(stt(dkm[:, :, :], dkm[:, :, :], 1.0, dx[:, 2:4, :], ALU.add, ALU.mult))
                dl(tt(dv1[:, :, :], dx[:, 0:2, :], over(par("rk"), 2, B), ALU.mult))
                signal(tt(dq2[:, :], f2(dv1[:, :, :]), f2(dkm[:, :, :]), ALU.mult), "bonus_in")
                dve.wait_ge(smp["act"], AT("kknorm", l))
                dl(ts(dkk[:, :], dkk[:, :], 1e-12, None, ALU.max))
                dl(rcp(dkk[:, :], dkk[:, :]))
                dl(tt(dkk[:, :], dkk[:, :], f2(dkr[:, :, :]), ALU.mult))
                dl(tt(f2(da[:, :, :]), f2(da[:, :, :]), dkk[:, :], ALU.mult))
                S3, A3, C3 = (v.rearrange("p (u v) -> p u v", v=HD) for v in (dS, dT1, dT2))
                dve.wait_ge(smp["kv_in"], (l + 1) * 96)
                signal(tt(A3, S3, over(dkk[:, :], 2, HD), ALU.mult), "skk")
                signal(tt(C3, over(dcon("stack"), 1, 16), over(f2(dx[:, 4:6, :]), 2, HD), ALU.mult), "vdiag")
                dve.wait_ge(smp["pe"], AT("bonus_mm", l))
                signal(tt(dbv[:, :], M4[:, 0:16], f2(dx[:, 4:6, :]), ALU.mult), "bonus")
                dve.wait_ge(smp["pe"], AT("perm_mm", l))
                dl(ts(drq[:, :, :], pj[:, 7:12, :], dcon("cos"), None, ALU.mult))
                dl(stt(drq[:, :, :], M5[:, 0:5 * B].rearrange("p (c b) -> p c b", b=B), dcon("sin"), drq[:, :, :],
                       ALU.mult, ALU.add))
                cp(KTs[:, :, P:P + 1], drq[:, 0, :].unsqueeze(2))
                dl(ms(stB[:, :], 0.0))
                for g in range(KV):
                    for c in range(4):
                        last = cp(stB[HD * g:HD * g + HD, 4 * g + c:512:72], drq[HD * g:HD * g + HD, 1 + c, :])
                signal(last, "qrows")
                dl(tt(S3, S3, over(f2(dw[:, :, :]), 2, HD), ALU.mult))
                dve.wait_ge(smp["pe"], AT("sa_mm", l))
                ab, kb = f2(da[:, :, :]), f2(dkm[:, :, :])
                m3 = lambda m: m[:, :].rearrange("p (u v) -> p u v", v=HD)
                tt(A3[:, 0:8], m3(M2), over(ab[:, 0:8], 2, HD), ALU.mult)
                dl(tt(A3[:, 8:16], m3(M3), over(ab[:, 8:16], 2, HD), ALU.mult))
                dve.wait_ge(smp["pe"], AT("vb_mm", l))
                dl(tt(S3, S3, A3, ALU.subtract))
                tt(A3[:, 0:8], m3(M4), over(kb[:, 0:8], 2, HD), ALU.mult)
                dl(tt(A3[:, 8:16], m3(M5), over(kb[:, 8:16], 2, HD), ALU.mult))
                signal(tt(S3, S3, A3, ALU.add), "s_new")
                signal(tt(A3, S3, over(f2(dx[:, 0:2, :]), 2, HD), ALU.mult), "sr")
                dve.wait_ge(smp["pe"], AT("sr_mm", l))
                st = over(dcon("stack"), 1, 8)
                tt(C3[:, 0:8], m3(M2), st, ALU.mult)
                dl(tt(C3[:, 8:16], m3(M3), st, ALU.mult))
                signal(red(dyv[:, :], C3, AX_X, ALU.add), "y")
                dve.wait_ge(smp["pe"], AT("s_mm", l))
                dl(red(dm[0:64, 0:1], M4[0:64, 0:P + 1], AX_X, ALU.max))
                dl(stt(dm[0:64, 1:2], dm[0:64, 0:1], SCALE, par("dsink", 64), ALU.mult, ALU.max))
                ts(dm[0:64, 2:3], dm[0:64, 1:2], -1.0, None, ALU.mult)
                signal(tt(dm[0:64, 3:4], par("dsink", 64), dm[0:64, 1:2], ALU.subtract), "neg")
                dve.wait_ge(smp["pe"], AT("mean_mm", l))
                dl(stt(dyv[:, :], M0[:, 0:16], -1.0 / HD, dyv[:, :], ALU.mult, ALU.add))
                signal(tt(dq1[:, :], dyv[:, :], dyv[:, :], ALU.mult), "ysq")
                dve.wait_ge(smp["act"], AT("lru_exps", l))
                dl(tt(dv1[:, :, :], daa[:, :, :], daa[:, :, :], ALU.mult))
                signal(stt(dth[:, :, :], dv1[:, :, :], 1.0, dth[:, :, :], ALU.add, ALU.mult), "lru_t")
                dve.wait_ge(smp["pe"], AT("var_mm", l))
                signal(ts(dq1[:, :], M0[:, 16:32], 1.0 / HD, LNX_EPS, ALU.mult, ALU.add), "var")
                dve.wait_ge(smp["act"], AT("exp", l))
                dl(tt(dm[0:64, 4:5], dm[0:64, 4:5], dm[0:64, 5:6], ALU.add))
                dl(rcp(dm[0:64, 4:5], dm[0:64, 4:5]))
                dl(ts(Pd[0:64, :], Pd[0:64, :], dm[0:64, 4:5], None, ALU.mult))
                signal(ts(dg64[0:64, :], ident[0:64, 0:64], Pd[0:64, P:P + 1], None, ALU.mult), "pd")
                dve.wait_ge(smp["act"], AT("lru_root", l))
                dl(tt(dgi[:, :, :], dgi[:, :, :], du[:, :, :], ALU.mult))
                dl(tt(dgi[:, :, :], dgi[:, :, :], dth[:, :, :], ALU.mult))
                dl(tt(dh0[:, :, :], dh0[:, :, :], daa[:, :, :], ALU.mult))
                signal(tt(dh0[:, :, :], dh0[:, :, :], dgi[:, :, :], ALU.add), "h_new")
                dve.wait_ge(smp["act"], AT("silu", l))
                tt(ys[:, 6:8, :], dh0[:, :, :], dsg[:, 2:4, :], ALU.mult)
                dve.wait_ge(smp["act"], AT("yroot", l))
                dl(rcp(dq2[:, :], dq2[:, :]))
                dl(tt(dyv[:, :], dyv[:, :], dq2[:, :], ALU.mult))
                yv3 = dyv[:, :].rearrange("p (c b) -> p c b", b=B)
                dl(tt(yv3, yv3, over(par("lnw"), 2, B), ALU.mult))
                dl(tt(yv3, yv3, over(par("lnb"), 2, B), ALU.add))
                dl(tt(dyv[:, :], dyv[:, :], dbv[:, :], ALU.add))
                tt(ys[:, 4:6, :], yv3, dsg[:, 0:2, :], ALU.mult)
                dve.wait_ge(smp["pe"], AT("pt_mm", l))
                cp(PTd[:, :], M5[:, 0:64])
                cp(Pnd[0:8, :], M1[0:8, 0:64])
                signal(cp(Vnd[0:8, :], M1[0:8, 64:64 + P]), "pt")
                dve.wait_ge(smp["pe"], AT("pv_mm", l))
                for g in range(KV):
                    r = slice(HD * g, HD * g + HD)
                    last = tt(ys[r, 0:4, :], M2[r, 0:64].rearrange("p (b h) -> p h b", h=8)[:, 4 * g:4 * g + 4, :],
                              dsg[r, 4:8, :], ALU.mult)
                signal(last, "ys")
                dve.wait_ge(smp["pe"], AT("o_mm", l))
                dl(cp(dh[:, :, :], M3[:, 0:64].rearrange("p (c b) -> p c b", b=B)))
                signal(tt(dsq[:, :, :], dh[:, :, :], dh[:, :, :], ALU.mult), "osq")
                dve.wait_ge(smp["pe"], AT("ossq_mm", l))
                signal(ts(dr1[:, :], M4[:, 0:B], 1.0 / D, EPS, ALU.mult, ALU.add), "oms")
                dve.wait_ge(smp["act"], AT("oroot", l))
                dl(rcp(dr2[:, :], dr2[:, :]))
                dl(tt(dh[:, :, :], dh[:, :, :], over(dr2[:, :], 1, KC), ALU.mult))
                dl(tt(dh[:, :, :], dh[:, :, :], gpc[:, :, 1:1 + B], ALU.mult))
                dve.wait_ge(smp["stored"], (l + 1) * 96)
                dl.end()
                tt(xsT[:, :, :], xsT[:, :, :], dh[:, :, :], ALU.add).then_inc(L["layer_end"], 1)
                dve.wait_ge(L["layer_end"], l + 2)



def _lay_out(inp):
    f = np.float32
    g = {k: np.ascontiguousarray(np.asarray(v)) for k, v in inp.items()}

    def channels(x, n):
        return x.reshape(DEPTH, n, P).transpose(0, 2, 1)

    def heads(x, axis):
        sh = list(x.shape)
        x = x.reshape(sh[:axis] + [KV, 4, HD] + sh[axis + 1:])
        x = np.moveaxis(x, axis, axis + 1)
        return x.reshape(sh)

    w = g["w_in"]
    o = np.cumsum([0, 512, 128, 128, 512, 832, 256, 256, 256])
    q, ka, va, ga, pb, gb, xc, gc = (w[:, :, o[k]:o[k + 1]] for k in range(8))
    w = np.concatenate([pb, ka, heads(q, 2), xc, va, gb, gc, heads(ga, 2)], axis=2)
    a = {"w_in": w.reshape(DEPTH, KC, P, PIN).transpose(0, 2, 1, 3)}
    wo = g["w_out"]
    wo = np.concatenate([heads(wo[:, 0:512], 1), wo[:, 512:]], axis=1)
    a["w_out"] = wo.reshape(DEPTH, KC, P, D).transpose(0, 2, 1, 3)
    a["w_mod"] = g["w_mod"].reshape(DEPTH, KC, P, 24, P).transpose(0, 3, 2, 1, 4)
    mu = np.concatenate([g["rwkv_mu"], np.zeros((DEPTH, 64), f)], axis=1)
    sinks = g["attn_sinks"]
    slots = sinks.reshape(DEPTH, KV, 4).transpose(0, 2, 1).reshape(DEPTH, 1, HEADS)
    dsink = np.concatenate([np.tile(sinks, (1, B)), np.zeros((DEPTH, 64), f)], axis=1)[:, :, None]
    cw = g["lru_conv_w"].reshape(DEPTH, 4, 2, P).transpose(0, 3, 1, 2).reshape(DEPTH, P, 8)
    a["prm"] = np.concatenate([
        channels(g["norm_pre"], 8), channels(g["norm_post"], 8), channels(g["b_mod"], 24), channels(mu, 7),
        channels(g["rwkv_w0"], 2), channels(g["rwkv_a0"], 2), channels(g["rwkv_k_k"], 2), channels(g["rwkv_k_a"], 2),
        channels(g["rwkv_r_k"].reshape(DEPTH, 256), 2), channels(g["rwkv_lnx_w"], 2), channels(g["rwkv_lnx_b"], 2),
        cw, channels(g["lru_conv_b"], 2), channels(g["lru_gate_a_b"], 2), channels(g["lru_gate_x_b"], 2),
        channels(g["lru_lambda"], 2), np.broadcast_to(slots, (DEPTH, P, HEADS)), dsink], axis=2)
    lo = np.zeros((DEPTH, 2 * LORA, 512), f)
    lo[:, 0:LORA, 0:256] = g["rwkv_w_up"]
    lo[:, LORA:, 256:512] = g["rwkv_a_up"]
    a["lora"] = lo
    gw = np.zeros((DEPTH, P, 4, P), f)
    for k, name in ((0, "lru_gate_a_w"), (2, "lru_gate_x_w")):
        for n in range(4):
            r = slice(HD * (n % 2), HD * (n % 2) + HD)
            gw[:, r, k + n // 2, r] = g[name][:, n]
    a["gatew"] = gw
    a["cT"] = np.concatenate([g["c_prompt"], g["c_sample"]]).T.reshape(KC, P, 1 + B).transpose(1, 0, 2)
    a["x_prompt"] = g["x_prompt"].reshape(SEQ, D)
    a["x_s"] = g["x_sample"].reshape(B, D).T.reshape(KC, P, B).transpose(1, 0, 2)
    a["kc"] = g["cache_swa_k"].reshape(DEPTH, B, P, P).transpose(0, 3, 1, 2)
    a["vc"] = g["cache_swa_v"].reshape(DEPTH, B, P, P).transpose(0, 2, 1, 3)
    sh = np.concatenate([g["state_rwkv_shift"], np.zeros((DEPTH, B, 64), f)], axis=2)
    a["shift_s"] = sh.reshape(DEPTH, B, 7, P).transpose(0, 3, 2, 1)
    a["wkv_s"] = g["state_rwkv_wkv"].reshape(DEPTH, B, 2, 2, HD, HD).transpose(0, 3, 5, 2, 1, 4).reshape(DEPTH, P, 1024)
    a["conv_s"] = g["state_lru_conv"].reshape(DEPTH, B, 3, 2, P).transpose(0, 4, 3, 2, 1)
    a["h_s"] = g["state_lru_h"].reshape(DEPTH, B, 2, P).transpose(0, 3, 2, 1)
    i = np.arange(P)
    same = (i[:, None] // CH) == (i[None, :] // CH)
    ident = np.eye(P, dtype=f)
    reset = np.tile((np.arange(256) % CH != 0).astype(f), (P, 1))
    a["cst"] = np.concatenate([ident, same.astype(f), (same & (i[:, None] < i[None, :])).astype(f),
                               (same & (i[:, None] > i[None, :])).astype(f),
                               (same & (i[:, None] <= i[None, :])).astype(f), reset], axis=1)
    neg = np.full((P, P), NEG, f)
    a["masks"] = np.concatenate([neg, np.where(i[None, :] >= i[:, None], 0, neg),
                                 np.where(i[None, :] <= i[:, None], 0, neg)], axis=1).astype(f)
    inv = (10000.0 ** (-np.arange(HALF) / HALF)).astype(f)
    ang = (np.arange(SEQ + 1, dtype=f)[:, None] * inv[None, :]).astype(f)
    cos, sin = np.cos(ang).astype(f), np.sin(ang).astype(f)
    a["rope"] = np.concatenate([cos, sin], axis=1)[:SEQ].reshape(NT, P, 64)
    perm = ident[(i // HD) * HD + (i % HD + HALF) % HD]
    sign = np.where(i % HD < HALF, -1, 1).astype(f)
    rowb = np.zeros((P, B), f)
    rowb[np.arange(64), np.arange(64) // 8] = 1
    a["dcst"] = np.concatenate([perm, np.tile(np.eye(HD, dtype=f), (2, 1)), rowb, cos[PAST, i % HALF][:, None],
                                (sin[PAST, i % HALF] * sign)[:, None]], axis=1)
    return {k: np.ascontiguousarray(v, dtype=f) for k, v in a.items()}


_OUTS = {
    "y_prompt": (SEQ, D), "y_s": (P, KC, B), "k_p": (DEPTH, P, P), "v_p": (DEPTH, P, P), "shift_p": (DEPTH, P, 7),
    "wkv_p": (DEPTH, P, PAIRS, HD), "conv_p": (DEPTH, P, 2, 3), "h_p": (DEPTH, P, 2),
    "ko_s": (DEPTH, P, B), "vo_s": (DEPTH, P, B), "shifto_s": (DEPTH, P, 7, B), "wkvo_s": (DEPTH, P, 1024),
    "convo_s": (DEPTH, P, 2, 3, B), "ho_s": (DEPTH, P, 2, B)}


def kernel(**inputs):
    import concourse.bacc as bacc
    from concourse.bass_utils import run_bass_kernel_spmd

    nc = bacc.Bacc("TRN2", target_bir_lowering=False, num_devices=1)
    arrays = _lay_out(inputs)
    d = {k: nc.dram_tensor("in_" + k, v.shape, F32, kind="ExternalInput").ap() for k, v in arrays.items()}
    d.update({k: nc.dram_tensor("out_" + k, v, F32, kind="ExternalOutput").ap() for k, v in _OUTS.items()})
    d["x_mid"] = nc.dram_tensor("x_mid", (SEQ, D), F32, kind="Internal").ap()
    program(nc, d)
    res = run_bass_kernel_spmd(nc, [{"in_" + k: v for k, v in arrays.items()}], core_ids=[0]).results[0]
    r = {k: np.asarray(res["out_" + k]).reshape(v) for k, v in _OUTS.items()}
    c = np.ascontiguousarray
    return (
        r["y_prompt"].reshape(1, SEQ, D),
        c(r["y_s"].transpose(2, 1, 0)).reshape(B, 1, D),
        c(r["k_p"].transpose(0, 2, 1)).reshape(DEPTH, 1, P, KV, HD),
        r["v_p"].reshape(DEPTH, 1, P, KV, HD),
        c(r["shift_p"].transpose(0, 2, 1).reshape(DEPTH, 1, 896)[:, :, :SHIFT]),
        c(r["wkv_p"].reshape(DEPTH, 2, HD, 2, HD).transpose(0, 3, 1, 4, 2)).reshape(DEPTH, 1, 4, HD, HD),
        c(r["conv_p"].transpose(0, 3, 2, 1)).reshape(DEPTH, 1, 3, 256),
        c(r["h_p"].transpose(0, 2, 1)).reshape(DEPTH, 1, 256),
        c(r["ko_s"].transpose(0, 2, 1)).reshape(DEPTH, B, 1, KV, HD),
        c(r["vo_s"].transpose(0, 2, 1)).reshape(DEPTH, B, 1, KV, HD),
        c(r["shifto_s"].transpose(0, 3, 2, 1).reshape(DEPTH, B, 896)[:, :, :SHIFT]),
        c(r["wkvo_s"].reshape(DEPTH, 2, HD, 2, B, HD).transpose(0, 4, 3, 1, 5, 2)).reshape(DEPTH, B, 4, HD, HD),
        c(r["convo_s"].transpose(0, 4, 3, 2, 1)).reshape(DEPTH, B, 3, 256),
        c(r["ho_s"].transpose(0, 3, 2, 1)).reshape(DEPTH, B, 256),
    )
```

```python
from contextlib import ExitStack

import numpy as np

import concourse.bass as bass
from concourse import mybir

ALU = mybir.AluOpType
ACT = mybir.ActivationFunctionType
F32 = mybir.dt.float32
BF16 = mybir.dt.bfloat16
AX_X = mybir.AxisListType.X

P = 128
D = 1024
KC = D // P
SEQ = 2048
NT = SEQ // P
DEPTH = 2
B = 8
HD = 64
HALF = HD // 2
HEADS = 8
KV = 2
CH = 64
NCH = P // CH
PAIRS = 2
U = PAIRS * NCH
LORA = 32
SHIFT = 832
PAST = 2048
SCALE = HD ** -0.5
EPS = 1e-6
LNX_EPS = 64e-5
LRU_C = 8.0
DECAY = float(np.exp(-0.5))
NEG = -1e30
PIN = 2880

C_R, C_K, C_V, C_WA, C_KA, C_Q, C_XC, C_VA, C_GB, C_GC, C_GA = (
    0, 256, 512, 768, 832, 960, 1472, 1728, 1856, 2112, 2368)

PRM = {}
for _name, _n in (("npre", 8), ("npost", 8), ("bmod", 24), ("mu", 7), ("w0", 2), ("a0", 2), ("kk", 2),
                  ("ka", 2), ("rk", 2), ("lnw", 2), ("lnb", 2), ("cw", 8), ("cb", 2), ("gab", 2),
                  ("gxb", 2), ("lam", 2), ("sink", 8), ("dsink", 1)):
    PRM[_name] = (sum(n for _, n in PRM.values()), _n)
NPRM = sum(n for _, n in PRM.values())

CST = {}
for _name, _n in (("ident", 128), ("ones", 128), ("mst", 128), ("ms", 128), ("mit", 128), ("reset", 256)):
    CST[_name] = (sum(n for _, n in CST.values()), _n)
NCST = sum(n for _, n in CST.values())
DCST = {}
for _name, _n in (("perm", 128), ("stack", 64), ("rowb", 8), ("cos", 1), ("sin", 1)):
    DCST[_name] = (sum(n for _, n in DCST.values()), _n)
NDCST = sum(n for _, n in DCST.values())


def DONE(n):
    return n + 2


def BEFORE(n):
    return n + 1


def STEP(n, k, per):
    return n * per + (per + k)


class Link:

    def __init__(self, eng, sem, per):
        self.eng, self.sem, self.per, self.k, self.base = eng, sem, per, 0, 0

    def start(self, n):
        self.k, self.base = 0, n * self.per

    def __call__(self, ins):
        self.k += 1
        ins.then_inc(self.sem, 1)
        self.eng.wait_ge(self.sem, self.base + self.k)

    def end(self):
        assert self.k == self.per, (self.sem, self.k, self.per)


def over(ap, axis, count):
    v = ap.unsqueeze(axis)
    shape = list(v.shape)
    shape[axis] = count
    return v.to_broadcast(shape)


TILE_SEMS = """x_squared rms_root xn_ready xT_lo xT_hi hT_lo hT_hi
 rk_mm vwk_mm rk_out vwk_out rkT_mm vwT_mm pB_ready q_mm q_out xs_ready carried tw_ready lora_mm vbT_mm vst_ready
 sq_ready kksum_mm sgw_ready a_ready kknorm cum_ready exps_ready bonus_in bd_ready bonus_mm bonus_out
 g1T_mm g1_mm g2T_mm g3T_mm g4T_mm ntn_ready g_ready btT_mm bt_out
 xv_mm xv_out xcT_mm xcb_ready conv_ready lru_mm gates_ready lru_exps lru_t lru_root h_ready yC_ready
 gbc_mm gbc_out gbcT_mm gates_T ga_mm ga_out
 rope_ready qT_mm kT_mm qT_ready kT_ready qbd
 s0_mm s1_mm neg0 neg1 es0 es1 exp0 exp1 pT0_mm pT1_mm pT0_act pT0_dve pT1_act pT1_dve pv_mm yA_tm yAT_mm yA_ready window_moved
 u_out y_mm y_sq y_root yn_ready ynT_mm yB_ready ytm_ready
 s_mm o0_mm o1_mm o_squared o_root o_ready""".split()
TILE_STEPS = {"inv_mm": 5, "inv_act": 5, "inv_dve": 4, "q_mm5": 5, "q_dve": 4, "rh_ready": 2, "rh_mm": 2, "u_mm": 2,
              "u_act": 2, "s_ready": 2}


ACT_SEMS = """rms_root hT_lo x_squared rk_out vwk_out pB_ready q_out xv_out tw_ready sgw_ready a_ready xcb_ready kknorm
 exps_ready gbc_out inv_act bt_out gates_T gates_ready lru_exps qT_ready kT_ready lru_root ga_out es0 es1 exp0 exp1
 u_act pT0_act pT1_act y_sq y_root yA_ready o_squared o_root""".split()
PE_SEMS = [k for k in TILE_SEMS + list(TILE_STEPS) if k.endswith("_mm") or k in ("xT_lo", "xT_hi", "q_mm5")]
DVE_SEMS = [k for k in TILE_SEMS + list(TILE_STEPS) if k not in PE_SEMS and k not in ACT_SEMS]
PE_STEPS = """ssq_mm proj_mm perm_mm lora_mm kk_mm lru_mm bonus_mm sa_mm vb_mm sr_mm s_mm mean_mm var_mm pt_mm pv_mm o_mm
 ossq_mm""".split()
ACT_STEPS = """root silu tw sig w kknorm gates lru_exps lru_root exp yroot oroot""".split()
DVE_STEPS = """sq ms h proj xs u kksq bonus_in skk vdiag bonus qrows s_new sr y neg ysq lru_t var pd h_new pt ys osq oms""".split()
SAMPLE_SEMS = ("pe", "act", "dve", "x_s", "in_small", "kv_in", "stored")


def AT(step, l):
    steps = next(x for x in (PE_STEPS, ACT_STEPS, DVE_STEPS) if step in x)
    return l * len(steps) + steps.index(step) + 1


DCHUNKS = [(128 * j, 128) for j in range(6)] + [(C_WA, 64), (C_KA, 128)] + [(C_Q + 128 * j, 128) for j in range(4)] + \
    [(C_XC, 128), (C_XC + 128, 128), (C_VA, 128), (C_GB, 128), (C_GB + 128, 128), (C_GC, 128), (C_GC + 128, 128)] + \
    [(C_GA + 128 * j, 128) for j in range(4)]
DGROUPS = ((C_R, 512, (0, 1, 2, 3)), (C_V, 448, (4, 5, 6, 7)), (C_Q, 512, (8, 9, 10, 11)), (C_XC, 384, (12, 13, 14)),
           (C_GB, 512, (15, 16, 17, 18)), (C_GA, 512, (19, 20, 21, 22)))
MODG = 3 * D // 512
ROWS = MODG + len(DGROUPS) + 2
DVE_X = 5
DVE_T, DVE_L, DVE_D, YVAR, OVAR = 38, 13, 49, 29, 36


def program(nc, d):
    with ExitStack() as ctx:
        def sb(name, shape, dt=F32):
            return ctx.enter_context(nc.sbuf_tensor(name, shape, dt))

        def sem(name):
            return ctx.enter_context(nc.semaphore(name))

        Win = sb("w_in", [P, KC, PIN])
        Wout = sb("w_out", [P, KC, D])
        prm = sb("prm", [P, NPRM])
        cst = sb("cst", [P, NCST])
        lora = sb("lora", [2 * LORA, 4 * P])
        gatew = sb("gatew", [P, 4, P])
        mod = sb("mod", [P, 24, 1 + B])
        gs = sb("gs", [P, KC, 1 + B])
        gpc = sb("gpc", [P, KC, 1 + B])
        gp = sb("gp", [P, D])
        cT = sb("cT", [P, KC, 1 + B])
        spc = sb("spc", [P, 12, 2])
        identb = sb("identb", [P, P], BF16)
        mk = sb("mk", [P, 2 * P], BF16)
        mkprev = sb("mkprev", [P, 2, P], BF16)
        xa = sb("xa", [P, D])
        hT = sb("hT", [P, KC, P])
        stA = sb("stA", [P, 512])
        stB = sb("stB", [P, 512])
        qk = sb("qk", [P, 640])
        rope = sb("rope", [P, 64])
        pB = sb("pB", [P, 7, P + 1])
        xs = sb("xs", [P, 7, P])
        yT = sb("yT", [P, KC, P])
        kT = sb("kT", [P, 2 * P])
        Vt = sb("Vt", [P, 2, P])
        RA = sb("RA", [P, 2048])
        RB = sb("RB", [P, 1024])
        small = sb("small", [P, 64])
        tw = sb("tw", [2 * LORA, P])
        W1 = sb("W1", [P, 4, 256])
        W2 = sb("W2", [P, 4, 256])
        Ep = sb("Ep", [P, 256])
        kap = sb("kap", [P, U, P])
        bti = sb("bti", [P, U, P])
        kti = sb("kti", [P, U, P])
        rti = sb("rti", [P, U, P])
        Vst = sb("Vst", [P, U, HD])
        G = sb("G", [P, 3, 512])
        Q = sb("Q", [P, U, CH])
        RH = sb("RH", [P, PAIRS, HD])
        Ub = sb("Ub", [P, PAIRS, HD])
        S = sb("S", [P, 2, PAIRS, HD])
        bonv = sb("bonv", [P, 256])
        xcb = sb("xcb", [P, 2, P + 3])
        hcar = sb("hcar", [P, 2])
        flag = sb("flag", [P, 1])
        xsT = sb("xsT", [P, KC, B])

        sgw, cum, cx, Em = (W1[:, k, :] for k in range(4))
        Ex = cx
        Nbd = W1[:, 0:2, :].rearrange("p a (b c) -> p (a b) c", c=P)
        NTbd = W1[:, 2:4, :].rearrange("p a (b c) -> p (a b) c", c=P)
        Qbd = NTbd
        av, kkv, kmod, tmp = (W2[:, k, :] for k in range(4))
        btk = W2[:, 0:2, :].rearrange("p a (b c) -> p (a b) c", c=P)
        ktk = W2[:, 2:4, :].rearrange("p a (b c) -> p (a b) c", c=P)
        ytm = W2[:, 0, :].rearrange("p (u v) -> p u v", v=HD)
        qT = stA[:, :].rearrange("p (c t) -> p c t", c=4)
        G2T, G3T, G4T = (G[:, k, :].rearrange("p (u c) -> p u c", c=P) for k in range(3))
        xr = G[:, 0:2, :].rearrange("p a b -> p (a b)")
        xn = RA[:, 0:1024]
        ob = RA[:, 1024:2048]
        lu, lgr, lgi, lth, laa, la2, lh = (RA[:, 256 * k:256 * k + 256].rearrange("p (c t) -> p c t", c=2)
                                           for k in range(7))
        Pm = RA[:, :].rearrange("p (j s k) -> p j s k", j=2, k=256)
        PT = RB[:, :].rearrange("p (f s q) -> p f s q", f=2, q=P)
        rot = RB[:, 0:640]


        s = {k: sem("s_" + k) for k in TILE_SEMS + list(TILE_STEPS)}
        smp = {k: sem("d_" + k) for k in SAMPLE_SEMS}
        L = {k: sem("l_" + k) for k in (
            "const", "prm", "win", "wout", "wmod0", "wmod1", "wmod2", "mod_mm", "modT_mm", "row_mm", "row_out", "silu_c", "mod_out", "gpc", "gp_mm",
            "gp_out", "sp1", "sp2", "sp3", "cleared", "cast", "state", "x_in", "rope_in", "xr_in", "y_out",
            "dve_t", "dve_x", "act_t", "dve_l", "act_l", "zeros", "layer_end", "dve_d")}

        at = [0]

        def view(n, *shape):
            v = RA[:, at[0]:at[0] + n]
            at[0] += n
            if len(shape) == 2:
                v = v.rearrange("p (a b) -> p a b", b=shape[1])
            elif len(shape) == 3:
                v = v.rearrange("p (a b c) -> p a b c", b=shape[1], c=shape[2])
            return v

        KTs = view(B * (P + 1), B, P + 1)
        dcst = view(NDCST)
        dshift = view(7 * B, 7, B)
        dconv = view(6 * B, 2, 3, B)
        dcnew = view(6 * B, 2, 3, B)
        dh0 = view(2 * B, 2, B)
        pj = view(23 * B, 23, B)
        dx = view(7 * B, 7, B)
        du, dv1, dkr, dkm, da, dw, dgr, dgi, dth, daa = (view(2 * B, 2, B) for _ in range(10))
        dq1, dq2, dkk, dyv, dbv = (view(2 * B) for _ in range(5))
        Vc = RB[:, :].rearrange("p (b c) -> p b c", b=B)
        dS = W1[:, :, :].rearrange("p a b -> p (a b)")
        dT1 = W2[:, :, :].rearrange("p a b -> p (a b)")
        dT2 = xa[:, :]
        dsq = stA[:, 0:64].rearrange("p (c b) -> p c b", b=B)
        dh = stA[:, 64:128].rearrange("p (c b) -> p c b", b=B)
        dsg = stA[:, 128:192].rearrange("p (c b) -> p c b", b=B)
        drq = stA[:, 192:232].rearrange("p (c b) -> p c b", b=B)
        dtw = stA[:, 232:240]
        dr1, dr2, dm = stA[:, 240:248], stA[:, 248:256], stA[:, 256:264]
        Pd = stA[:, 264:393]
        dg64 = stA[:, 393:457]
        ys = yT[:, 0, 0:64].rearrange("p (c b) -> p c b", b=B)
        PTd = yT[:, 1, 0:64]
        Pnd = yT[:, 2, 0:64]
        Vnd = yT[:, 3, :]
        kkr = bonv[:, :]

        def dcon(name):
            o, n = DCST[name]
            return dcst[:, o:o + n]

        wmod = [v.rearrange("p (k c) -> p k c", c=P) for v in (RA[:, 0:1024], RA[:, 1024:2048], RB[:, :])]
        wmod_in = [L["wmod0"], L["wmod1"], L["wmod2"]]

        def par(name, rows=P):
            o, n = PRM[name]
            return prm[0:rows, o:o + n]

        def con(name):
            o, n = CST[name]
            return cst[:, o:o + n]

        ident = con("ident")
        ones = con("ones")
        rowbuf = [hT[:, 4 * b:4 * b + 4, :].rearrange("p k t -> p (k t)") for b in range(2)]

        PS = {k: ctx.enter_context(nc.psum_tensor(k, [P, 512], F32))
              for k in ("G0", "G1", "M0", "M1", "M2", "M3", "M4", "M5")}
        G0, G1, M0, M1, M2, M3, M4, M5 = PS["G0"], PS["G1"], PS["M0"], PS["M1"], PS["M2"], PS["M3"], PS["M4"], PS["M5"]
        block = ctx.enter_context(nc.Block())

        @block.sync
        def _(sp):
            sp.sem_inc(L["y_out"], 16)
            sp.sem_inc(L["state"], 16)
            sp.dma_start(cst[:, :], d["cst"]).then_inc(L["const"], 16)
            sp.dma_start(cT[:, :, :], d["cT"]).then_inc(L["const"], 16)
            sp.dma_start(RB[:, 0:384], d["masks"]).then_inc(L["const"], 16)
            sp.dma_start(xsT[:, :, :], d["x_s"]).then_inc(smp["x_s"], 16)
            for l in range(DEPTH):
                src = d["x_prompt"] if l == 0 else d["x_mid"]
                dst = d["y_prompt"] if l == DEPTH - 1 else d["x_mid"]

                def rows(x, i):
                    return x[bass.ds(i * P, P), :]

                def load(i, n):
                    sp.dma_start(xa[:, :], rows(src, i)).then_inc(L["x_in"], 16)
                    sp.wait_ge(s["rope_ready"], BEFORE(n))
                    sp.dma_start(rope[:, :], d["rope"][i]).then_inc(L["rope_in"], 16)

                def residual_and_store(i, n):
                    sp.wait_ge(s["y_mm"], DONE(n))
                    sp.dma_start(xr, rows(src, i)).then_inc(L["xr_in"], 16)
                    sp.wait_ge(s["o_ready"], DONE(n))
                    sp.dma_start(rows(dst, i), ob).then_inc(L["y_out"], 16)

                sp.wait_ge(L["layer_end"], l + 1)
                load(0, l * NT)
                if l == 0:
                    sp.wait_ge(L["mod_mm"], 21)
                    sp.dma_start(Win[:, :, :], d["w_in"][0]).then_inc(L["win"], 16)
                    sp.dma_start(Wout[:, :, :], d["w_out"][0]).then_inc(L["wout"], 16)
                with sp.Fori(0, NT - 1) as i:
                    n = l * NT + i
                    sp.wait_ge(s["xn_ready"], DONE(n))
                    load(i + 1, n + 1)
                    residual_and_store(i, n)
                residual_and_store(NT - 1, l * NT + NT - 1)
                for out, carry in ((d["k_p"], kT[:, 0:P]), (d["v_p"], Vt[:, 0, :]), (d["shift_p"], pB[:, :, 0]),
                                   (d["wkv_p"], S[:, 0, :, :]), (d["conv_p"], xcb[:, :, 0:3]), (d["h_p"], hcar[:, :])):
                    sp.dma_start(out[l], carry, allow_slow_non_contiguous=out is d["shift_p"]).then_inc(L["state"], 16)
                sp.wait_ge(L["y_out"], (l + 1) * NT * 16 + 16)
                for buf, x in ((dcst, d["dcst"]), (dshift, d["shift_s"][l]), (dconv, d["conv_s"][l]), (dh0, d["h_s"][l])):
                    sp.dma_start(buf, x).then_inc(smp["in_small"], 16)
                for k in range(4):
                    sp.dma_start(KTs[:, 2 * k:2 * k + 2, 0:P], d["kc"][l][:, 2 * k:2 * k + 2, :]).then_inc(smp["kv_in"], 16)
                sp.dma_start(Vc, d["vc"][l]).then_inc(smp["kv_in"], 16)
                sp.dma_start(dS, d["wkv_s"][l]).then_inc(smp["kv_in"], 16)
                sp.wait_ge(smp["dve"], AT("u", l))
                sp.wait_ge(smp["dve"], AT("qrows", l))
                sp.dma_start(d["ko_s"][l], drq[:, 0, :]).then_inc(smp["stored"], 16)
                sp.dma_start(d["vo_s"][l], pj[:, 14, :]).then_inc(smp["stored"], 16)
                sp.dma_start(d["shifto_s"][l], pj[:, 0:7, :]).then_inc(smp["stored"], 16)
                sp.dma_start(d["convo_s"][l], dcnew).then_inc(smp["stored"], 16)
                sp.wait_ge(smp["dve"], AT("s_new", l))
                sp.dma_start(d["wkvo_s"][l], dS).then_inc(smp["stored"], 16)
                sp.wait_ge(smp["dve"], AT("h_new", l))
                sp.dma_start(d["ho_s"][l], dh0).then_inc(smp["stored"], 16)
                if l < DEPTH - 1:
                    sp.wait_ge(smp["pe"], AT("proj_mm", l))
                    sp.dma_start(Win[:, :, :], d["w_in"][l + 1]).then_inc(L["win"], 16)
                    sp.wait_ge(smp["pe"], AT("o_mm", l))
                    sp.dma_start(Wout[:, :, :], d["w_out"][l + 1]).then_inc(L["wout"], 16)
            sp.wait_ge(L["layer_end"], DEPTH + 1)
            sp.dma_start(d["y_s"], xsT[:, :, :]).then_inc(smp["x_s"], 16)
            sp.wait_ge(smp["x_s"], 32)
            sp.wait_ge(L["state"], DEPTH * 96 + 16)
            sp.wait_ge(smp["stored"], DEPTH * 96)
            sp.wait_ge(L["y_out"], DEPTH * NT * 16 + 16)

        @block.tensor
        def _(pe):
            for name in PE_SEMS:
                pe.sem_inc(s[name], TILE_STEPS.get(name, 1))
            mm = nc.tensor.matmul

            def T(out, in_, rows=P):
                return nc.tensor.transpose(out, in_, ident[0:rows, 0:rows])

            def fill(out, col, width, ks):
                for k in ks:
                    last = mm(out[:, 0:width], hT[:, k, :], Win[:, k, col:col + width], start=k == 0, stop=k == KC - 1)
                return last

            with pe.Fori(0, DEPTH) as l:
                def to_channels(group, row, out, rows, chunks):
                    pe.wait_ge(L["row_out"], l * ROWS + (row + 1))
                    for start, width, column in chunks:
                        last = mm(out[0:width, column:column + rows], rowbuf[group % 2][0:rows, start:start + width],
                                  ident[0:rows, 0:rows], start=True, stop=True)
                    return last

                def mod_channels(g):
                    return to_channels(g, g, M0, 1 + B, [(P * j, P, 9 * (4 * g + j)) for j in range(4)])

                pe.wait_ge(L["silu_c"], 1)
                pe.wait_ge(L["const"], 48)
                pe.wait_ge(L["layer_end"], l + 1)
                for q in range(24):
                    pe.wait_ge(wmod_in[q % 3], (l * 8 + (q // 3 + 1)) * 16)
                    g, j = q // 4, q % 4
                    for k in range(KC):
                        last = mm((G0, G1)[g % 2][0:1 + B, P * j:P * j + P], cT[:, k, :], wmod[q % 3][:, k, :],
                                  start=k == 0, stop=k == KC - 1)
                    last.then_inc(L["mod_mm"], 1)
                    if j == 3 and g > 0:
                        mod_channels(g - 1)
                mod_channels(MODG - 1).then_inc(L["modT_mm"], 1)
                pe.wait_ge(L["gpc"], l + 1)
                for k in range(KC):
                    last = mm((M1 if k < 4 else M2)[:, P * (k % 4):P * (k % 4) + P],
                              gpc[:, k, 0:1].to_broadcast([P, P]), ident, start=True, stop=True)
                last.then_inc(L["gp_mm"], 1)
                pe.wait_ge(L["gp_out"], l + 1)
                pe.wait_ge(L["mod_out"], l + 1)

                def x_lo(m):
                    pe.wait_ge(s["xn_ready"], DONE(m))
                    pe.wait_ge(s["gbc_out"], BEFORE(m))
                    for k in range(4):
                        last = T(G0[:, P * k:P * k + P], xn[:, P * k:P * k + P])
                    last.then_inc(s["xT_lo"], 1)

                def x_hi(m):
                    pe.wait_ge(s["pT0_act"], BEFORE(m))
                    for k in range(4, 8):
                        last = T(M3[:, P * (k - 4):P * (k - 4) + P], xn[:, P * k:P * k + P])
                    last.then_inc(s["xT_hi"], 1)

                def fill_rk(m):
                    pe.wait_ge(s["hT_lo"], DONE(m))
                    pe.wait_ge(s["hT_hi"], DONE(m))
                    fill(G0, C_R, 512, range(KC)).then_inc(s["rk_mm"], 1)

                def fill_vwk(m):
                    pe.wait_ge(s["yA_tm"], BEFORE(m))
                    fill(G1, C_V, 448, range(KC)).then_inc(s["vwk_mm"], 1)

                def channels_rk(m):
                    pe.wait_ge(s["rk_out"], DONE(m))
                    pe.wait_ge(s["ytm_ready"], BEFORE(m))
                    for k in range(4):
                        last = T(M2[:, P * k:P * k + P], stA[:, P * k:P * k + P])
                    last.then_inc(s["rkT_mm"], 1)

                def channels_vw(m):
                    pe.wait_ge(s["vwk_out"], DONE(m))
                    pe.wait_ge(s["yB_ready"], BEFORE(m))
                    T(M3[:, 0:P], stB[:, 0:P])
                    T(M3[:, P:2 * P], stB[:, P:2 * P])
                    T(M3[0:64, 2 * P:3 * P], stB[:, 256:320]).then_inc(s["vwT_mm"], 1)

                def tile(n, ahead):
                    pe.wait_ge(s["xs_ready"], DONE(n))
                    pe.wait_ge(s["pT1_dve"], BEFORE(n))
                    T(M1[:, 0:P], xs[:, 4, :])
                    T(M1[:, P:2 * P], xs[:, 5, :]).then_inc(s["vbT_mm"], 1)
                    pe.wait_ge(s["tw_ready"], DONE(n))
                    pe.wait_ge(s["pT1_act"], BEFORE(n))
                    for k in range(4):
                        last = mm(M0[:, P * k:P * k + P], lora[:, P * k:P * k + P], tw[:, :], start=True, stop=True)
                    last.then_inc(s["lora_mm"], 1)
                    pe.wait_ge(s["sq_ready"], DONE(n))
                    pe.wait_ge(s["pB_ready"], DONE(n))
                    mm(M2[:, 0:256], ones, tmp, start=True, stop=True).then_inc(s["kksum_mm"], 1)
                    fill(G0, C_Q, 512, range(KC)).then_inc(s["q_mm"], 1)
                    fill(G1, C_XC, 384, range(KC)).then_inc(s["xv_mm"], 1)
                    pe.wait_ge(s["q_out"], DONE(n))
                    fill(G0, C_GB, 512, range(KC)).then_inc(s["gbc_mm"], 1)
                    pe.wait_ge(s["xv_out"], DONE(n))
                    pe.wait_ge(s["o_ready"], BEFORE(n))
                    T(M4[:, 0:P], stA[:, 0:P])
                    T(M4[:, P:2 * P], stA[:, P:2 * P]).then_inc(s["xcT_mm"], 1)
                    pe.wait_ge(s["bonus_in"], DONE(n))
                    pe.wait_ge(s["kknorm"], DONE(n))
                    mm(M2[:, 256:512], ones, bonv[:, :], start=True, stop=True).then_inc(s["bonus_mm"], 1)
                    pe.wait_ge(s["bd_ready"], DONE(n))
                    pe.wait_ge(s["a_ready"], DONE(n))
                    pe.wait_ge(s["vst_ready"], DONE(n))
                    pe.wait_ge(s["s_ready"], STEP(n, 0, 2))

                    def gram(out, a, b):
                        for u in range(U):
                            last = mm(out[:, P * u:P * u + P], a[:, u, :], b[:, u, :], start=True, stop=True)
                        return last

                    gram(M0, bti, kap).then_inc(s["g1T_mm"], 1)
                    gram(M1, kap, bti).then_inc(s["g1_mm"], 1)
                    gram(M3, kti, kap).then_inc(s["g2T_mm"], 1)
                    pe.wait_ge(s["xcb_ready"], DONE(n))
                    gram(M4, bti, rti).then_inc(s["g3T_mm"], 1)
                    gram(M5, kti, rti).then_inc(s["g4T_mm"], 1)
                    pe.wait_ge(s["ntn_ready"], DONE(n))

                    def squares(level):
                        for u in range(U):
                            last = mm(M0[:, P * u:P * u + P], NTbd[:, u, :], Nbd[:, u, :], start=True, stop=True)
                        if level < 5:
                            for u in range(U):
                                last = mm(M1[:, P * u:P * u + P], Nbd[:, u, :], NTbd[:, u, :], start=True, stop=True)
                        last.then_inc(s["inv_mm"], 1)

                    def multiply(level):
                        pe.wait_ge(s["inv_act"], STEP(n, level, 5))
                        if level > 1:
                            pe.wait_ge(s["q_dve"], STEP(n, level - 1, 4))
                        for u in range(U):
                            last = mm(M2[:, CH * u:CH * u + CH], Nbd[:, u, :], Q[:, u, :], start=True, stop=True)
                        last.then_inc(s["q_mm5"], 1)

                    squares(1)
                    pe.wait_ge(s["g_ready"], DONE(n))
                    for u in range(U):
                        T(M3[:, P * u:P * u + P], bti[:, u, :])
                    for u in range(U):
                        last = T(M4[:, P * u:P * u + P], kti[:, u, :])
                    last.then_inc(s["btT_mm"], 1)
                    fill(G1, C_GA, 512, range(0, 2))
                    pe.wait_ge(s["bonus_out"], DONE(n))
                    multiply(1)
                    pe.wait_ge(s["inv_dve"], STEP(n, 1, 4))
                    squares(2)
                    pe.wait_ge(s["conv_ready"], DONE(n))
                    pe.wait_ge(s["bt_out"], DONE(n))
                    for k in range(4):
                        last = mm(M3[:, P * k:P * k + P], gatew[:, k, :], lu[:, k % 2, :], start=True, stop=True)
                    last.then_inc(s["lru_mm"], 1)
                    pe.wait_ge(s["gbc_out"], DONE(n))
                    for k in range(4):
                        last = T(M4[:, P * k:P * k + P], stA[:, P * k:P * k + P])
                    last.then_inc(s["gbcT_mm"], 1)
                    fill(G1, C_GA, 512, range(2, 4))
                    multiply(2)
                    pe.wait_ge(s["inv_dve"], STEP(n, 2, 4))
                    squares(3)
                    fill(G1, C_GA, 512, range(4, 6))
                    pe.wait_ge(s["rope_ready"], DONE(n))
                    pe.wait_ge(s["gates_ready"], DONE(n))
                    for k in range(4):
                        last = T(M3[:, P * k:P * k + P], qk[:, P * k:P * k + P])
                    last.then_inc(s["qT_mm"], 1)
                    pe.wait_ge(s["gates_T"], DONE(n))
                    T(M4[:, 0:P], qk[:, 512:640]).then_inc(s["kT_mm"], 1)
                    multiply(3)
                    pe.wait_ge(s["inv_dve"], STEP(n, 3, 4))
                    squares(4)
                    fill(G1, C_GA, 512, range(6, 8)).then_inc(s["ga_mm"], 1)

                    def scores(j, ma, mb):
                        for g, m in ((0, ma), (1, mb)):
                            mm(m[:, :].rearrange("p (c k) -> p c k", c=2), identb[:, :], over(mk[:, :], 1, 2),
                               start=True, stop=False, skip_group_check=True)
                            for c in range(2):
                                last = mm(m[:, 256 * c:256 * c + 256], qT[HD * g:HD * g + HD, 2 * j + c, :],
                                          kT[HD * g:HD * g + HD, :], start=False, stop=True, skip_group_check=True)
                        return last

                    multiply(4)
                    pe.wait_ge(s["inv_dve"], STEP(n, 4, 4))
                    squares(5)
                    pe.wait_ge(s["qT_ready"], DONE(n))
                    pe.wait_ge(s["kT_ready"], DONE(n))
                    scores(0, M3, M4).then_inc(s["s0_mm"], 1)
                    multiply(5)

                    def probs(j, ma, mb):
                        for f, m in ((0, ma), (1, mb)):
                            for k in range(4):
                                last = T(m[:, P * k:P * k + P], Pm[:, j, k, P * f:P * f + P])
                        return last

                    def values(j):
                        for k in range(4):
                            g = k % 2
                            for f in range(2):
                                last = mm(G1[:, HD * (4 * j + k):HD * (4 * j + k) + HD], PT[:, f, k, :],
                                          Vt[:, f, HD * g:HD * g + HD], start=f == 0, stop=f == 1)
                        return last

                    def right_side(m):
                        prev = S[:, m % 2]
                        for p in range(PAIRS):
                            u = NCH * p + m
                            mm(M5[:, HD * p:HD * p + HD], kap[:, u, :], prev[:, p, :], start=True, stop=False)
                            last = mm(M5[:, HD * p:HD * p + HD], G2T[:, u, :], Vst[:, u, :], start=False, stop=True)
                        last.then_inc(s["rh_mm"], 1)

                    def solve(m):
                        pe.wait_ge(s["rh_ready"], STEP(n, m + 1, 2))
                        for p in range(PAIRS):
                            u = NCH * p + m
                            last = mm(M5[:, P + HD * p:P + HD * p + HD], Qbd[:, u, :], RH[:, p, :], start=True, stop=True)
                        last.then_inc(s["u_mm"], 1)

                    def next_state(m):
                        prev = S[:, m % 2]
                        pe.wait_ge(s["u_act"], STEP(n, m + 1, 2))
                        for p in range(PAIRS):
                            u = NCH * p + m
                            o = M5[:, 256 + HD * p:256 + HD * p + HD]
                            mm(o, ident, prev[:, p, :], start=True, stop=False)
                            mm(o, btk[:, u, :], Ub[:, p, :], start=False, stop=False)
                            last = mm(o, ktk[:, u, :], Vst[:, u, :], start=False, stop=True)
                        return last

                    def outputs(m):
                        prev = S[:, m % 2]
                        for p in range(PAIRS):
                            u = NCH * p + m
                            o = M2[:, HD * u:HD * u + HD]
                            mm(o, rti[:, u, :], prev[:, p, :], start=True, stop=False)
                            mm(o, G3T[:, u, :], Ub[:, p, :], start=False, stop=False)
                            last = mm(o, G4T[:, u, :], Vst[:, u, :], start=False, stop=True)
                        return last

                    pe.wait_ge(L["zeros"], l + 1)
                    right_side(0)
                    scores(1, M0, M1).then_inc(s["s1_mm"], 1)
                    pe.wait_ge(s["qbd"], DONE(n))
                    solve(0)
                    pe.wait_ge(s["exp0"], DONE(n))
                    probs(0, M3, M4).then_inc(s["pT0_mm"], 1)
                    next_state(0).then_inc(s["s_mm"], 1)
                    outputs(0)
                    if ahead:
                        x_lo(n + 1)
                    pe.wait_ge(s["s_ready"], STEP(n, 1, 2))
                    right_side(1)
                    pe.wait_ge(s["pT0_act"], DONE(n))
                    pe.wait_ge(s["pT0_dve"], DONE(n))
                    pe.wait_ge(s["ga_out"], DONE(n))
                    values(0)
                    solve(1)
                    pe.wait_ge(s["exp1"], DONE(n))
                    probs(1, M0, M1).then_inc(s["pT1_mm"], 1)
                    if ahead:
                        x_hi(n + 1)
                    next_state(1)
                    outputs(1).then_inc(s["y_mm"], 1)
                    pe.wait_ge(s["pT1_act"], DONE(n))
                    pe.wait_ge(s["pT1_dve"], DONE(n))
                    values(1).then_inc(s["pv_mm"], 1)
                    if ahead:
                        fill_rk(n + 1)
                    pe.wait_ge(s["yA_tm"], DONE(n))
                    pe.wait_ge(s["yn_ready"], DONE(n))
                    for k in range(4):
                        last = T(M4[:, P * k:P * k + P], stA[:, P * k:P * k + P])
                    last.then_inc(s["yAT_mm"], 1)
                    for u in range(U):
                        last = T(M3[0:HD, P * u:P * u + P], ytm[:, u, :])
                    last.then_inc(s["ynT_mm"], 1)
                    if ahead:
                        fill_vwk(n + 1)
                        channels_rk(n + 1)
                    pe.wait_ge(s["yC_ready"], DONE(n))
                    pe.wait_ge(s["s_ready"], STEP(n, 2, 2))
                    pe.wait_ge(s["yA_ready"], DONE(n))
                    pe.wait_ge(s["yB_ready"], DONE(n))

                    def project(h, o):
                        for k in range(KC):
                            last = mm(o[:, :], yT[:, k, :], Wout[:, k, 512 * h:512 * h + 512], start=k == 0,
                                      stop=k == KC - 1)
                        return last

                    project(0, M5).then_inc(s["o0_mm"], 1)
                    if ahead:
                        channels_vw(n + 1)
                    project(1, M4).then_inc(s["o1_mm"], 1)

                x_lo(l * NT)
                x_hi(l * NT)
                pe.wait_ge(L["win"], (l + 1) * 16)
                fill_rk(l * NT)
                fill_vwk(l * NT)
                channels_rk(l * NT)
                pe.wait_ge(L["wout"], (l + 1) * 16)
                channels_vw(l * NT)
                with pe.Fori(0, NT - 1) as i:
                    tile(l * NT + i, True)
                tile(l * NT + NT - 1, False)

                one = con("reset")[:, 1:2].to_broadcast([P, P])
                pe.wait_ge(s["o1_mm"], BEFORE((l + 1) * NT))
                pe.wait_ge(smp["dve"], AT("sq", l))
                for k in range(KC):
                    last = mm(M0[:, 0:B], one, dsq[:, k, :], start=k == 0, stop=k == KC - 1)
                last.then_inc(smp["pe"], 1)
                pe.wait_ge(smp["dve"], AT("h", l))

                def proj_channels(g):
                    first, _, chunks = DGROUPS[g]
                    return to_channels(g, MODG + g, M1, B, [(DCHUNKS[j][0] - first, DCHUNKS[j][1], B * j) for j in chunks])

                for g, (col, width, _) in enumerate(DGROUPS):
                    for k in range(KC):
                        last = mm((G0, G1)[g % 2][0:B, 0:width], dh[:, k, :], Win[:, k, col:col + width],
                                  start=k == 0, stop=k == KC - 1)
                    last.then_inc(L["row_mm"], 1)
                    if g > 0:
                        proj_channels(g - 1)
                proj_channels(len(DGROUPS) - 1).then_inc(smp["pe"], 1)
                pe.wait_ge(smp["dve"], AT("proj", l))
                mm(M5[:, 0:5 * B], dcon("perm"), pj[:, 7:12, :], start=True, stop=True).then_inc(smp["pe"], 1)
                pe.wait_ge(smp["act"], AT("tw", l))
                for k in range(4):
                    last = mm(M0[:, B * k:B * k + B], lora[:, P * k:P * k + P], dtw[0:64, :], start=True, stop=True)
                last.then_inc(smp["pe"], 1)
                pe.wait_ge(smp["dve"], AT("kksq", l))
                mm(M2[:, 0:16], ones, dq1[:, :], start=True, stop=True).then_inc(smp["pe"], 1)
                pe.wait_ge(smp["dve"], AT("u", l))
                for k in range(4):
                    last = mm(M3[:, B * k:B * k + B], gatew[:, k, :], du[:, k % 2, :], start=True, stop=True)
                last.then_inc(smp["pe"], 1)
                pe.wait_ge(smp["dve"], AT("bonus_in", l))
                mm(M4[:, 0:16], ones, dq2[:, :], start=True, stop=True).then_inc(smp["pe"], 1)
                pe.wait_ge(smp["dve"], AT("skk", l))
                pe.wait_ge(smp["act"], AT("gates", l))
                pe.wait_ge(smp["act"], AT("kknorm", l))
                mm(M2[:, :], ones, dT1[:, 0:512], start=True, stop=True)
                mm(M3[:, :], ones, dT1[:, 512:1024], start=True, stop=True).then_inc(smp["pe"], 1)
                pe.wait_ge(smp["dve"], AT("vdiag", l))
                pe.wait_ge(smp["dve"], AT("qrows", l))
                mm(M4[:, :], ones, dT2[:, 0:512], start=True, stop=True)
                mm(M5[:, :], ones, dT2[:, 512:1024], start=True, stop=True).then_inc(smp["pe"], 1)
                pe.wait_ge(smp["dve"], AT("sr", l))
                mm(M2[:, :], ones, dT1[:, 0:512], start=True, stop=True)
                mm(M3[:, :], ones, dT1[:, 512:1024], start=True, stop=True).then_inc(smp["pe"], 1)
                pe.wait_ge(smp["dve"], AT("qrows", l))
                pe.wait_ge(smp["kv_in"], (l + 1) * 96)
                for b in range(B):
                    last = mm(M4[0:64, 0:P + 1], stB[:, 64 * b:64 * b + 64], KTs[:, b, :], start=b == 0, stop=b == B - 1)
                last.then_inc(smp["pe"], 1)
                pe.wait_ge(smp["dve"], AT("y", l))
                mm(M0[:, 0:16], ones, dyv[:, :], start=True, stop=True).then_inc(smp["pe"], 1)
                pe.wait_ge(smp["dve"], AT("ysq", l))
                mm(M0[:, 16:32], ones, dq1[:, :], start=True, stop=True).then_inc(smp["pe"], 1)
                pe.wait_ge(smp["dve"], AT("pd", l))
                T(M1[0:8, 64:64 + P], pj[:, 14, :])
                mm(M1[0:8, 0:64], dcon("rowb")[0:64, :], dg64[0:64, :], start=True, stop=True)
                T(M5[:, 0:64], Pd[0:64, 0:P], 64).then_inc(smp["pe"], 1)
                pe.wait_ge(smp["dve"], AT("pt", l))
                mm(M2[:, 0:64], Vnd[0:8, :], Pnd[0:8, :], start=True, stop=False, skip_group_check=True)
                for b in range(B):
                    last = mm(M2[:, 8 * b:8 * b + 8], Vc[:, b, :], PTd[:, 8 * b:8 * b + 8], start=False, stop=True,
                              skip_group_check=True)
                last.then_inc(smp["pe"], 1)
                pe.wait_ge(smp["dve"], AT("ys", l))
                for h in range(2):
                    for k in range(KC):
                        last = mm((G0, G1)[h][0:B, :], ys[:, k, :], Wout[:, k, 512 * h:512 * h + 512], start=k == 0,
                                  stop=k == KC - 1)
                    last.then_inc(L["row_mm"], 1)
                for h in range(2):
                    last = to_channels(h, MODG + len(DGROUPS) + h, M3, B, [(P * j, P, B * (4 * h + j)) for j in range(4)])
                last.then_inc(smp["pe"], 1)
                pe.wait_ge(smp["dve"], AT("osq", l))
                for k in range(KC):
                    last = mm(M4[:, 0:B], one, dsq[:, k, :], start=k == 0, stop=k == KC - 1)
                last.then_inc(smp["pe"], 1)

        @block.scalar
        def _(act):
            for name in ACT_SEMS:
                act.sem_inc(s[name], TILE_STEPS.get(name, 1))
            A = nc.scalar.activation
            link = Link(act, L["act_t"], 1)
            act.wait_ge(L["const"], 48)
            A(cT[:, :, :], cT[:, :, :], ACT.Silu).then_inc(L["silu_c"], 1)
            A(identb[:, :], ident, ACT.Copy).then_inc(L["cast"], 1)
            A(mkprev[:, :, :], RB[:, 0:256].rearrange("p (a b) -> p a b", a=2), ACT.Copy).then_inc(L["cast"], 1)
            A(mk[:, P:2 * P], RB[:, 256:384], ACT.Copy).then_inc(L["cast"], 1)
            with act.Fori(0, DEPTH) as l:
                act.wait_ge(s["o1_mm"], BEFORE(l * NT))
                act.wait_ge(L["layer_end"], l + 1)
                act.dma_start(prm[:, :], d["prm"][l]).then_inc(L["prm"], 16)
                act.dma_start(lora[:, :], d["lora"][l]).then_inc(L["prm"], 16)
                act.dma_start(gatew[:, :, :], d["gatew"][l]).then_inc(L["prm"], 16)
                act.wait_ge(L["cast"], 3)
                act.wait_ge(L["y_out"], l * NT * 16 + 16)
                for q in range(24):
                    if q >= 3:
                        act.wait_ge(L["mod_mm"], l * 24 + (q - 2))
                    act.dma_start(wmod[q % 3], d["w_mod"][l, q]).then_inc(wmod_in[q % 3], 16)
                act.wait_ge(L["sp1"], l + 1)
                A(spc[:, 1, :], spc[:, 0, :], ACT.Exp, scale=-1.0).then_inc(L["sp2"], 1)
                act.wait_ge(L["sp1"], l + 1)
                act.wait_ge(L["sp3"], 2 * l + 1)
                A(spc[:, 5, :], spc[:, 2, :], ACT.Ln).then_inc(L["sp2"], 1)
                act.wait_ge(L["mod_mm"], (l + 1) * 24)
                act.wait_ge(L["mod_out"], l + 1)
                act.wait_ge(L["zeros"], l + 1)

                def x_square(m):
                    act.wait_ge(L["x_in"], (m + 1) * 16)
                    act.wait_ge(s["rope_ready"], BEFORE(m))
                    A(RB[:, :], xa[:, :], ACT.Square, accum_out=small[:, 0:1]).then_inc(s["x_squared"], 1)

                def x_root(m):
                    act.wait_ge(L["dve_x"], m * DVE_X + 1)
                    A(small[:, 2:3], small[:, 1:2], ACT.Sqrt).then_inc(s["rms_root"], 1)

                def h_lo(m):
                    act.wait_ge(s["xT_lo"], DONE(m))
                    for k in range(4):
                        last = A(hT[:, k, :], G0[:, P * k:P * k + P], ACT.Identity, bias=mod[:, k, 0:1],
                                 scale=gs[:, k, 0:1])
                    last.then_inc(s["hT_lo"], 1)

                def copy_rk(m):
                    act.wait_ge(s["rk_mm"], DONE(m))
                    act.wait_ge(s["yAT_mm"], BEFORE(m))
                    A(stA[:, :], G0[:, :], ACT.Copy).then_inc(s["rk_out"], 1)

                def copy_vwk(m):
                    act.wait_ge(s["vwk_mm"], DONE(m))
                    act.wait_ge(s["yA_tm"], BEFORE(m))
                    A(stB[:, 0:320], G1[:, 0:320], ACT.Copy)
                    A(qk[:, 512:640], G1[:, 320:448], ACT.Copy).then_inc(s["vwk_out"], 1)

                def channels_rk(m):
                    act.wait_ge(s["rkT_mm"], DONE(m))
                    act.wait_ge(s["carried"], BEFORE(m))
                    A(pB[:, 0:4, 1:P + 1], M2[:, :].rearrange("p (c t) -> p c t", c=4), ACT.Copy)

                def channels_vw(m):
                    act.wait_ge(s["vwT_mm"], DONE(m))
                    A(pB[:, 4:6, 1:P + 1], M3[:, 0:256].rearrange("p (c t) -> p c t", c=2), ACT.Copy)
                    A(pB[0:64, 6, 1:P + 1], M3[0:64, 256:384], ACT.Copy).then_inc(s["pB_ready"], 1)

                def low_rank(m):
                    act.wait_ge(s["xs_ready"], DONE(m))
                    A(tw[0:32, :], xs[0:32, 6, :], ACT.Tanh)
                    A(tw[32:64, :], xs[32:64, 6, :], ACT.Copy).then_inc(s["tw_ready"], 1)

                def tile(n, ahead):
                    act.wait_ge(s["lora_mm"], DONE(n))
                    act.wait_ge(s["y_mm"], BEFORE(n))
                    for p in range(PAIRS):
                        last = A(sgw[:, P * p:P * p + P], M0[:, P * p:P * p + P], ACT.Sigmoid, bias=par("w0")[:, p:p + 1])
                    last.then_inc(s["sgw_ready"], 1)
                    for p in range(PAIRS):
                        last = A(av[:, P * p:P * p + P], M0[:, 256 + P * p:256 + P * p + P], ACT.Sigmoid,
                                 bias=par("a0")[:, p:p + 1])
                    last.then_inc(s["a_ready"], 1)
                    act.wait_ge(s["kksum_mm"], DONE(n))
                    A(kkv, M2[:, 0:256], ACT.Sqrt).then_inc(s["kknorm"], 1)
                    act.wait_ge(s["cum_ready"], DONE(n))
                    A(Em, cum, ACT.Exp, scale=DECAY)
                    A(Ep[:, :], cum, ACT.Exp, scale=-DECAY)
                    A(Ex, cx, ACT.Exp, scale=-DECAY).then_inc(s["exps_ready"], 1)
                    act.wait_ge(s["q_mm"], DONE(n))
                    A(qk[:, 0:512], G0[:, :], ACT.Copy).then_inc(s["q_out"], 1)
                    act.wait_ge(s["xv_mm"], DONE(n))
                    act.wait_ge(s["window_moved"], BEFORE(n))
                    A(stA[:, 0:256], G1[:, 0:256], ACT.Copy)
                    A(Vt[:, 1, :], G1[:, 256:384], ACT.Copy).then_inc(s["xv_out"], 1)
                    act.wait_ge(s["xcT_mm"], DONE(n))
                    act.wait_ge(s["conv_ready"], BEFORE(n))
                    A(xcb[:, :, 3:P + 3], M4[:, 0:256].rearrange("p (c t) -> p c t", c=2), ACT.Copy)\
                        .then_inc(s["xcb_ready"], 1)
                    act.wait_ge(s["gbc_mm"], DONE(n))
                    A(stA[:, :], G0[:, :], ACT.Silu).then_inc(s["gbc_out"], 1)
                    def power(level):
                        act.wait_ge(s["inv_mm"], STEP(n, level, 5))
                        if level > 1:
                            act.wait_ge(s["q_mm5"], STEP(n, level - 1, 5))
                        A(Nbd, M0[:, :].rearrange("p (u c) -> p u c", c=P), ACT.Copy).then_inc(s["inv_act"], 1)
                    power(1)
                    act.wait_ge(s["btT_mm"], DONE(n))
                    A(btk, M3[:, :].rearrange("p (u c) -> p u c", c=P), ACT.Copy)
                    A(ktk, M4[:, :].rearrange("p (u c) -> p u c", c=P), ACT.Copy).then_inc(s["bt_out"], 1)
                    power(2)
                    act.wait_ge(s["gbcT_mm"], DONE(n))
                    act.wait_ge(s["o1_mm"], BEFORE(n))
                    A(yT[:, 4:8, :], M4[:, :].rearrange("p (c t) -> p c t", c=4), ACT.Copy).then_inc(s["gates_T"], 1)
                    act.wait_ge(s["lru_mm"], DONE(n))
                    for c in range(2):
                        A(lgr[:, c, :], M3[:, P * c:P * c + P], ACT.Sigmoid, bias=par("gab")[:, c:c + 1])
                        last = A(lgi[:, c, :], M3[:, 256 + P * c:256 + P * c + P], ACT.Sigmoid, bias=par("gxb")[:, c:c + 1])
                    last.then_inc(s["gates_ready"], 1)
                    act.wait_ge(s["gates_ready"], DONE(n))
                    act.wait_ge(L["y_out"], n * 16 + 16)
                    power(3)
                    for c in range(2):
                        A(lth[:, c, :], lgr[:, c, :], ACT.Tanh, scale=spc[:, 9, c:c + 1])
                        last = A(laa[:, c, :], lgr[:, c, :], ACT.Exp, scale=spc[:, 9, c:c + 1])
                    link.start(n)
                    link(last)
                    link.end()
                    A(la2, laa, ACT.Square).then_inc(s["lru_exps"], 1)
                    act.wait_ge(s["qT_mm"], DONE(n))
                    A(qT[:, :, :], M3[:, :].rearrange("p (c t) -> p c t", c=4), ACT.Copy).then_inc(s["qT_ready"], 1)
                    act.wait_ge(s["kT_mm"], DONE(n))
                    A(kT[:, P:2 * P], M4[:, 0:P], ACT.Copy).then_inc(s["kT_ready"], 1)
                    power(4)
                    if ahead:
                        x_square(n + 1)
                    act.wait_ge(s["lru_t"], DONE(n))
                    A(lth, lth, ACT.Sqrt, scale=-1.0).then_inc(s["lru_root"], 1)
                    if ahead:
                        x_root(n + 1)
                    power(5)
                    act.wait_ge(s["ga_mm"], DONE(n))
                    A(stB[:, :], G1[:, :], ACT.Silu).then_inc(s["ga_out"], 1)

                    def exps(j, ma, mb, neg, es, done):
                        act.wait_ge(neg, DONE(n))
                        if j == 0:
                            act.wait_ge(s["yC_ready"], DONE(n))
                        A(small[:, 40 + 4 * j:44 + 4 * j], small[:, 32 + 4 * j:36 + 4 * j], ACT.Exp).then_inc(es, 1)
                        for k in range(4):
                            m = mb if k % 2 else ma
                            last = A(Pm[:, j, k, :], m[:, 256 * (k // 2):256 * (k // 2) + 256], ACT.Exp,
                                     bias=small[:, 16 + 4 * j + k:17 + 4 * j + k], scale=SCALE,
                                     accum_out=small[:, 24 + 4 * j + k:25 + 4 * j + k])
                        last.then_inc(done, 1)

                    exps(0, M3, M4, s["neg0"], s["es0"], s["exp0"])
                    act.wait_ge(s["u_mm"], STEP(n, 1, 2))
                    A(Ub[:, :, :], M5[:, P:2 * P].rearrange("p (a b) -> p a b", a=2), ACT.Copy).then_inc(s["u_act"], 1)
                    act.wait_ge(s["pT0_mm"], DONE(n))
                    A(PT[:, 0, :, :], M3[:, :].rearrange("p (k q) -> p k q", k=4), ACT.Copy).then_inc(s["pT0_act"], 1)
                    exps(1, M0, M1, s["neg1"], s["es1"], s["exp1"])
                    if ahead:
                        h_lo(n + 1)
                    act.wait_ge(s["u_mm"], STEP(n, 2, 2))
                    A(Ub[:, :, :], M5[:, P:2 * P].rearrange("p (a b) -> p a b", a=2), ACT.Copy).then_inc(s["u_act"], 1)
                    act.wait_ge(s["pT1_mm"], DONE(n))
                    A(PT[:, 0, :, :], M0[:, :].rearrange("p (k q) -> p k q", k=4), ACT.Copy).then_inc(s["pT1_act"], 1)
                    act.wait_ge(s["ytm_ready"], DONE(n))
                    A(Q[:, :, :], ytm[:, :, :], ACT.Square).then_inc(s["y_sq"], 1)
                    act.wait_ge(L["dve_t"], n * DVE_T + YVAR)
                    A(small[:, 56:60], small[:, 52:56], ACT.Sqrt).then_inc(s["y_root"], 1)
                    act.wait_ge(s["yAT_mm"], DONE(n))
                    A(yT[:, 0:4, :], M4[:, :].rearrange("p (c t) -> p c t", c=4), ACT.Copy).then_inc(s["yA_ready"], 1)
                    if ahead:
                        copy_rk(n + 1)
                        copy_vwk(n + 1)
                        channels_rk(n + 1)
                    act.wait_ge(s["o0_mm"], DONE(n))
                    A(RB[:, 0:512], M5[:, :], ACT.Square, accum_out=small[:, 3:4])
                    if ahead:
                        channels_vw(n + 1)
                        low_rank(n + 1)
                    act.wait_ge(s["o1_mm"], DONE(n))
                    A(RB[:, 512:1024], M4[:, :], ACT.Square, accum_out=small[:, 4:5]).then_inc(s["o_squared"], 1)
                    act.wait_ge(L["dve_t"], n * DVE_T + OVAR)
                    A(small[:, 6:7], small[:, 5:6], ACT.Sqrt).then_inc(s["o_root"], 1)

                for step in (x_square, x_root, h_lo, copy_rk, copy_vwk, channels_rk, channels_vw, low_rank):
                    step(l * NT)
                with act.Fori(0, NT - 1) as i:
                    tile(l * NT + i, True)
                tile(l * NT + NT - 1, False)

                act.wait_ge(smp["dve"], AT("ms", l))
                A(dr2[:, :], dr1[:, :], ACT.Sqrt).then_inc(smp["act"], 1)
                act.wait_ge(smp["dve"], AT("proj", l))
                A(dsg[:, :, :], pj[:, 15:23, :], ACT.Silu).then_inc(smp["act"], 1)
                act.wait_ge(smp["dve"], AT("xs", l))
                A(dtw[0:32, :], dx[0:32, 6, :], ACT.Tanh)
                A(dtw[32:64, :], dx[32:64, 6, :], ACT.Copy).then_inc(smp["act"], 1)
                act.wait_ge(smp["pe"], AT("lora_mm", l))
                for p in range(PAIRS):
                    A(dw[:, p, :], M0[:, B * p:B * p + B], ACT.Sigmoid, bias=par("w0")[:, p:p + 1])
                    last = A(da[:, p, :], M0[:, 16 + B * p:16 + B * p + B], ACT.Sigmoid, bias=par("a0")[:, p:p + 1])
                last.then_inc(smp["act"], 1)
                act.wait_ge(smp["act"], AT("sig", l))
                A(dw[:, :, :], dw[:, :, :], ACT.Exp, scale=-DECAY).then_inc(smp["act"], 1)
                act.wait_ge(smp["pe"], AT("kk_mm", l))
                A(dkk[:, :], M2[:, 0:16], ACT.Sqrt).then_inc(smp["act"], 1)
                act.wait_ge(smp["pe"], AT("lru_mm", l))
                for c in range(2):
                    A(dgr[:, c, :], M3[:, B * c:B * c + B], ACT.Sigmoid, bias=par("gab")[:, c:c + 1])
                    last = A(dgi[:, c, :], M3[:, 16 + B * c:16 + B * c + B], ACT.Sigmoid, bias=par("gxb")[:, c:c + 1])
                last.then_inc(smp["act"], 1)
                act.wait_ge(smp["act"], AT("gates", l))
                for c in range(2):
                    A(dth[:, c, :], dgr[:, c, :], ACT.Tanh, scale=spc[:, 9, c:c + 1])
                    last = A(daa[:, c, :], dgr[:, c, :], ACT.Exp, scale=spc[:, 9, c:c + 1])
                last.then_inc(smp["act"], 1)
                act.wait_ge(smp["dve"], AT("lru_t", l))
                A(dth[:, :, :], dth[:, :, :], ACT.Sqrt, scale=-1.0).then_inc(smp["act"], 1)
                act.wait_ge(smp["dve"], AT("neg", l))
                A(dm[0:64, 5:6], dm[0:64, 3:4], ACT.Exp)
                A(Pd[0:64, :], M4[0:64, 0:P + 1], ACT.Exp, bias=dm[0:64, 2:3], scale=SCALE,
                  accum_out=dm[0:64, 4:5]).then_inc(smp["act"], 1)
                act.wait_ge(smp["dve"], AT("var", l))
                A(dq2[:, :], dq1[:, :], ACT.Sqrt).then_inc(smp["act"], 1)
                act.wait_ge(smp["dve"], AT("oms", l))
                A(dr2[:, :], dr1[:, :], ACT.Sqrt).then_inc(smp["act"], 1)

        @block.vector
        def _(dve):
            for name in DVE_SEMS:
                dve.sem_inc(s[name], TILE_STEPS.get(name, 1))
            tt, stt, ts = nc.vector.tensor_tensor, nc.vector.scalar_tensor_tensor, nc.vector.tensor_scalar
            cp, red, rcp, ms = nc.vector.tensor_copy, nc.vector.tensor_reduce, nc.vector.reciprocal, nc.vector.memset
            dve.wait_ge(L["const"], 48)
            for t in (kap, bti, kti, rti):
                ms(t[:, :, :], 0.0)
            ms(pB[:, :, :], 0.0)
            ms(xs[:, :, :], 0.0).then_inc(L["cleared"], 1)
            dve.wait_ge(L["cleared"], 1)
            dve.wait_ge(L["cast"], 3)
            link = Link(dve, L["dve_t"], DVE_T)
            front = Link(dve, L["dve_x"], DVE_X)
            ll = Link(dve, L["dve_l"], DVE_L)
            dl = Link(dve, L["dve_d"], DVE_D)
            dve.sem_inc(L["layer_end"], 1)
            with dve.Fori(0, DEPTH) as l:
                ll.start(l)
                dve.wait_ge(L["state"], l * 96 + 16)
                ms(pB[:, :, 0:1], 0.0)
                ms(kT[:, 0:P], 0.0)
                ms(Vt[:, 0, :], 0.0)
                ms(S[:, 0, :, :], 0.0)
                ms(xcb[:, :, 0:3], 0.0)
                ms(hcar[:, :], 0.0)
                ms(flag[:, :], 1.0)
                cp(mk[:, 0:P], mkprev[:, 0, :]).then_inc(L["zeros"], 1)
                dve.wait_ge(L["zeros"], l + 1)
                dve.wait_ge(L["prm"], (l + 1) * 48)
                for g in range(MODG):
                    dve.wait_ge(L["mod_mm"], l * 24 + 4 * (g + 1))
                    cp(rowbuf[g % 2][0:1 + B, :], (G0, G1)[g % 2][0:1 + B, :]).then_inc(L["row_out"], 1)
                dve.wait_ge(L["modT_mm"], l + 1)
                ll(tt(mod[:, :, :], M0[:, 0:216].rearrange("p (q b) -> p q b", q=24), over(par("bmod"), 2, 9), ALU.add))
                ll(ts(gs[:, :, :], mod[:, 8:16, :], 1.0, None, ALU.add))
                tt(gs[:, :, :], gs[:, :, :], over(par("npre"), 2, 9), ALU.mult).then_inc(L["mod_out"], 1)
                tt(gpc[:, :, :], mod[:, 16:24, :], over(par("npost"), 2, 9), ALU.mult).then_inc(L["gpc"], 1)
                dve.wait_ge(L["gp_mm"], l + 1)
                cp(gp[:, 0:512], M1[:, :])
                cp(gp[:, 512:1024], M2[:, :]).then_inc(L["gp_out"], 1)
                lam = par("lam")
                ll(ts(spc[:, 10, :], lam, -1.0, None, ALU.mult))
                tt(spc[:, 0, :], lam, spc[:, 10, :], ALU.max).then_inc(L["sp1"], 1)
                dve.wait_ge(L["sp2"], 2 * l + 1)
                ll(ts(spc[:, 2, :], spc[:, 1, :], 1.0, None, ALU.add))
                ll(ts(spc[:, 3, :], spc[:, 2, :], -1.0, None, ALU.add))
                ts(spc[:, 4, :], spc[:, 3, :], 0.0, None, ALU.is_equal).then_inc(L["sp3"], 1)
                dve.wait_ge(L["sp3"], 2 * l + 1)
                ll(tt(spc[:, 3, :], spc[:, 3, :], spc[:, 4, :], ALU.add))
                ll(rcp(spc[:, 6, :], spc[:, 3, :]))
                ll(tt(spc[:, 6, :], spc[:, 6, :], spc[:, 1, :], ALU.mult))
                dve.wait_ge(L["sp2"], 2 * l + 2)
                ll(tt(spc[:, 6, :], spc[:, 6, :], spc[:, 5, :], ALU.mult))
                ll(tt(spc[:, 7, :], spc[:, 4, :], spc[:, 1, :], ALU.mult))
                ll(tt(spc[:, 6, :], spc[:, 6, :], spc[:, 7, :], ALU.add))
                ll(ts(spc[:, 8, :], spc[:, 10, :], 0.0, None, ALU.max))
                ll(tt(spc[:, 8, :], spc[:, 8, :], spc[:, 6, :], ALU.add))
                ts(spc[:, 9, :], spc[:, 8, :], -LRU_C, None, ALU.mult).then_inc(L["sp3"], 1)
                dve.wait_ge(L["sp3"], 2 * l + 2)
                ll.end()

                def x_mean(m):
                    front.start(m)
                    dve.wait_ge(s["x_squared"], DONE(m))
                    front(ts(small[:, 1:2], small[:, 0:1], 1.0 / D, EPS, ALU.mult, ALU.add))

                def x_norm(m):
                    dve.wait_ge(s["rms_root"], DONE(m))
                    front(rcp(small[:, 7:8], small[:, 2:3]))
                    ts(xn, xa[:, :], small[:, 7:8], None, ALU.mult).then_inc(s["xn_ready"], 1)

                def h_hi(m):
                    dve.wait_ge(s["xT_hi"], DONE(m))
                    for k in range(4, 8):
                        last = ts(hT[:, k, :], M3[:, P * (k - 4):P * (k - 4) + P], gs[:, k, 0:1], mod[:, k, 0:1],
                                  ALU.mult, ALU.add)
                    last.then_inc(s["hT_hi"], 1)

                xsk = xs[:, 2:4, :].rearrange("p c t -> p (c t)")
                xsr = xs[:, 0:2, :].rearrange("p c t -> p (c t)")
                xsv = xs[:, 4:6, :].rearrange("p c t -> p (c t)")

                def token_shift(m):
                    dve.wait_ge(s["pB_ready"], DONE(m))
                    dve.wait_ge(s["bonus_out"], BEFORE(m))
                    tt(xs[:, 0:6, :], pB[:, 0:6, 0:P], pB[:, 0:6, 1:P + 1], ALU.subtract)
                    front(tt(xs[0:64, 6, :], pB[0:64, 6, 0:P], pB[0:64, 6, 1:P + 1], ALU.subtract))
                    front(tt(xs[:, :, :], xs[:, :, :], over(par("mu"), 2, P), ALU.mult))
                    tt(xs[:, 0:6, :], xs[:, 0:6, :], pB[:, 0:6, 1:P + 1], ALU.add)
                    tt(xs[0:64, 6, :], xs[0:64, 6, :], pB[0:64, 6, 1:P + 1], ALU.add).then_inc(s["xs_ready"], 1)
                    dve.wait_ge(s["xs_ready"], DONE(m))
                    cp(pB[:, :, 0:1], pB[:, :, P:P + 1]).then_inc(s["carried"], 1)
                    dve.wait_ge(s["y_mm"], BEFORE(m))
                    front(tt(kkr.rearrange("p (c t) -> p c t", c=2), xs[:, 2:4, :], over(par("kk"), 2, P), ALU.mult))
                    tt(tmp, kkr, kkr, ALU.mult).then_inc(s["sq_ready"], 1)
                    front.end()

                def tile(n, ahead):
                    link.start(n)
                    dve.wait_ge(s["vbT_mm"], DONE(n))
                    vv = Vst[:, :, :].rearrange("p (a m) v -> p a m v", m=NCH)
                    mv = M1[:, 0:256].rearrange("p (a h v) -> p a h v", a=PAIRS, h=2)
                    for m in range(NCH):
                        for h in range(2):
                            last = cp(vv[HD * h:HD * h + HD, :, m, :], mv[CH * m:CH * m + CH, :, h, :])
                    last.then_inc(s["vst_ready"], 1)
                    dve.wait_ge(s["sgw_ready"], DONE(n))
                    link(nc.vector.tensor_tensor_scan(cum, con("reset"), sgw, 0.0, ALU.mult, ALU.add))
                    tt(cx, cum, sgw, ALU.subtract).then_inc(s["cum_ready"], 1)
                    dve.wait_ge(s["kknorm"], DONE(n))
                    link(ts(kkv, kkv, 1e-12, None, ALU.max))
                    link(rcp(kkv, kkv))
                    link(tt(kkv, kkr, kkv, ALU.mult))
                    dve.wait_ge(s["a_ready"], DONE(n))
                    v3 = lambda t: t.rearrange("p (c t) -> p c t", c=2)
                    link(stt(v3(kmod), v3(av), -1.0, over(par("ka"), 2, P), ALU.add, ALU.mult))
                    link(stt(kmod, kmod, 1.0, xsk, ALU.add, ALU.mult))
                    link(tt(av, av, kkv, ALU.mult))
                    link(tt(v3(bonv[:, :]), xs[:, 0:2, :], over(par("rk"), 2, P), ALU.mult))
                    tt(bonv[:, :], bonv[:, :], kmod, ALU.mult).then_inc(s["bonus_in"], 1)
                    dve.wait_ge(s["exps_ready"], DONE(n))
                    for h in range(2):
                        r = slice(HD * h, HD * h + HD)
                        v4 = lambda t: t[r, :].rearrange("p (u c) -> p u c", c=CH)
                        tt(kap[r, :, r], v4(kkv), v4(Ex), ALU.mult)
                        tt(bti[r, :, r], v4(av), v4(Em), ALU.mult)
                        tt(kti[r, :, r], v4(kmod), v4(Em), ALU.mult)
                        last = tt(rti[r, :, r], v4(xsr), v4(Ep), ALU.mult)
                    last.then_inc(s["bd_ready"], 1)
                    dve.wait_ge(s["bd_ready"], DONE(n))
                    dve.wait_ge(s["q_out"], DONE(n))
                    dve.wait_ge(s["vwk_out"], DONE(n))
                    dve.wait_ge(L["rope_in"], (n + 1) * 16)
                    q4 = qk[:, :].rearrange("p (h a f) -> p h a f", a=2, f=HALF)
                    r4 = rot.rearrange("p (h a f) -> p h a f", a=2, f=HALF)
                    tt(r4[:, :, 0, :], q4[:, :, 1, :], over(rope[:, 32:64], 1, 10), ALU.mult)
                    link(tt(r4[:, :, 1, :], q4[:, :, 0, :], over(rope[:, 32:64], 1, 10), ALU.mult))
                    link(tt(qk[:, :].rearrange("p (h f) -> p h f", f=HALF),
                            qk[:, :].rearrange("p (h f) -> p h f", f=HALF), over(rope[:, 0:32], 1, 20), ALU.mult))
                    tt(q4[:, :, 0, :], q4[:, :, 0, :], r4[:, :, 0, :], ALU.subtract)
                    tt(q4[:, :, 1, :], q4[:, :, 1, :], r4[:, :, 1, :], ALU.add).then_inc(s["rope_ready"], 1)
                    u3 = lambda m: m[:, :].rearrange("p (u c) -> p u c", c=P)
                    dve.wait_ge(s["g1T_mm"], DONE(n))
                    stt(NTbd, u3(M0), -1.0, over(con("mst"), 1, U), ALU.mult, ALU.mult)
                    dve.wait_ge(s["g1_mm"], DONE(n))
                    stt(Nbd, u3(M1), -1.0, over(con("ms"), 1, U), ALU.mult, ALU.mult).then_inc(s["ntn_ready"], 1)
                    dve.wait_ge(s["ntn_ready"], DONE(n))
                    for h in range(2):
                        r = slice(HD * h, HD * h + HD)
                        last = tt(Q[r, :, :], NTbd[r, :, r], over(ident[r, r], 1, U), ALU.add)
                    link(last)
                    dve.wait_ge(s["o_ready"], BEFORE(n))
                    dve.wait_ge(s["g2T_mm"], DONE(n))
                    tt(G2T, u3(M3), over(con("mst"), 1, U), ALU.mult)
                    dve.wait_ge(s["g3T_mm"], DONE(n))
                    tt(G3T, u3(M4), over(con("mit"), 1, U), ALU.mult)
                    dve.wait_ge(s["g4T_mm"], DONE(n))
                    tt(G4T, u3(M5), over(con("mit"), 1, U), ALU.mult).then_inc(s["g_ready"], 1)
                    dve.wait_ge(s["bonus_mm"], DONE(n))
                    tt(bonv[:, :], M2[:, 256:512], xsv, ALU.mult).then_inc(s["bonus_out"], 1)

                    def power_T(level):
                        dve.wait_ge(s["inv_mm"], STEP(n, level, 5))
                        cp(NTbd, u3(M1)).then_inc(s["inv_dve"], 1)

                    def product(level):
                        dve.wait_ge(s["q_mm5"], STEP(n, level, 5))
                        tt(Q[:, :, :], Q[:, :, :], M2[:, 0:256].rearrange("p (u c) -> p u c", c=CH), ALU.add)\
                            .then_inc(s["q_dve"], 1)

                    power_T(1)
                    dve.wait_ge(s["xcb_ready"], DONE(n))
                    cw, cb = par("cw"), par("cb")
                    for c in range(2):
                        last = ts(lu[:, c, :], xcb[:, c, 0:P], cw[:, c:c + 1], cb[:, c:c + 1], ALU.mult, ALU.add)
                    link(last)
                    for t in range(1, 4):
                        for c in range(2):
                            last = stt(lu[:, c, :], xcb[:, c, t:t + P], cw[:, 2 * t + c:2 * t + c + 1], lu[:, c, :],
                                       ALU.mult, ALU.add)
                        link(last)
                    cp(xcb[:, :, 0:3], xcb[:, :, P:P + 3]).then_inc(s["conv_ready"], 1)
                    product(1)
                    power_T(2)
                    product(2)
                    power_T(3)
                    dve.wait_ge(s["lru_exps"], DONE(n))
                    stt(lth, la2, 1.0, lth, ALU.add, ALU.mult).then_inc(s["lru_t"], 1)
                    product(3)
                    power_T(4)
                    product(4)
                    if ahead:
                        x_mean(n + 1)
                    dve.wait_ge(s["lru_root"], DONE(n))
                    ts(lth[:, :, 0:1], lth[:, :, 0:1], flag[:, 0:1], None, ALU.max)
                    link(tt(la2, lgi, lu, ALU.mult))
                    tt(la2, la2, lth, ALU.mult)
                    link(ms(flag[:, :], 0.0))
                    for c in range(2):
                        last = nc.vector.tensor_tensor_scan(lh[:, c, :], laa[:, c, :], la2[:, c, :], hcar[:, c:c + 1],
                                                            ALU.mult, ALU.add)
                    link(last)
                    cp(hcar[:, :].unsqueeze(2), lh[:, :, P - 1:P])
                    dve.wait_ge(s["gates_T"], DONE(n))
                    tt(yT[:, 6:8, :], yT[:, 6:8, :], lh, ALU.mult).then_inc(s["yC_ready"], 1)

                    def maxima(j, ma, mb, ready, neg):
                        dve.wait_ge(ready, DONE(n))
                        mx = small[:, 8 + 4 * j:12 + 4 * j].rearrange("p (c g) -> p c g", g=2)
                        for g, m in ((0, ma), (1, mb)):
                            last = red(mx[:, :, g], m[:, :].rearrange("p (c k) -> p c k", c=2), AX_X, ALU.max)
                        link(last)
                        m4, sk = small[:, 8 + 4 * j:12 + 4 * j], par("sink")[:, 4 * j:4 * j + 4]
                        link(stt(m4, m4, SCALE, sk, ALU.mult, ALU.max))
                        ts(small[:, 16 + 4 * j:20 + 4 * j], m4, -1.0, None, ALU.mult)
                        tt(small[:, 32 + 4 * j:36 + 4 * j], sk, m4, ALU.subtract).then_inc(neg, 1)

                    dve.wait_ge(s["inv_mm"], STEP(n, 5, 5))
                    link(ms(Qbd, 0.0))
                    maxima(0, M3, M4, s["s0_mm"], s["neg0"])
                    dve.wait_ge(s["q_mm5"], STEP(n, 5, 5))
                    for h in range(2):
                        r = slice(HD * h, HD * h + HD)
                        last = tt(Qbd[r, :, r], Q[r, :, :], M2[r, 0:256].rearrange("p (u c) -> p u c", c=CH), ALU.add)
                    last.then_inc(s["qbd"], 1)

                    def rhs(m):
                        dve.wait_ge(s["rh_mm"], STEP(n, m + 1, 2))
                        ts(RH[:, :, :], M5[:, 0:P].rearrange("p (a b) -> p a b", a=2), -1.0, None, ALU.mult)\
                            .then_inc(s["rh_ready"], 1)

                    def state(m, ready, value):
                        dve.wait_ge(ready, value)
                        pend = Ep[:, :].rearrange("p (a t) -> p a t", a=2)[:, :, CH * m + CH - 1:CH * m + CH]
                        tt(S[:, (m + 1) % 2, :, :], M5[:, 256:384].rearrange("p (a b) -> p a b", a=2),
                           pend.to_broadcast([P, 2, HD]), ALU.mult).then_inc(s["s_ready"], 1)

                    rhs(0)
                    maxima(1, M0, M1, s["s1_mm"], s["neg1"])
                    dve.wait_ge(s["pT0_mm"], DONE(n))
                    cp(PT[:, 1, :, :], M4[:, :].rearrange("p (k q) -> p k q", k=4)).then_inc(s["pT0_dve"], 1)
                    if ahead:
                        x_norm(n + 1)
                    state(0, s["s_mm"], DONE(n))
                    rhs(1)
                    dve.wait_ge(s["pT1_mm"], DONE(n))
                    cp(PT[:, 1, :, :], M1[:, :].rearrange("p (k q) -> p k q", k=4)).then_inc(s["pT1_dve"], 1)
                    if ahead:
                        h_hi(n + 1)
                    state(1, s["y_mm"], DONE(n))
                    link(red(small[:, 48:52], M2[:, 0:256].rearrange("p (u v) -> p u v", v=HD), AX_X, ALU.add))
                    link(ts(small[:, 48:52], small[:, 48:52], -1.0 / HD, None, ALU.mult))
                    tt(ytm[:, :, :], M2[:, 0:256].rearrange("p (u v) -> p u v", v=HD), over(small[:, 48:52], 2, HD),
                       ALU.add).then_inc(s["ytm_ready"], 1)
                    dve.wait_ge(s["exp1"], DONE(n))
                    link(tt(small[:, 24:32], small[:, 24:32], small[:, 40:48], ALU.add))
                    link(rcp(small[:, 24:32], small[:, 24:32]))
                    dve.wait_ge(s["y_sq"], DONE(n))
                    link(red(small[:, 52:56], Q[:, :, :], AX_X, ALU.add))
                    link(ts(small[:, 52:56], small[:, 52:56], 1.0 / HD, LNX_EPS, ALU.mult, ALU.add))
                    assert link.k == YVAR, link.k
                    dve.wait_ge(s["pv_mm"], DONE(n))
                    dve.wait_ge(s["gbcT_mm"], DONE(n))
                    link(tt(stA[:, :].rearrange("p (k v) -> p k v", v=HD), G1[:, :].rearrange("p (k v) -> p k v", v=HD),
                            over(small[:, 24:32], 2, HD), ALU.mult))
                    dve.wait_ge(s["ga_out"], DONE(n))
                    tt(stA[:, :], stA[:, :], stB[:, :], ALU.mult).then_inc(s["yA_tm"], 1)
                    dve.wait_ge(s["y_root"], DONE(n))
                    link(rcp(small[:, 56:60], small[:, 56:60]))
                    tt(ytm[:, :, :], ytm[:, :, :], over(small[:, 56:60], 2, HD), ALU.mult).then_inc(s["yn_ready"], 1)
                    cp(kT[:, 0:P], kT[:, P:2 * P])
                    cp(Vt[:, 0, :], Vt[:, 1, :])
                    cp(mk[:, 0:P], mkprev[:, 1, :]).then_inc(s["window_moved"], 1)
                    dve.wait_ge(s["ynT_mm"], DONE(n))
                    yb = Ep
                    for h in range(2):
                        last = cp(yb[HD * h:HD * h + HD, :].rearrange("p (u t) -> p u t", t=CH),
                                  M3[0:HD, :].rearrange("p (u k) -> p u k", k=P)[:, :, CH * h:CH * h + CH])
                    link(last)
                    for p in range(PAIRS):
                        last = ts(yb[:, P * p:P * p + P], yb[:, P * p:P * p + P], par("lnw")[:, p:p + 1],
                                  par("lnb")[:, p:p + 1], ALU.mult, ALU.add)
                    link(last)
                    link(tt(yb[:, :], yb[:, :], bonv[:, :], ALU.add))
                    tt(yT[:, 4:6, :], yT[:, 4:6, :], yb[:, :].rearrange("p (c t) -> p c t", c=2), ALU.mult)\
                        .then_inc(s["yB_ready"], 1)
                    if ahead:
                        token_shift(n + 1)
                    dve.wait_ge(s["o_squared"], DONE(n))
                    link(tt(small[:, 5:6], small[:, 3:4], small[:, 4:5], ALU.add))
                    link(ts(small[:, 5:6], small[:, 5:6], 1.0 / D, EPS, ALU.mult, ALU.add))
                    assert link.k == OVAR, link.k
                    dve.wait_ge(s["o_root"], DONE(n))
                    link(rcp(small[:, 60:61], small[:, 6:7]))
                    stt(ob[:, 0:512], M5[:, :], small[:, 60:61], gp[:, 0:512], ALU.mult, ALU.mult)
                    link(stt(ob[:, 512:1024], M4[:, :], small[:, 60:61], gp[:, 512:1024], ALU.mult, ALU.mult))
                    dve.wait_ge(L["xr_in"], (n + 1) * 16)
                    tt(ob, ob, xr, ALU.add).then_inc(s["o_ready"], 1)
                    link.end()

                for step in (x_mean, x_norm, h_hi, token_shift):
                    step(l * NT)
                with dve.Fori(0, NT - 1) as i:
                    tile(l * NT + i, True)
                tile(l * NT + NT - 1, False)
                dve.wait_ge(s["o_ready"], BEFORE((l + 1) * NT))

                dl.start(l)

                def signal(ins, step):
                    ins.then_inc(smp["dve"], 1)
                    dve.wait_ge(smp["dve"], AT(step, l))

                signal(tt(dsq[:, :, :], xsT[:, :, :], xsT[:, :, :], ALU.mult), "sq")
                dve.wait_ge(smp["pe"], AT("ssq_mm", l))
                signal(ts(dr1[:, :], M0[:, 0:B], 1.0 / D, EPS, ALU.mult, ALU.add), "ms")
                dve.wait_ge(smp["act"], AT("root", l))
                dl(rcp(dr2[:, :], dr2[:, :]))
                dl(tt(dh[:, :, :], xsT[:, :, :], over(dr2[:, :], 1, KC), ALU.mult))
                dl(tt(dh[:, :, :], dh[:, :, :], gs[:, :, 1:1 + B], ALU.mult))
                signal(tt(dh[:, :, :], dh[:, :, :], mod[:, 0:8, 1:1 + B], ALU.add), "h")
                for g, (_, width, _) in enumerate(DGROUPS):
                    dve.wait_ge(L["row_mm"], l * (ROWS - MODG) + (g + 1))
                    cp(rowbuf[g % 2][0:B, 0:width], (G0, G1)[g % 2][0:B, 0:width]).then_inc(L["row_out"], 1)
                dve.wait_ge(smp["in_small"], (l + 1) * 64)
                dve.wait_ge(smp["pe"], AT("proj_mm", l))
                dl(ms(pj[:, 6, :], 0.0))
                cp(pj[0:64, 6, :], M1[0:64, 6 * B:7 * B])
                cp(pj[:, 0:6, :], M1[:, 0:6 * B].rearrange("p (c b) -> p c b", b=B))
                signal(cp(pj[:, 7:23, :], M1[:, 7 * B:23 * B].rearrange("p (c b) -> p c b", b=B)), "proj")
                dl(tt(dx[:, :, :], dshift[:, :, :], pj[:, 0:7, :], ALU.subtract))
                dl(tt(dx[:, :, :], dx[:, :, :], over(par("mu"), 2, B), ALU.mult))
                signal(tt(dx[:, :, :], dx[:, :, :], pj[:, 0:7, :], ALU.add), "xs")
                cw, cb = par("cw"), par("cb")
                dl(tt(du[:, :, :], pj[:, 12:14, :], over(cw[:, 6:8], 2, B), ALU.mult))
                for k in range(3):
                    dl(tt(dv1[:, :, :], dconv[:, :, k, :], over(cw[:, 2 * k:2 * k + 2], 2, B), ALU.mult))
                    dl(tt(du[:, :, :], du[:, :, :], dv1[:, :, :], ALU.add))
                dl(tt(du[:, :, :], du[:, :, :], over(cb, 2, B), ALU.add))
                cp(dcnew[:, :, 0:2, :], dconv[:, :, 1:3, :])
                signal(cp(dcnew[:, :, 2, :], pj[:, 12:14, :]), "u")
                f2 = lambda v: v.rearrange("p c b -> p (c b)")
                dl(tt(dkr[:, :, :], dx[:, 2:4, :], over(par("kk"), 2, B), ALU.mult))
                signal(tt(dq1[:, :], f2(dkr[:, :, :]), f2(dkr[:, :, :]), ALU.mult), "kksq")
                dve.wait_ge(smp["act"], AT("w", l))
                dl(stt(dkm[:, :, :], da[:, :, :], -1.0, over(par("ka"), 2, B), ALU.add, ALU.mult))
                dl(stt(dkm[:, :, :], dkm[:, :, :], 1.0, dx[:, 2:4, :], ALU.add, ALU.mult))
                dl(tt(dv1[:, :, :], dx[:, 0:2, :], over(par("rk"), 2, B), ALU.mult))
                signal(tt(dq2[:, :], f2(dv1[:, :, :]), f2(dkm[:, :, :]), ALU.mult), "bonus_in")
                dve.wait_ge(smp["act"], AT("kknorm", l))
                dl(ts(dkk[:, :], dkk[:, :], 1e-12, None, ALU.max))
                dl(rcp(dkk[:, :], dkk[:, :]))
                dl(tt(dkk[:, :], dkk[:, :], f2(dkr[:, :, :]), ALU.mult))
                dl(tt(f2(da[:, :, :]), f2(da[:, :, :]), dkk[:, :], ALU.mult))
                S3, A3, C3 = (v.rearrange("p (u v) -> p u v", v=HD) for v in (dS, dT1, dT2))
                dve.wait_ge(smp["kv_in"], (l + 1) * 96)
                signal(tt(A3, S3, over(dkk[:, :], 2, HD), ALU.mult), "skk")
                signal(tt(C3, over(dcon("stack"), 1, 16), over(f2(dx[:, 4:6, :]), 2, HD), ALU.mult), "vdiag")
                dve.wait_ge(smp["pe"], AT("bonus_mm", l))
                signal(tt(dbv[:, :], M4[:, 0:16], f2(dx[:, 4:6, :]), ALU.mult), "bonus")
                dve.wait_ge(smp["pe"], AT("perm_mm", l))
                dl(ts(drq[:, :, :], pj[:, 7:12, :], dcon("cos"), None, ALU.mult))
                dl(stt(drq[:, :, :], M5[:, 0:5 * B].rearrange("p (c b) -> p c b", b=B), dcon("sin"), drq[:, :, :],
                       ALU.mult, ALU.add))
                cp(KTs[:, :, P:P + 1], drq[:, 0, :].unsqueeze(2))
                dl(ms(stB[:, :], 0.0))
                for g in range(KV):
                    for c in range(4):
                        last = cp(stB[HD * g:HD * g + HD, 4 * g + c:512:72], drq[HD * g:HD * g + HD, 1 + c, :])
                signal(last, "qrows")
                dl(tt(S3, S3, over(f2(dw[:, :, :]), 2, HD), ALU.mult))
                dve.wait_ge(smp["pe"], AT("sa_mm", l))
                ab, kb = f2(da[:, :, :]), f2(dkm[:, :, :])
                m3 = lambda m: m[:, :].rearrange("p (u v) -> p u v", v=HD)
                tt(A3[:, 0:8], m3(M2), over(ab[:, 0:8], 2, HD), ALU.mult)
                dl(tt(A3[:, 8:16], m3(M3), over(ab[:, 8:16], 2, HD), ALU.mult))
                dve.wait_ge(smp["pe"], AT("vb_mm", l))
                dl(tt(S3, S3, A3, ALU.subtract))
                tt(A3[:, 0:8], m3(M4), over(kb[:, 0:8], 2, HD), ALU.mult)
                dl(tt(A3[:, 8:16], m3(M5), over(kb[:, 8:16], 2, HD), ALU.mult))
                signal(tt(S3, S3, A3, ALU.add), "s_new")
                signal(tt(A3, S3, over(f2(dx[:, 0:2, :]), 2, HD), ALU.mult), "sr")
                dve.wait_ge(smp["pe"], AT("sr_mm", l))
                st = over(dcon("stack"), 1, 8)
                tt(C3[:, 0:8], m3(M2), st, ALU.mult)
                dl(tt(C3[:, 8:16], m3(M3), st, ALU.mult))
                signal(red(dyv[:, :], C3, AX_X, ALU.add), "y")
                dve.wait_ge(smp["pe"], AT("s_mm", l))
                dl(red(dm[0:64, 0:1], M4[0:64, 0:P + 1], AX_X, ALU.max))
                dl(stt(dm[0:64, 1:2], dm[0:64, 0:1], SCALE, par("dsink", 64), ALU.mult, ALU.max))
                ts(dm[0:64, 2:3], dm[0:64, 1:2], -1.0, None, ALU.mult)
                signal(tt(dm[0:64, 3:4], par("dsink", 64), dm[0:64, 1:2], ALU.subtract), "neg")
                dve.wait_ge(smp["pe"], AT("mean_mm", l))
                dl(stt(dyv[:, :], M0[:, 0:16], -1.0 / HD, dyv[:, :], ALU.mult, ALU.add))
                signal(tt(dq1[:, :], dyv[:, :], dyv[:, :], ALU.mult), "ysq")
                dve.wait_ge(smp["act"], AT("lru_exps", l))
                dl(tt(dv1[:, :, :], daa[:, :, :], daa[:, :, :], ALU.mult))
                signal(stt(dth[:, :, :], dv1[:, :, :], 1.0, dth[:, :, :], ALU.add, ALU.mult), "lru_t")
                dve.wait_ge(smp["pe"], AT("var_mm", l))
                signal(ts(dq1[:, :], M0[:, 16:32], 1.0 / HD, LNX_EPS, ALU.mult, ALU.add), "var")
                dve.wait_ge(smp["act"], AT("exp", l))
                dl(tt(dm[0:64, 4:5], dm[0:64, 4:5], dm[0:64, 5:6], ALU.add))
                dl(rcp(dm[0:64, 4:5], dm[0:64, 4:5]))
                dl(ts(Pd[0:64, :], Pd[0:64, :], dm[0:64, 4:5], None, ALU.mult))
                signal(ts(dg64[0:64, :], ident[0:64, 0:64], Pd[0:64, P:P + 1], None, ALU.mult), "pd")
                dve.wait_ge(smp["act"], AT("lru_root", l))
                dl(tt(dgi[:, :, :], dgi[:, :, :], du[:, :, :], ALU.mult))
                dl(tt(dgi[:, :, :], dgi[:, :, :], dth[:, :, :], ALU.mult))
                dl(tt(dh0[:, :, :], dh0[:, :, :], daa[:, :, :], ALU.mult))
                signal(tt(dh0[:, :, :], dh0[:, :, :], dgi[:, :, :], ALU.add), "h_new")
                dve.wait_ge(smp["act"], AT("silu", l))
                tt(ys[:, 6:8, :], dh0[:, :, :], dsg[:, 2:4, :], ALU.mult)
                dve.wait_ge(smp["act"], AT("yroot", l))
                dl(rcp(dq2[:, :], dq2[:, :]))
                dl(tt(dyv[:, :], dyv[:, :], dq2[:, :], ALU.mult))
                yv3 = dyv[:, :].rearrange("p (c b) -> p c b", b=B)
                dl(tt(yv3, yv3, over(par("lnw"), 2, B), ALU.mult))
                dl(tt(yv3, yv3, over(par("lnb"), 2, B), ALU.add))
                dl(tt(dyv[:, :], dyv[:, :], dbv[:, :], ALU.add))
                tt(ys[:, 4:6, :], yv3, dsg[:, 0:2, :], ALU.mult)
                dve.wait_ge(smp["pe"], AT("pt_mm", l))
                cp(PTd[:, :], M5[:, 0:64])
                cp(Pnd[0:8, :], M1[0:8, 0:64])
                signal(cp(Vnd[0:8, :], M1[0:8, 64:64 + P]), "pt")
                dve.wait_ge(smp["pe"], AT("pv_mm", l))
                for g in range(KV):
                    r = slice(HD * g, HD * g + HD)
                    last = tt(ys[r, 0:4, :], M2[r, 0:64].rearrange("p (b h) -> p h b", h=8)[:, 4 * g:4 * g + 4, :],
                              dsg[r, 4:8, :], ALU.mult)
                signal(last, "ys")
                for h in range(2):
                    dve.wait_ge(L["row_mm"], l * (ROWS - MODG) + (len(DGROUPS) + h + 1))
                    cp(rowbuf[h][0:B, :], (G0, G1)[h][0:B, :]).then_inc(L["row_out"], 1)
                dve.wait_ge(smp["pe"], AT("o_mm", l))
                dl(cp(dh[:, :, :], M3[:, 0:64].rearrange("p (c b) -> p c b", b=B)))
                signal(tt(dsq[:, :, :], dh[:, :, :], dh[:, :, :], ALU.mult), "osq")
                dve.wait_ge(smp["pe"], AT("ossq_mm", l))
                signal(ts(dr1[:, :], M4[:, 0:B], 1.0 / D, EPS, ALU.mult, ALU.add), "oms")
                dve.wait_ge(smp["act"], AT("oroot", l))
                dl(rcp(dr2[:, :], dr2[:, :]))
                dl(tt(dh[:, :, :], dh[:, :, :], over(dr2[:, :], 1, KC), ALU.mult))
                dl(tt(dh[:, :, :], dh[:, :, :], gpc[:, :, 1:1 + B], ALU.mult))
                dve.wait_ge(smp["stored"], (l + 1) * 96)
                dl.end()
                tt(xsT[:, :, :], xsT[:, :, :], dh[:, :, :], ALU.add).then_inc(L["layer_end"], 1)
                dve.wait_ge(L["layer_end"], l + 2)



def _lay_out(inp):
    f = np.float32
    g = {k: np.ascontiguousarray(np.asarray(v)) for k, v in inp.items()}

    def channels(x, n):
        return x.reshape(DEPTH, n, P).transpose(0, 2, 1)

    def heads(x, axis):
        sh = list(x.shape)
        x = x.reshape(sh[:axis] + [KV, 4, HD] + sh[axis + 1:])
        x = np.moveaxis(x, axis, axis + 1)
        return x.reshape(sh)

    w = g["w_in"]
    o = np.cumsum([0, 512, 128, 128, 512, 832, 256, 256, 256])
    q, ka, va, ga, pb, gb, xc, gc = (w[:, :, o[k]:o[k + 1]] for k in range(8))
    w = np.concatenate([pb, ka, heads(q, 2), xc, va, gb, gc, heads(ga, 2)], axis=2)
    a = {"w_in": w.reshape(DEPTH, KC, P, PIN).transpose(0, 2, 1, 3)}
    wo = g["w_out"]
    wo = np.concatenate([heads(wo[:, 0:512], 1), wo[:, 512:]], axis=1)
    a["w_out"] = wo.reshape(DEPTH, KC, P, D).transpose(0, 2, 1, 3)
    a["w_mod"] = g["w_mod"].reshape(DEPTH, KC, P, 24, P).transpose(0, 3, 2, 1, 4)
    mu = np.concatenate([g["rwkv_mu"], np.zeros((DEPTH, 64), f)], axis=1)
    sinks = g["attn_sinks"]
    slots = sinks.reshape(DEPTH, KV, 4).transpose(0, 2, 1).reshape(DEPTH, 1, HEADS)
    dsink = np.concatenate([np.tile(sinks, (1, B)), np.zeros((DEPTH, 64), f)], axis=1)[:, :, None]
    cw = g["lru_conv_w"].reshape(DEPTH, 4, 2, P).transpose(0, 3, 1, 2).reshape(DEPTH, P, 8)
    a["prm"] = np.concatenate([
        channels(g["norm_pre"], 8), channels(g["norm_post"], 8), channels(g["b_mod"], 24), channels(mu, 7),
        channels(g["rwkv_w0"], 2), channels(g["rwkv_a0"], 2), channels(g["rwkv_k_k"], 2), channels(g["rwkv_k_a"], 2),
        channels(g["rwkv_r_k"].reshape(DEPTH, 256), 2), channels(g["rwkv_lnx_w"], 2), channels(g["rwkv_lnx_b"], 2),
        cw, channels(g["lru_conv_b"], 2), channels(g["lru_gate_a_b"], 2), channels(g["lru_gate_x_b"], 2),
        channels(g["lru_lambda"], 2), np.broadcast_to(slots, (DEPTH, P, HEADS)), dsink], axis=2)
    lo = np.zeros((DEPTH, 2 * LORA, 512), f)
    lo[:, 0:LORA, 0:256] = g["rwkv_w_up"]
    lo[:, LORA:, 256:512] = g["rwkv_a_up"]
    a["lora"] = lo
    gw = np.zeros((DEPTH, P, 4, P), f)
    for k, name in ((0, "lru_gate_a_w"), (2, "lru_gate_x_w")):
        for n in range(4):
            r = slice(HD * (n % 2), HD * (n % 2) + HD)
            gw[:, r, k + n // 2, r] = g[name][:, n]
    a["gatew"] = gw
    a["cT"] = np.concatenate([g["c_prompt"], g["c_sample"]]).T.reshape(KC, P, 1 + B).transpose(1, 0, 2)
    a["x_prompt"] = g["x_prompt"].reshape(SEQ, D)
    a["x_s"] = g["x_sample"].reshape(B, D).T.reshape(KC, P, B).transpose(1, 0, 2)
    a["kc"] = g["cache_swa_k"].reshape(DEPTH, B, P, P).transpose(0, 3, 1, 2)
    a["vc"] = g["cache_swa_v"].reshape(DEPTH, B, P, P).transpose(0, 2, 1, 3)
    sh = np.concatenate([g["state_rwkv_shift"], np.zeros((DEPTH, B, 64), f)], axis=2)
    a["shift_s"] = sh.reshape(DEPTH, B, 7, P).transpose(0, 3, 2, 1)
    a["wkv_s"] = g["state_rwkv_wkv"].reshape(DEPTH, B, 2, 2, HD, HD).transpose(0, 3, 5, 2, 1, 4).reshape(DEPTH, P, 1024)
    a["conv_s"] = g["state_lru_conv"].reshape(DEPTH, B, 3, 2, P).transpose(0, 4, 3, 2, 1)
    a["h_s"] = g["state_lru_h"].reshape(DEPTH, B, 2, P).transpose(0, 3, 2, 1)
    i = np.arange(P)
    same = (i[:, None] // CH) == (i[None, :] // CH)
    ident = np.eye(P, dtype=f)
    reset = np.tile((np.arange(256) % CH != 0).astype(f), (P, 1))
    a["cst"] = np.concatenate([ident, same.astype(f), (same & (i[:, None] < i[None, :])).astype(f),
                               (same & (i[:, None] > i[None, :])).astype(f),
                               (same & (i[:, None] <= i[None, :])).astype(f), reset], axis=1)
    neg = np.full((P, P), NEG, f)
    a["masks"] = np.concatenate([neg, np.where(i[None, :] >= i[:, None], 0, neg),
                                 np.where(i[None, :] <= i[:, None], 0, neg)], axis=1).astype(f)
    inv = (10000.0 ** (-np.arange(HALF) / HALF)).astype(f)
    ang = (np.arange(SEQ + 1, dtype=f)[:, None] * inv[None, :]).astype(f)
    cos, sin = np.cos(ang).astype(f), np.sin(ang).astype(f)
    a["rope"] = np.concatenate([cos, sin], axis=1)[:SEQ].reshape(NT, P, 64)
    perm = ident[(i // HD) * HD + (i % HD + HALF) % HD]
    sign = np.where(i % HD < HALF, -1, 1).astype(f)
    rowb = np.zeros((P, B), f)
    rowb[np.arange(64), np.arange(64) // 8] = 1
    a["dcst"] = np.concatenate([perm, np.tile(np.eye(HD, dtype=f), (2, 1)), rowb, cos[PAST, i % HALF][:, None],
                                (sin[PAST, i % HALF] * sign)[:, None]], axis=1)
    return {k: np.ascontiguousarray(v, dtype=f) for k, v in a.items()}


_OUTS = {
    "y_prompt": (SEQ, D), "y_s": (P, KC, B), "k_p": (DEPTH, P, P), "v_p": (DEPTH, P, P), "shift_p": (DEPTH, P, 7),
    "wkv_p": (DEPTH, P, PAIRS, HD), "conv_p": (DEPTH, P, 2, 3), "h_p": (DEPTH, P, 2),
    "ko_s": (DEPTH, P, B), "vo_s": (DEPTH, P, B), "shifto_s": (DEPTH, P, 7, B), "wkvo_s": (DEPTH, P, 1024),
    "convo_s": (DEPTH, P, 2, 3, B), "ho_s": (DEPTH, P, 2, B)}


def kernel(**inputs):
    import concourse.bacc as bacc
    from concourse.bass_utils import run_bass_kernel_spmd

    nc = bacc.Bacc("TRN2", target_bir_lowering=False, num_devices=1)
    arrays = _lay_out(inputs)
    d = {k: nc.dram_tensor("in_" + k, v.shape, F32, kind="ExternalInput").ap() for k, v in arrays.items()}
    d.update({k: nc.dram_tensor("out_" + k, v, F32, kind="ExternalOutput").ap() for k, v in _OUTS.items()})
    d["x_mid"] = nc.dram_tensor("x_mid", (SEQ, D), F32, kind="Internal").ap()
    program(nc, d)
    res = run_bass_kernel_spmd(nc, [{"in_" + k: v for k, v in arrays.items()}], core_ids=[0]).results[0]
    r = {k: np.asarray(res["out_" + k]).reshape(v) for k, v in _OUTS.items()}
    c = np.ascontiguousarray
    return (
        r["y_prompt"].reshape(1, SEQ, D),
        c(r["y_s"].transpose(2, 1, 0)).reshape(B, 1, D),
        c(r["k_p"].transpose(0, 2, 1)).reshape(DEPTH, 1, P, KV, HD),
        r["v_p"].reshape(DEPTH, 1, P, KV, HD),
        c(r["shift_p"].transpose(0, 2, 1).reshape(DEPTH, 1, 896)[:, :, :SHIFT]),
        c(r["wkv_p"].reshape(DEPTH, 2, HD, 2, HD).transpose(0, 3, 1, 4, 2)).reshape(DEPTH, 1, 4, HD, HD),
        c(r["conv_p"].transpose(0, 3, 2, 1)).reshape(DEPTH, 1, 3, 256),
        c(r["h_p"].transpose(0, 2, 1)).reshape(DEPTH, 1, 256),
        c(r["ko_s"].transpose(0, 2, 1)).reshape(DEPTH, B, 1, KV, HD),
        c(r["vo_s"].transpose(0, 2, 1)).reshape(DEPTH, B, 1, KV, HD),
        c(r["shifto_s"].transpose(0, 3, 2, 1).reshape(DEPTH, B, 896)[:, :, :SHIFT]),
        c(r["wkvo_s"].reshape(DEPTH, 2, HD, 2, B, HD).transpose(0, 4, 3, 1, 5, 2)).reshape(DEPTH, B, 4, HD, HD),
        c(r["convo_s"].transpose(0, 4, 3, 2, 1)).reshape(DEPTH, B, 3, 256),
        c(r["ho_s"].transpose(0, 3, 2, 1)).reshape(DEPTH, B, 256),
    )
```
